# Optimizing a Trainium2 kernel written in Bass

```python
import jax, jax.numpy as jnp
from jax import lax
import numpy as np

D_MODEL = 2048
BATCH = 1
SEQ = 256
DEPTH = 1

HEAD_DIM = 128
N_ATT_HEADS = 8
N_KV_GROUPS = 2
HEADS_PER_GROUP = N_ATT_HEADS // N_KV_GROUPS
ATT_WIDTH = N_ATT_HEADS * HEAD_DIM
KV_WIDTH = N_KV_GROUPS * HEAD_DIM
N_CONV_GROUPS = 8
CONV_WIDTH = N_CONV_GROUPS * HEAD_DIM
MIX_WIDTH = ATT_WIDTH + CONV_WIDTH
N_MIX_GROUPS = N_ATT_HEADS + N_CONV_GROUPS
N_BRANCH = 3
CMP_BLOCK = 32
CMP_STRIDE = 16
CMP_HIDDEN = 512
SLC_BLOCK = 64
N_SELECT = 16
WINDOW = 512
Q_BLOCK = 128
CONV_K = 3
PEER_HEADS = 8
N_KEYS = 128
N_EXPERTS = N_KEYS * N_KEYS
PEER_QDIM = 256
PEER_HALF = PEER_QDIM // 2
PEER_TOPK = 16
TOKEN_CHUNK = 128
ALPHA = (2.0 * DEPTH) ** 0.25
BETA = (8.0 * DEPTH) ** -0.25
LN_EPS = 1e-5
RMS_EPS = 1e-6
NEG_INF = -1e30
FORCE_BONUS = 1e4
SPLIT_SIZES = (ATT_WIDTH, KV_WIDTH, KV_WIDTH, KV_WIDTH, KV_WIDTH, KV_WIDTH, KV_WIDTH,
               N_ATT_HEADS * N_BRANCH, CONV_WIDTH, CONV_WIDTH, CONV_WIDTH)
IN_WIDTH = sum(SPLIT_SIZES)

kernel_name = 'hybrid_nsa_shortconv_peer_deepnorm'

def _layernorm(x, g, b):
    xf = x.astype(jnp.float32)
    mu = xf.mean(-1, keepdims=True)
    var = jnp.square(xf - mu).mean(-1, keepdims=True)
    return ((xf - mu) * lax.rsqrt(var + LN_EPS) * g + b).astype(x.dtype)

def _head_rmsnorm(y, g):
    B, S, _ = y.shape
    yf = y.astype(jnp.float32).reshape(B, S, N_MIX_GROUPS, HEAD_DIM)
    yf = yf * lax.rsqrt(jnp.mean(jnp.square(yf), -1, keepdims=True) + RMS_EPS)
    return (yf.reshape(B, S, MIX_WIDTH) * g).astype(y.dtype)

def _alibi_slopes():
    return 2.0 ** (-8.0 * jnp.arange(1, N_ATT_HEADS + 1, dtype=jnp.float32) / N_ATT_HEADS)

def _compress(kv, pos, w1, b1, w2):
    B, S, G, D = kv.shape
    n_cmp = (S - CMP_BLOCK) // CMP_STRIDE + 1
    idx = jnp.arange(n_cmp)[:, None] * CMP_STRIDE + jnp.arange(CMP_BLOCK)[None, :]
    blocks = kv[:, idx] + pos[None, None, :, None, :]
    blocks = blocks.transpose(0, 1, 3, 2, 4).reshape(B, n_cmp, G, CMP_BLOCK * D)
    return jax.nn.gelu(blocks @ w1 + b1) @ w2

def _nsa(q, k_cmp, v_cmp, k_slc, v_slc, k_win, v_win, gates):
    B, S = q.shape[:2]
    G, R, D = N_KV_GROUPS, HEADS_PER_GROUP, HEAD_DIM
    f32 = jnp.float32
    n_cmp = k_cmp.shape[1]
    n_slc = S // SLC_BLOCK
    n_sel = min(N_SELECT, n_slc)
    n_qb = S // Q_BLOCK
    scale = D ** -0.5
    slopes = _alibi_slopes().reshape(G, R)
    sl5 = slopes[None, :, :, None, None]
    sl6 = slopes[None, :, :, None, None, None]
    q = q.astype(f32)
    k_cmp, v_cmp = k_cmp.astype(f32), v_cmp.astype(f32)
    cmp_pos = jnp.arange(n_cmp, dtype=f32) * CMP_STRIDE + (CMP_BLOCK - 1) / 2.0
    cmp_end = jnp.arange(n_cmp) * CMP_STRIDE + CMP_BLOCK - 1
    ci = jnp.arange(n_cmp, dtype=f32)[:, None] * CMP_STRIDE
    sj = jnp.arange(n_slc, dtype=f32)[None, :] * SLC_BLOCK
    overlap = ((ci < sj + SLC_BLOCK) & (ci + CMP_BLOCK > sj)).astype(f32)
    k_blocks = k_slc.astype(f32).reshape(B, n_slc, SLC_BLOCK, G, D).transpose(0, 3, 1, 2, 4)
    v_blocks = v_slc.astype(f32).reshape(B, n_slc, SLC_BLOCK, G, D).transpose(0, 3, 1, 2, 4)
    k_wpad = jnp.pad(k_win.astype(f32), ((0, 0), (WINDOW, 0), (0, 0), (0, 0)))
    v_wpad = jnp.pad(v_win.astype(f32), ((0, 0), (WINDOW, 0), (0, 0), (0, 0)))
    b_ix = jnp.arange(B)[:, None, None, None]
    g_ix = jnp.arange(G)[None, :, None, None]
    jb = jnp.arange(n_slc)

    def block(nb):
        s0 = nb * Q_BLOCK
        t = s0 + jnp.arange(Q_BLOCK)
        tf = t.astype(f32)
        qb = lax.dynamic_slice_in_dim(q, s0, Q_BLOCK, axis=1).reshape(B, Q_BLOCK, G, R, D) * scale
        gb = lax.dynamic_slice_in_dim(gates, s0, Q_BLOCK, axis=1).reshape(B, Q_BLOCK, G, R, N_BRANCH)
        s = jnp.einsum('bqgrd,bngd->bgrqn', qb, k_cmp) - sl5 * (tf[:, None] - cmp_pos[None, :])
        valid = cmp_end[None, :] <= t[:, None]
        p_cmp = jax.nn.softmax(jnp.where(valid, s, NEG_INF), axis=-1) * valid
        o_cmp = jnp.einsum('bgrqn,bngd->bqgrd', p_cmp, v_cmp)
        imp = jnp.einsum('bgrqn,nj->bgqj', p_cmp, overlap)
        cur = t // SLC_BLOCK
        valid_s = jb[None, :] * SLC_BLOCK <= t[:, None]
        forced = (jb[None, :] == 0) | (jb[None, :] == cur[:, None]) | (jb[None, :] == cur[:, None] - 1)
        score = jnp.where(valid_s, imp + FORCE_BONUS * forced, -1.0)
        _, sel = lax.top_k(score, n_sel)
        kb = k_blocks[b_ix, g_ix, sel]
        vb = v_blocks[b_ix, g_ix, sel]
        pos = sel[..., None] * SLC_BLOCK + jnp.arange(SLC_BLOCK)
        dist = (t[:, None, None] - pos)[:, :, None]
        s = jnp.einsum('bqgrd,bgqkpd->bgrqkp', qb, kb) - sl6 * dist.astype(f32)
        s = jnp.where(dist >= 0, s, NEG_INF)
        p = jax.nn.softmax(s.reshape(B, G, R, Q_BLOCK, n_sel * SLC_BLOCK), axis=-1)
        p = p.reshape(B, G, R, Q_BLOCK, n_sel, SLC_BLOCK)
        o_slc = jnp.einsum('bgrqkp,bgqkpd->bqgrd', p, vb)
        kw = lax.dynamic_slice_in_dim(k_wpad, s0, WINDOW + Q_BLOCK, axis=1)
        vw = lax.dynamic_slice_in_dim(v_wpad, s0, WINDOW + Q_BLOCK, axis=1)
        posw = s0 - WINDOW + jnp.arange(WINDOW + Q_BLOCK)
        dw = t[:, None] - posw[None, :]
        mw = (dw >= 0) & (dw < WINDOW) & (posw[None, :] >= 0)
        s = jnp.einsum('bqgrd,bkgd->bgrqk', qb, kw) - sl5 * dw.astype(f32)
        p = jax.nn.softmax(jnp.where(mw, s, NEG_INF), axis=-1)
        o_win = jnp.einsum('bgrqk,bkgd->bqgrd', p, vw)
        o = gb[..., 0:1] * o_cmp + gb[..., 1:2] * o_slc + gb[..., 2:3] * o_win
        return o.reshape(B, Q_BLOCK, ATT_WIDTH)

    out = lax.map(block, jnp.arange(n_qb))
    return out.transpose(1, 0, 2, 3).reshape(B, S, ATT_WIDTH)

def _short_conv(u, gate_b, gate_c, conv_w):
    y = lax.conv_general_dilated(gate_c * u, conv_w[:, None, :].astype(u.dtype), window_strides=(1,),
                                 padding=[(CONV_K - 1, 0)], dimension_numbers=('NWC', 'WIO', 'NWC'),
                                 feature_group_count=CONV_WIDTH)
    return gate_b * y

def _peer(h, w_query, sub_keys, expert_u, expert_v):
    B, S, D = h.shape
    q = (h @ w_query).reshape(B, S, PEER_HEADS, 2, PEER_HALF).astype(jnp.float32)
    s = jnp.einsum('bshcd,hckd->bshck', q, sub_keys.astype(jnp.float32))
    top_s, top_i = lax.top_k(s, PEER_TOPK)
    cand = top_s[..., 0, :, None] + top_s[..., 1, None, :]
    cand = cand.reshape(B, S, PEER_HEADS, PEER_TOPK * PEER_TOPK)
    best_s, best_i = lax.top_k(cand, PEER_TOPK)
    i1 = jnp.take_along_axis(top_i[..., 0, :], best_i // PEER_TOPK, axis=-1)
    i2 = jnp.take_along_axis(top_i[..., 1, :], best_i % PEER_TOPK, axis=-1)
    eid = i1 * N_KEYS + i2
    g = jax.nn.softmax(best_s, axis=-1).astype(h.dtype)
    n_ch = (B * S) // TOKEN_CHUNK
    hc = h.reshape(n_ch, TOKEN_CHUNK, D)
    ec = eid.reshape(n_ch, TOKEN_CHUNK, PEER_HEADS, PEER_TOPK)
    gc = g.reshape(n_ch, TOKEN_CHUNK, PEER_HEADS, PEER_TOPK)

    def chunk(args):
        hx, e, gw = args
        a = jax.nn.gelu(jnp.einsum('td,thkd->thk', hx, expert_u[e]))
        return jnp.einsum('thk,thkd->td', gw * a, expert_v[e])

    return lax.map(chunk, (hc, ec, gc)).reshape(B, S, D)

def setup_inputs(seed: int = 0) -> dict:
    key = jax.random.key(seed)
    ks = jax.random.split(key, 24)
    L, D = DEPTH, D_MODEL
    nrm = lambda k, shape, sc: jax.random.normal(k, shape, jnp.float32) * sc
    col_scale = np.concatenate([
        np.ones(ATT_WIDTH), np.ones(KV_WIDTH), np.full(KV_WIDTH, BETA), np.ones(KV_WIDTH),
        np.full(KV_WIDTH, BETA), np.ones(KV_WIDTH), np.full(KV_WIDTH, BETA),
        np.ones(N_ATT_HEADS * N_BRANCH), np.full(CONV_WIDTH, BETA), np.ones(CONV_WIDTH),
        np.ones(CONV_WIDTH)]).astype(np.float32)
    return {
        'x': nrm(ks[0], (BATCH, SEQ, D), 1.0),
        'w_in': nrm(ks[1], (L, D, IN_WIDTH), D ** -0.5) * jnp.asarray(col_scale),
        'cmp_k_pos': nrm(ks[2], (L, CMP_BLOCK, HEAD_DIM), 0.1),
        'cmp_k_w1': nrm(ks[3], (L, CMP_BLOCK * HEAD_DIM, CMP_HIDDEN), (CMP_BLOCK * HEAD_DIM) ** -0.5),
        'cmp_k_b1': nrm(ks[4], (L, CMP_HIDDEN), 0.01),
        'cmp_k_w2': nrm(ks[5], (L, CMP_HIDDEN, HEAD_DIM), CMP_HIDDEN ** -0.5),
        'cmp_v_pos': nrm(ks[6], (L, CMP_BLOCK, HEAD_DIM), 0.1),
        'cmp_v_w1': nrm(ks[7], (L, CMP_BLOCK * HEAD_DIM, CMP_HIDDEN), (CMP_BLOCK * HEAD_DIM) ** -0.5),
        'cmp_v_b1': nrm(ks[8], (L, CMP_HIDDEN), 0.01),
        'cmp_v_w2': nrm(ks[9], (L, CMP_HIDDEN, HEAD_DIM), CMP_HIDDEN ** -0.5),
        'conv_w': nrm(ks[10], (L, CONV_K, CONV_WIDTH), 0.5),
        'head_norm_g': 1.0 + nrm(ks[11], (L, MIX_WIDTH), 0.02),
        'w_out': nrm(ks[12], (L, MIX_WIDTH, D), BETA * MIX_WIDTH ** -0.5),
        'ln1_g': 1.0 + nrm(ks[13], (L, D), 0.02),
        'ln1_b': nrm(ks[14], (L, D), 0.01),
        'w_query': nrm(ks[15], (L, D, PEER_HEADS * PEER_QDIM), D ** -0.5),
        'sub_keys': nrm(ks[16], (L, PEER_HEADS, 2, N_KEYS, PEER_HALF), PEER_HALF ** -0.5),
        'expert_u': nrm(ks[17], (L, N_EXPERTS, D), D ** -0.5),
        'expert_v': nrm(ks[18], (L, N_EXPERTS, D), BETA),
        'ln2_g': 1.0 + nrm(ks[19], (L, D), 0.02),
        'ln2_b': nrm(ks[20], (L, D), 0.01),
    }

def reference(x, w_in, cmp_k_pos, cmp_k_w1, cmp_k_b1, cmp_k_w2, cmp_v_pos, cmp_v_w1, cmp_v_b1,
              cmp_v_w2, conv_w, head_norm_g, w_out, ln1_g, ln1_b, w_query, sub_keys, expert_u,
              expert_v, ln2_g, ln2_b):
    B, S, _ = x.shape
    offs = np.cumsum(SPLIT_SIZES)[:-1].tolist()
    for l in range(DEPTH):
        proj = x @ w_in[l]
        q, k_c, v_c, k_s, v_s, k_w, v_w, gate_logits, u, gate_b, gate_c = jnp.split(proj, offs, axis=-1)
        grp = lambda t: t.reshape(B, S, N_KV_GROUPS, HEAD_DIM)
        kc = _compress(grp(k_c), cmp_k_pos[l], cmp_k_w1[l], cmp_k_b1[l], cmp_k_w2[l])
        vc = _compress(grp(v_c), cmp_v_pos[l], cmp_v_w1[l], cmp_v_b1[l], cmp_v_w2[l])
        gates = jax.nn.sigmoid(gate_logits).reshape(B, S, N_ATT_HEADS, N_BRANCH)
        o_att = _nsa(q.reshape(B, S, N_ATT_HEADS, HEAD_DIM), kc, vc, grp(k_s), grp(v_s),
                     grp(k_w), grp(v_w), gates).astype(x.dtype)
        o_conv = _short_conv(u, gate_b, gate_c, conv_w[l])
        mix = _head_rmsnorm(jnp.concatenate([o_att, o_conv], axis=-1), head_norm_g[l])
        h = _layernorm(ALPHA * x + mix @ w_out[l], ln1_g[l], ln1_b[l])
        x = _layernorm(ALPHA * h + _peer(h, w_query[l], sub_keys[l], expert_u[l], expert_v[l]),
                       ln2_g[l], ln2_b[l])
    return x


_drawn_inputs = setup_inputs


def setup_inputs(seed=0):
    import zlib

    import numpy as np

    out = dict(_drawn_inputs(seed))
    spreads = {}
    factors = {'cmp_k_pos': 3.051, 'cmp_k_b1': 31.207, 'cmp_v_b1': 2.96, 'ln2_g': 8.508, 'ln2_b': 16.746}
    for name, (base, spread) in spreads.items():
        noise = np.random.default_rng([zlib.crc32(name.encode()), seed]).standard_normal(out[name].shape)
        drawn = base * np.exp(spread * noise) if base else spread * noise
        out[name] = __import__('jax').numpy.asarray(drawn.astype(out[name].dtype))
    for name, factor in factors.items():
        out[name] = (out[name] * factor).astype(out[name].dtype)
    return out
```

```python
import concourse.bass as bass
from concourse import mybir

F32 = mybir.dt.float32
F32R = mybir.dt.float32r
U32 = mybir.dt.uint32
ALU = mybir.AluOpType
ACT = mybir.ActivationFunctionType
AX = mybir.AxisListType

P = 128
D = 2048
SEQ = 256
KC = D // P
HD = 128
NH, NG = 8, 2
R = NH // NG
ATT_W = NH * HD
CONV_W = 1024
KV0 = ATT_W
GATE0 = KV0 + 6 * 256
U0 = GATE0 + 3 * NH
B0 = U0 + CONV_W
C0 = B0 + CONV_W
NCMP = (SEQ - 32) // 16 + 1
CHID = 512
NKEY = 128
TOPK = 16
PH = 8
ET = 128
HALF = ET // 2
ALPHA = 2.0 ** 0.25
SCALE = HD ** -0.5
LN_EPS = 1e-5
RMS_EPS = 1e-6
MASKED = 1e30
SLOPES = [2.0 ** (-8.0 * (h + 1) / NH) for h in range(NH)]

S_KV = 0
S_GRP = S_KV + 16
GRP_SLOTS = 80
S_OUT = S_GRP + NG * GRP_SLOTS
S_Q = S_OUT + 64
S_U = S_Q + 64
S_V = S_U + 4 * ET


def build(nc, x, w_in, cmp_k_pos, cmp_k_w1, cmp_k_b1, cmp_k_w2, cmp_v_pos, cmp_v_w1, cmp_v_b1, cmp_v_w2,
          conv_w, head_norm_g, w_out, ln1_g, ln1_b, w_query, sub_keys, expert_u, expert_v, ln2_g, ln2_b, out):
    h_spill = nc.dram_tensor("h_spill", (SEQ, D), F32).ap()

    x_v = x[0].rearrange("(t p) d -> p t d", p=P)
    out_v = out[0].rearrange("(t p) d -> p t d", p=P)
    h_v = h_spill.rearrange("(t p) d -> p t d", p=P)
    win_v = w_in[0].rearrange("(k p) c -> p k c", p=P)
    kv_v = w_in[0][:, KV0 + 512:GATE0].rearrange("(k p) (b v g c) -> v g b p k c", p=P, b=2, v=2, g=NG)
    wout_v = w_out[0].rearrange("(k p) c -> p k c", p=P)
    wq_v = w_query[0].rearrange("(k p) c -> p k c", p=P)
    w1_v = [w[0].rearrange("(j p) c -> p j c", p=P) for w in (cmp_k_w1, cmp_v_w1)]
    eu_v = expert_u[0].rearrange("(t p) d -> t p d", p=P)
    ev_v = expert_v[0].rearrange("(q e p) (c d) -> q c p e d", e=2, p=P, c=2)

    base = (nc.sbuf_base + 63) // 64 * 64
    top = [base]

    def at(name, shape, dt, offset=None):
        n = 4
        for s in shape[1:]:
            n *= s
        if offset is None:
            offset, top[0] = top[0], top[0] + (n + 31) // 32 * 32
        assert offset + n <= nc.sbuf_usable_end, name
        return nc.alloc_sbuf_tensor_at(name, shape, dt, offset=offset)

    K = 1024
    o_act = top[0]
    act_hi = at("act_hi", [P, KC, SEQ], F32R)
    act_lo = at("act_lo", [P, KC, SEQ], F32R)
    w_hi = at("w_hi", [P, 4, 512], F32R)
    w_lo = at("w_lo", [P, 4, 512], F32R)
    o_ring = top[0]
    u_ring = at("u_ring", [P, 2, D], F32)
    v_ring = at("v_ring", [P, 2, 2, 1024], F32, o_ring)
    w_ring = at("w_ring", [P, 4, 8, 256], F32, o_ring)
    coef = at("coef", [P, ET, SEQ], F32)
    oc = o_ring + 16 * K
    end_coef = oc + 128 * K
    xh = at("xh", [P, 2, D], F32, oc + 16 * K)
    mix_hi = at("mix_hi", [P, KC, SEQ], F32R, oc + 32 * K)
    mix_lo = at("mix_lo", [P, KC, SEQ], F32R, oc + 48 * K)
    pos = [oc + 64 * K]

    def tmp(name, shape, dt=F32):
        n = 4
        for s in shape[1:]:
            n *= s
        t = at(name, shape, dt, pos[0])
        pos[0] += (n + 31) // 32 * 32
        assert pos[0] <= oc + 112 * K, name
        return t

    kT = tmp("kT", [P, 2, SEQ])
    v_sb = tmp("v_sb", [P, 2, 2, HD])
    qT = tmp("qT", [P, R, SEQ])
    sc1 = tmp("sc1", [P, 2, 256])
    sc0 = tmp("sc0", [P, 2, 128])
    scc = tmp("scc", [P, 2, 16])
    pT1 = tmp("pT1", [P, 2, 2, 128])
    pT0 = tmp("pT0", [P, 2, 128])
    pTc = tmp("pTc", [16, 2, 128])
    mx = tmp("mx", [P, 6])
    nmx = tmp("nmx", [P, 6])
    sums = tmp("sums", [P, 6])
    rg = tmp("rg", [P, 6])
    cu = tmp("cu", [P, 2, SEQ + 2])
    dist1 = tmp("dist1", [P, 256])
    dist0 = tmp("dist0", [P, 128])
    distc = tmp("distc", [P, 2, 16])
    validc = tmp("validc", [P, 2, 16])
    nslope = tmp("nslope", [P, NH])
    gates = tmp("gates", [P, NH, 6])
    params = tmp("params", [P, 104])
    prow = tmp("prow", [104, P])
    kc_all = tmp("kc_all", [P, 2, 16])
    vc_all = tmp("vc_all", [16, 2, HD])
    nslope_g = tmp("nslope_g", [P, R])
    gates_g = tmp("gates_g", [P, R, 6])
    conv_g = tmp("conv_g", [P, 3, 4])
    norm_g = tmp("norm_g", [P, 2, 4])
    kc_g = tmp("kc_g", [P, 16])
    vc_g = tmp("vc_g", [16, HD])
    ones = tmp("ones", [P, P])
    onerow = tmp("onerow", [1, 32])
    eps = tmp("eps", [P, 2])
    b1row = tmp("b1row", [1, 2, CHID])
    gsig = tmp("gsig", [P, 2, 3 * NH])
    lnst = tmp("lnst", [P, 2, 4, 6])
    lnmv = tmp("lnmv", [P, 2, 2])
    lnrs = tmp("lnrs", [P, 2])
    assert pos[0] <= oc + 96 * K, pos[0] - oc
    c_sb = tmp("c_sb", [P, 2, SEQ])
    cv = tmp("cv", [P, 2, SEQ])
    y_sb = tmp("y_sb", [P, 8, SEQ])
    sq = tmp("sq", [P, 8, SEQ])
    assert pos[0] <= oc + 116 * K
    w1_ring = at("w1_ring", [P, 4, 4, CHID], F32, oc + 96 * K)
    blk = at("blk", [P, 2, 32, 30], F32, oc + 32 * K)
    hid = at("hid", [32, 2, CHID], F32, oc + 40 * K)
    hidT = at("hidT", [P, 2, 4, 32], F32, oc + 44 * K)
    w2 = at("w2", [P, 2, 4, HD], F32, oc + 46 * K)
    gw = at("gw", [P, KC, 24], F32, oc + 52 * K)
    gw_hi = at("gw_hi", [P, KC, 24], F32R, oc + 54 * K)
    gw_lo = at("gw_lo", [P, KC, 24], F32R, oc + 56 * K)
    ln_g = at("ln_g", [P, D], F32, oc + 112 * K)
    ln_b = at("ln_b", [P, D], F32, oc + 120 * K)
    skeys = at("skeys", [P, 16, P], F32, oc + 32 * K)
    skT = at("skT", [P, 16, P], F32, oc + 40 * K)
    qp = at("qp", [P, 2, 2, SEQ], F32, oc + 48 * K)
    scores = at("scores", [P, 16, 2, NKEY], F32, oc + 112 * K)
    rpos = [oc + 104 * K]

    def rtmp(name, shape, dt=F32):
        n = 4
        for s in shape[1:]:
            n *= s
        t = at(name, shape, dt, rpos[0])
        rpos[0] += (n + 31) // 32 * 32
        assert rpos[0] <= oc + 112 * K, name
        return t

    rs = rtmp("rs", [P, 2, NKEY])
    rs2 = rtmp("rs2", [P, 2, NKEY])
    t_val = rtmp("t_val", [P, 2, TOPK])
    t_idx = rtmp("t_idx", [P, 2, TOPK], U32)
    t_idf = rtmp("t_idf", [P, 2, TOPK])
    cand = rtmp("cand", [P, 16, 16])
    cand2 = rtmp("cand2", [P, 16, 16])
    b_idx = rtmp("b_idx", [P, TOPK], U32)
    b_ij = rtmp("b_ij", [P, 2, TOPK], U32)
    b_ijf = rtmp("b_ijf", [P, 2, TOPK])
    b_val = rtmp("b_val", [P, TOPK])
    eq = rtmp("eq", [P, 2, TOPK, 16])
    b_id = rtmp("b_id", [P, 2, TOPK])
    iota16 = rtmp("iota16", [P, 16])
    picks = at("picks", [P, 3, 16, TOPK], F32, oc + 96 * K)
    picks_t = at("picks_t", [P, 3, 2, PH, TOPK], F32, oc + 99 * K)
    psum_k = at("psum_k", [P, 16], F32, oc + 102 * K)
    res = at("res", [P, 2, D], F32, o_act)
    c_hi = at("c_hi", [P, 2, SEQ], F32R, o_act + 16 * K)
    c_lo = at("c_lo", [P, 2, SEQ], F32R, o_act + 18 * K)
    l2st = at("l2st", [P, 2, 4, 6], F32, o_act + 20 * K)
    l2mv = at("l2mv", [P, 2, 2], F32, o_act + 21 * K)
    l2rs = at("l2rs", [P, 2], F32, o_act + 21 * K + 64)
    eps2 = at("eps2", [P, 1], F32, o_act + 21 * K + 128)
    ln2g_sb = at("ln2g_sb", [P, D], F32, oc)
    ln2b_sb = at("ln2b_sb", [P, D], F32, oc + 8 * K)
    ident = at("ident", [P, P], F32)
    iota = at("iota", [P, P], F32)
    tokT = at("tokT", [P, 3, SEQ], F32)
    oneB = at("oneB", [P, 4, NKEY], F32)
    oneA = at("oneA", [P, 4, HALF], F32)
    tok8 = at("tok8", [P, 3, 8], F32)

    bank = [nc.alloc_psum_tensor(f"bank{i}", [P, 512], F32) for i in range(8)]

    names = """s_const s_x s_small s_cw2 s_skeys s_lnrow s_ln2row s_hspill s_res s_out
        tr_done tr_hi tr_lo params_T params_ok gw_hi_ok gw_ready gate_mm gate_sig gate_ok
        blk_ready w1_used hid_mm hid_ready hidT_mm hidT_ok cmp_mm cmp_ok
        hi_done lo_done slot_used acc_act acc_dve grp_ready
        qk_done biased exps probs_ready pt_done pt_act pt_dve o_done y_att
        squared y_conv norm_mm rms_ok mixf_ready mix_hi_ok mix_ready
        var_ok std_ok ln1_done sk_mm sk_ok score_mm score_ok
        u_tr gelu_done picks_raw picks_exp picks_ok tok_mm tok_ok
        hot_ready hot_used g_mul c_hi_ok c_lo_ok pass_read var2_ok std2_ok final_ok""".split()
    S = {n: nc.alloc_semaphore(n) for n in names}
    s_w = [nc.alloc_semaphore(f"s_w{i}") for i in range(4)]
    s_w1 = [nc.alloc_semaphore(f"s_w1_{i}") for i in range(4)]
    s_u = [nc.alloc_semaphore(f"s_u{i}") for i in range(2)]
    s_v = [nc.alloc_semaphore(f"s_v{i}") for i in range(2)]

    def bview(i, *shape):
        n = 1
        for s in shape:
            n *= s
        names_ = "abc"[:len(shape)]
        if len(shape) == 1:
            return bank[i][:, 0:n]
        return bank[i][:, 0:n].rearrange("p (%s) -> p %s" % (" ".join(names_), " ".join(names_)),
                                         **dict(zip(names_, shape)))

    block_cm = nc.Block()
    block = block_cm.__enter__()

    @block.sync
    def _(sp):
        sp.dma_start(xh[:, :, :], x_v).then_inc(S["s_x"], 16)

        def load_w(c, src, after):
            if after is not None:
                sp.wait_ge(S["lo_done"], after)
            for n in range(2):
                sp.dma_start(w_ring[:, c % 4, 4 * n:4 * n + 4, :], src[:, 4 * n:4 * n + 4, :]
                             ).then_inc(s_w[c % 4], 16)

        for c in range(4):
            t, hh = divmod(c, 2)
            load_w(c, win_v[:, 8 * hh:8 * hh + 8, KV0 + 256 * t:KV0 + 256 * t + 256], None)
        with sp.Fori(0, NG) as g:
            for t in range(10):
                for hh in range(2):
                    c = 2 * t + hh
                    after = S_GRP + GRP_SLOTS * g + 4 * (c - 3)
                    if t < 2:
                        sp.wait_ge(S["lo_done"], after)
                        for b in range(2):
                            src = kv_v[t, bass.ds(g, 1), b].rearrange("g p k c -> p k (g c)")
                            sp.dma_start(w_ring[:, c % 4, :, 128 * b:128 * b + 128],
                                         src[:, 8 * hh:8 * hh + 8, :]).then_inc(s_w[c % 4], 16)
                        continue
                    col = (0, 256, C0, U0, B0, C0 + 256, U0 + 256, B0 + 256)[t - 2] + 512 * g
                    load_w(c, win_v[:, 8 * hh:8 * hh + 8, bass.ds(col, 256)], after)
        for s0, view in ((S_OUT, wout_v), (S_Q, wq_v)):
            with sp.Fori(0, 4) as j:
                for c in range(4):
                    t, hh = divmod(c, 2)
                    load_w(c, view[:, 8 * hh:8 * hh + 8, bass.ds(512 * j + 256 * t, 256)],
                           s0 + 16 * j + 4 * (c - 3))

        def load_u(t, r):
            sp.dma_start(u_ring[:, r, :], eu_v[bass.ds(t, 1)].rearrange("t p d -> p (t d)")).then_inc(s_u[r], 16)

        for r in range(2):
            sp.wait_ge(S["lo_done"], S_U - 8 + 4 * r)
            load_u(r, r)
        with sp.Fori(1, ET // 2) as j:
            for r in range(2):
                sp.wait_ge(S["u_tr"], 8 * j + 4 * r - 4)
                load_u(2 * j + r, r)
        sp.wait_ge(S["slot_used"], S_V)
        sp.dma_start(res[:, :, :], h_v).then_inc(S["s_res"], 16)
        for cc in range(2):
            def load_v(q, r):
                sp.dma_start(v_ring[:, r, :, :],
                             ev_v[bass.ds(q, 1), cc].rearrange("q p e d -> p (q e) d")).then_inc(s_v[r], 16)

            if cc == 0:
                for r in range(2):
                    load_v(r, r)
            with sp.Fori(1 - cc, 32) as j:
                for r in range(2):
                    sp.wait_ge(S["lo_done"], S_V + 256 * cc + 8 * j + 4 * r - 4)
                    load_v(2 * j + r, r)
            if cc == 1:
                sp.wait_ge(S["slot_used"], S_V + 2 * ET + 64)
                sp.dma_start(ln2g_sb[:, :], ln2_g.partition_broadcast(P).rearrange("p a d -> p (a d)")).then_inc(S["s_ln2row"], 16)
                sp.dma_start(ln2b_sb[:, :], ln2_b.partition_broadcast(P).rearrange("p a d -> p (a d)")).then_inc(S["s_ln2row"], 16)
        for t in range(2):
            sp.wait_ge(S["final_ok"], t + 1)
            sp.dma_start(out_v[:, t, :], res[:, t, :]).then_inc(S["s_out"], 16)
        sp.wait_ge(S["s_out"], 32)

    @block.gpsimd
    def _(pool):
        small = [
            (prow[0:24, :], conv_w[0].rearrange("j (b c) -> (j b) c", c=P)),
            (prow[24:40, :], head_norm_g[0].rearrange("(b c) -> b c", c=P)),
            (prow[40:72, :], cmp_k_pos[0]),
            (prow[72:104, :], cmp_v_pos[0]),
            (b1row[0:1, 0, :], cmp_k_b1),
            (b1row[0:1, 1, :], cmp_v_b1),
            (gw[:, :, :], win_v[:, :, GATE0:GATE0 + 24]),
        ]
        for dst, src in small:
            pool.dma_start(dst, src).then_inc(S["s_small"], 16)
        for kv in range(2):
            pool.dma_start(w2[:, kv, :, :], (cmp_k_w2, cmp_v_w2)[kv][0].rearrange("(m p) d -> p m d", p=P)
                           ).then_inc(S["s_cw2"], 16)
        for c in range(4):
            pool.dma_start(w1_ring[:, c, :, :], w1_v[0][:, 4 * c:4 * c + 4, :]).then_inc(s_w1[c], 16)
        nc.gpsimd.memset(ident[:, :], 0.0)
        nc.gpsimd.memset(ones[:, :], 1.0 / HD)
        nc.gpsimd.memset(onerow[:, :], 1.0)
        nc.gpsimd.memset(eps[:, 0:1], RMS_EPS)
        nc.gpsimd.memset(eps[:, 1:2], LN_EPS)
        nc.gpsimd.memset(cu[:, :, :], 0.0)
        nc.gpsimd.memset(scc[:, :, :], 0.0)
        nc.gpsimd.memset(validc[:, :, :], 1.0)
        nc.gpsimd.memset(kc_all[:, :, :], 0.0)
        for h in range(NH):
            nc.gpsimd.memset(nslope[:, h:h + 1], -SLOPES[h])
        kw = dict(allow_small_or_imprecise_dtypes=True)
        nc.gpsimd.iota(iota[:, :], [[1, P]], base=0, channel_multiplier=0, **kw)
        nc.gpsimd.iota(dist1[:, :], [[-1, 256]], base=128, channel_multiplier=1, **kw)
        nc.gpsimd.iota(dist0[:, :], [[-1, 128]], base=0, channel_multiplier=1, **kw)
        nc.gpsimd.iota(distc[:, :, :], [[128, 2], [-16, 16]], base=0, channel_multiplier=1, **kw)
        pool.drain()
        nc.gpsimd.tensor_scalar(distc[:, :, :], distc[:, :, :], -15.5, None, ALU.add)
        nc.gpsimd.affine_select(out=ident[:, :], in_=ident[:, :], compare_op=ALU.not_equal, fill=1.0,
                                base=0, pattern=[[-1, P]], channel_multiplier=1)
        nc.gpsimd.affine_select(out=dist1[:, :], in_=dist1[:, :], compare_op=ALU.is_ge, fill=MASKED,
                                base=128, pattern=[[-1, 256]], channel_multiplier=1)
        nc.gpsimd.affine_select(out=dist0[:, :], in_=dist0[:, :], compare_op=ALU.is_ge, fill=MASKED,
                                base=0, pattern=[[-1, 128]], channel_multiplier=1)
        pool.drain()
        nc.gpsimd.affine_select(out=distc[:, :, :], in_=distc[:, :, :], compare_op=ALU.is_ge, fill=MASKED,
                                base=-31, pattern=[[128, 2], [-16, 16]], channel_multiplier=1)
        nc.gpsimd.affine_select(out=validc[:, :, :], in_=validc[:, :, :], compare_op=ALU.is_ge, fill=0.0,
                                base=-31, pattern=[[128, 2], [-16, 16]], channel_multiplier=1)
        pool.drain()
        pool.nop().then_inc(S["s_const"], 1)
        for i in range(4, 16):
            pool.wait_ge(S["w1_used"], i - 3)
            pool.dma_start(w1_ring[:, i % 4, :, :], w1_v[i // 8][:, 4 * (i % 8):4 * (i % 8) + 4, :]
                           ).then_inc(s_w1[i % 4], 16)
        pool.wait_ge(S["w1_used"], 16)
        pool.dma_start(ln_g[:, :], ln1_g.partition_broadcast(P).rearrange("p a d -> p (a d)")).then_inc(S["s_lnrow"], 16)
        pool.dma_start(ln_b[:, :], ln1_b.partition_broadcast(P).rearrange("p a d -> p (a d)")).then_inc(S["s_lnrow"], 16)
        pool.wait_ge(S["slot_used"], S_Q)
        pool.dma_start(skeys[:, :, :], sub_keys[0].rearrange("h c n d -> n (h c) d")).then_inc(S["s_skeys"], 16)
        pool.wait_ge(S["ln1_done"], 2)
        pool.dma_start(h_v, xh[:, :, :]).then_inc(S["s_hspill"], 16)
        pool.wait_ge(S["s_hspill"], 16)

    @block.tensor
    def _(pe):
        def tile(kind, acc, s, lo=0, hi=8):
            for c in range(lo, hi):
                pe.wait_ge(S["lo_done"], s + c + 1)
                r = c % 4
                for kk in range(2):
                    k = 2 * c + kk
                    for b in range(2):
                        o = bank[acc][:, 256 * b:256 * b + 256]
                        half = slice(128 * b, 128 * b + 128)
                        if kind == "T":
                            w = slice(256 * kk + 128 * b, 256 * kk + 128 * b + 128)
                            pairs = ((w_hi[:, r, w], act_hi[:, k, :]), (w_hi[:, r, w], act_lo[:, k, :]),
                                     (w_lo[:, r, w], act_hi[:, k, :]))
                        else:
                            a_hi, a_lo = (act_hi, act_lo) if kind == "V" else (mix_hi, mix_lo)
                            w = slice(256 * kk, 256 * kk + 256)
                            pairs = ((a_hi[:, k, half], w_hi[:, r, w]), (a_hi[:, k, half], w_lo[:, r, w]),
                                     (a_lo[:, k, half], w_hi[:, r, w]))
                        for n, (st, mv) in enumerate(pairs):
                            ins = nc.tensor.matmul(o, st, mv, start=(k == 0 and b == 0 and n == 0),
                                                   stop=(k == KC - 1 and n == 2), skip_group_check=True)
                ins.then_inc(S["slot_used"], 1)

        def transpose_act(n0):
            for u in range(8):
                n = n0 + u
                if n >= 4:
                    pe.wait_ge(S["tr_lo"], n - 3)
                for kk in range(2):
                    for t in range(2):
                        col = 128 * (2 * u + kk)
                        ins = nc.tensor.transpose(bank[4 + u % 4][:, 256 * kk + 128 * t:256 * kk + 128 * t + 128],
                                                  xh[:, t, col:col + 128], ident[:, :])
                ins.then_inc(S["tr_done"], 1)

        pe.wait_ge(S["s_const"], 1)
        pe.wait_ge(S["s_x"], 16)
        transpose_act(0)
        pe.wait_ge(S["s_small"], 16 * 7)
        nc.tensor.transpose(bank[2][:, 0:104], prow[0:104, :], ident[0:104, 0:104]).then_inc(S["params_T"], 1)
        pe.wait_ge(S["tr_lo"], 8)
        for t in range(2):
            tile("T", t, S_KV + 8 * t)
        pe.wait_ge(S["gw_ready"], 1)
        for t in range(2):
            tk = slice(128 * t, 128 * t + 128)
            for k in range(KC):
                o = bank[3][:, 32 * t:32 * t + 24]
                nc.tensor.matmul(o, act_hi[:, k, tk], gw_hi[:, k, :], start=(k == 0), stop=False)
                nc.tensor.matmul(o, act_hi[:, k, tk], gw_lo[:, k, :], start=False, stop=False)
                ins = nc.tensor.matmul(o, act_lo[:, k, tk], gw_hi[:, k, :], start=False, stop=(k == KC - 1))
        ins.then_inc(S["gate_mm"], 1)
        pe.wait_ge(S["params_ok"], 1)
        for kv in range(2):
            pe.wait_ge(S["blk_ready"], kv + 1)
            for c in range(8):
                i = 8 * kv + c
                pe.wait_ge(s_w1[i % 4], 16 * (i // 4 + 1))
                for jj in range(4):
                    ins = nc.tensor.matmul(bank[(2, 4)[kv]][0:30, :], blk[:, kv, 4 * c + jj, :],
                                           w1_ring[:, i % 4, jj, :], start=(c == 0 and jj == 0), stop=False)
                ins.then_inc(S["w1_used"], 1)
            nc.tensor.matmul(bank[(2, 4)[kv]][0:30, :], onerow[0:1, 0:30], b1row[0:1, kv, :],
                             start=False, stop=True).then_inc(S["hid_mm"], 1)
        pe.wait_ge(S["hid_ready"], 2)
        for kv in range(2):
            for m in range(4):
                o = bank[5][:, 128 * kv + 32 * m:128 * kv + 32 * m + 30]
                ins = nc.tensor.transpose(o, hid[0:30, kv, 128 * m:128 * m + 128], ident[0:30, 0:30])
        ins.then_inc(S["hidT_mm"], 1)
        pe.wait_ge(S["hidT_ok"], 1)
        pe.wait_ge(S["s_cw2"], 32)
        for m in range(4):
            nc.tensor.matmul(bank[6][:, 0:30], w2[:, 0, m, :], hidT[:, 0, m, 0:30], start=(m == 0), stop=(m == 3))
        for g in range(NG):
            for m in range(4):
                ins = nc.tensor.matmul(bank[7][0:NCMP, 128 * g:128 * g + 128], hidT[:, 1, m, 15 * g:15 * g + 15],
                                       w2[:, 1, m, :], start=(m == 0), stop=(m == 3))
        ins.then_inc(S["cmp_mm"], 1)
        pe.wait_ge(S["cmp_ok"], 1)
        pe.wait_ge(S["gate_sig"], 1)

        with pe.Fori(0, NG) as g:
            s = S_GRP + GRP_SLOTS * g

            def score(r):
                for b in range(2):
                    nc.tensor.matmul(bank[2][:, 256 * b:256 * b + 256], qT[:, r, 128:256], kT[:, b, :],
                                     start=True, stop=True)
                for b in range(2):
                    nc.tensor.matmul(bank[3][:, 128 * b:128 * b + 128], qT[:, r, 0:128], kT[:, b, 0:128],
                                     start=True, stop=True)
                for t in range(2):
                    ins = nc.tensor.matmul(bank[3][:, 256 + 16 * t:272 + 16 * t], qT[:, r, 128 * t:128 * t + 128],
                                           kc_g[:, :], start=True, stop=True)
                ins.then_inc(S["qk_done"], 1)

            def transpose_probs(r):
                pe.wait_ge(S["probs_ready"], R * g + r + 1)
                for b in range(2):
                    for c in range(2):
                        nc.tensor.transpose(bank[4][:, 256 * b + 128 * c:256 * b + 128 * c + 128],
                                            sc1[:, b, 128 * c:128 * c + 128], ident[:, :])
                for b in range(2):
                    nc.tensor.transpose(bank[5][:, 128 * b:128 * b + 128], sc0[:, b, :], ident[:, :])
                for t in range(2):
                    ins = nc.tensor.transpose(bank[5][0:16, 256 + 128 * t:384 + 128 * t], scc[:, t, :], ident[:, :])
                ins.then_inc(S["pt_done"], 1)

            def attend(r):
                pe.wait_ge(S["pt_act"], R * g + r + 1)
                pe.wait_ge(S["pt_dve"], R * g + r + 1)
                if r:
                    pe.wait_ge(S["y_att"], R * g + r)
                parts0 = [(v_sb[:, 0, b, :], pT0[:, b, :]) for b in range(2)]
                parts0.append((vc_g[0:NCMP, :], pTc[0:NCMP, 0, :]))
                parts1 = [(v_sb[:, c, b, :], pT1[:, b, c, :]) for b in range(2) for c in range(2)]
                parts1.append((vc_g[0:NCMP, :], pTc[0:NCMP, 1, :]))
                for t, parts in ((0, parts0), (1, parts1)):
                    for n, (vv, pp) in enumerate(parts):
                        ins = nc.tensor.matmul(bank[6][:, 128 * t:128 * t + 128], vv, pp,
                                               start=(n == 0), stop=(n == len(parts) - 1))
                ins.then_inc(S["o_done"], 1)

            pe.wait_ge(S["acc_dve"], 4 * g + 1)
            tile("T", 0, s)
            pe.wait_ge(S["acc_dve"], 4 * g + 2)
            tile("V", 1, s + 8)
            pe.wait_ge(S["acc_act"], 6 * g + 1)
            tile("T", 0, s + 16)
            pe.wait_ge(S["acc_act"], 6 * g + 2)
            tile("T", 1, s + 24)
            pe.wait_ge(S["acc_act"], 6 * g + 3)
            pe.wait_ge(S["grp_ready"], g + 1)
            score(0)
            tile("T", 0, s + 32)
            transpose_probs(0)
            score(1)
            pe.wait_ge(S["acc_act"], 6 * g + 4)
            tile("T", 1, s + 40)
            attend(0)
            transpose_probs(1)
            score(2)
            pe.wait_ge(S["acc_act"], 6 * g + 5)
            tile("T", 0, s + 48)
            attend(1)
            transpose_probs(2)
            score(3)
            pe.wait_ge(S["acc_dve"], 4 * g + 3)
            tile("T", 1, s + 56)
            attend(2)
            transpose_probs(3)
            pe.wait_ge(S["acc_dve"], 4 * g + 4)
            tile("T", 0, s + 64)
            attend(3)
            pe.wait_ge(S["acc_act"], 6 * g + 6)
            tile("T", 1, s + 72)
            for n in range(4):
                pe.wait_ge(S["squared"], 4 * g + n + 1)
                nc.tensor.matmul(bank[2 + n][:, :], ones[:, :],
                                 sq[:, 2 * n:2 * n + 2, :].rearrange("p a t -> p (a t)"),
                                 start=True, stop=True).then_inc(S["norm_mm"], 1)

        pe.wait_ge(S["mix_ready"], NG)
        with pe.Fori(0, 4) as j:
            for t in range(2):
                pe.wait_ge(S["acc_dve"], 1 + 4 * NG + 2 * j + t)
                tile("M", t, S_OUT + 16 * j + 8 * t)

        pe.wait_ge(S["s_skeys"], 16)
        for n in range(4):
            if n >= 2:
                pe.wait_ge(S["sk_ok"], n - 1)
            for i in range(4):
                ins = nc.tensor.transpose(bank[2 + n % 2][:, 128 * i:128 * i + 128], skeys[:, 4 * n + i, :], ident[:, :])
            ins.then_inc(S["sk_mm"], 1)
        pe.wait_ge(S["ln1_done"], 2)
        transpose_act(8)
        pe.wait_ge(S["tr_lo"], 16)
        pe.wait_ge(S["sk_ok"], 4)
        pe.wait_ge(S["acc_dve"], 2 + 4 * NG + 8)

        def scores_of(h, b):
            pe.wait_ge(S["acc_act"], 6 * NG + h + 1)
            for t in range(2):
                for c in range(2):
                    ins = nc.tensor.matmul(bank[2 + b][:, 256 * t + 128 * c:256 * t + 128 * c + 128],
                                           qp[:, b, c, 128 * t:128 * t + 128],
                                           skT[:, bass.ds(2 * h + c, 1), :].rearrange("p a n -> p (a n)"),
                                           start=True, stop=True)
            ins.then_inc(S["score_mm"], 1)

        with pe.Fori(0, 4) as j:
            s = S_Q + 16 * j
            pe.wait_ge(S["acc_act"], 6 * NG + 2 * j)
            tile("T", 0, s)
            tile("T", 1, s + 8, 0, 4)
            scores_of(2 * j, 0)
            tile("T", 1, s + 8, 4, 8)
            scores_of(2 * j + 1, 1)
        pe.wait_ge(S["score_ok"], 8)

        def transpose_u(count, k, slot):
            if k == 0:
                pe.wait_ge(s_u[slot], count)
            for i in range(4):
                col = 512 * k + 128 * i
                ins = nc.tensor.transpose(bank[4 + k][:, 128 * i:128 * i + 128],
                                          u_ring[:, slot, col:col + 128], ident[:, :])
            ins.then_inc(S["u_tr"], 1)

        def gate_token(nb, c):
            if c % 8 == 0 and not (isinstance(nb, int) and nb == 0):
                pe.wait_ge(S["g_mul"], nb + c // 8 - 1)
            pe.wait_ge(S["hot_ready"], 8 * nb + c + 1)
            nc.tensor.matmul(bank[2 + c // 8][:, HALF * (c % 8):HALF * (c % 8) + HALF], oneB[:, c % 4, :],
                             oneA[:, c % 4, :], start=True, stop=True).then_inc(S["hot_used"], 1)

        def u_body(i, nb, last):
            for c in range(16):
                tt, k = divmod(c, 4)
                if not (last and c >= 13):
                    at_, ak = divmod(c + 3, 4)
                    transpose_u(16 * (2 * i + at_ // 2 + 1), ak, at_ % 2)
                pe.wait_ge(S["lo_done"], S_U + 16 * i + c + 1)
                if k == 0 and not (isinstance(i, int) and 4 * i + tt < 2):
                    pe.wait_ge(S["gelu_done"], 4 * i + tt - 1)
                for n in range(4):
                    dk = 4 * k + n
                    o = bank[tt % 2][:, 0:SEQ]
                    wh, wl = w_hi[:, k, 128 * n:128 * n + 128], w_lo[:, k, 128 * n:128 * n + 128]
                    nc.tensor.matmul(o, wh, act_hi[:, dk, :], start=(dk == 0), stop=False)
                    nc.tensor.matmul(o, wh, act_lo[:, dk, :], start=False, stop=False)
                    ins = nc.tensor.matmul(o, wl, act_hi[:, dk, :], start=False, stop=(dk == KC - 1))
                ins.then_inc(S["slot_used"], 1)
                if nb is not None:
                    gate_token(nb, c)

        for k in range(3):
            transpose_u(16, k, 0)
        u_body(0, None, False)
        with pe.Fori(1, 16) as i:
            u_body(i, None, False)
        pe.wait_ge(S["picks_ok"], 1)
        for n in range(6):
            a, t = divmod(n, 2)
            ins = nc.tensor.transpose(bank[2 + n // 4][:, 128 * (n % 4):128 * (n % 4) + 128],
                                      picks_t[:, a, t, :, :].rearrange("p h k -> p (h k)"), ident[:, :])
        ins.then_inc(S["tok_mm"], 1)
        pe.wait_ge(S["tok_ok"], 1)
        u_body(16, 0, False)
        with pe.Fori(17, 31) as i:
            u_body(i, 2 * i - 32, False)
        u_body(31, 30, True)

        def v_body(cc, i, nb, first, last):
            b0 = 4 - 4 * cc
            for tt in range(4):
                pe.wait_ge(S["c_lo_ok"], ET * cc + 4 * i + tt + 1)
                for jc in range(2):
                    c = 2 * tt + jc
                    r = c % 4
                    pe.wait_ge(S["lo_done"], S_V + 2 * ET * cc + 8 * i + c + 1)
                    for t in range(2):
                        o = bank[b0 + 2 * t + jc][:, :]
                        tk = slice(128 * t, 128 * t + 128)
                        nc.tensor.matmul(o, c_hi[:, tt % 2, tk], w_hi[:, r, :], start=first and tt == 0, stop=False)
                        nc.tensor.matmul(o, c_hi[:, tt % 2, tk], w_lo[:, r, :], start=False, stop=False)
                        ins = nc.tensor.matmul(o, c_lo[:, tt % 2, tk], w_hi[:, r, :], start=False,
                                               stop=last and tt == 3)
                    ins.then_inc(S["slot_used"], 1)
                    if nb is not None:
                        for q in range(2):
                            gate_token(nb, 2 * c + q)

        v_body(0, 0, 32, True, False)
        with pe.Fori(1, 16) as i:
            v_body(0, i, 32 + 2 * i, False, False)
        with pe.Fori(16, 31) as i:
            v_body(0, i, None, False, False)
        v_body(0, 31, None, False, True)
        pe.wait_ge(S["g_mul"], 64)
        v_body(1, 0, None, True, False)
        with pe.Fori(1, 31) as i:
            v_body(1, i, None, False, False)
        v_body(1, 31, None, False, True)

    @block.scalar
    def _(act):
        def hi_w(s, c, n):
            for q in range(c, c + n):
                if q % 4 == 0:
                    act.wait_ge(s_w[(q // 4) % 4], s_count(s, q))
                if not (isinstance(s, int) and s + q < 4):
                    act.wait_ge(S["slot_used"], s + q - 3)
                src = w_ring[:, (q // 4) % 4, 2 * (q % 4):2 * (q % 4) + 2, :].rearrange("p k c -> p (k c)")
                nc.scalar.activation(w_hi[:, q % 4, :], src, ACT.Copy).then_inc(S["hi_done"], 1)

        def s_count(s, q):
            return 2 * s + (q // 16 + 1) * 32

        def transpose_hi(n0):
            for u in range(8):
                act.wait_ge(S["tr_done"], n0 + u + 1)
                nc.scalar.activation(act_hi[:, 2 * u:2 * u + 2, :], bview(4 + u % 4, 2, SEQ), ACT.Copy
                                     ).then_inc(S["tr_hi"], 1)

        transpose_hi(0)
        hi_w(S_KV, 0, 8)
        act.wait_ge(S["s_small"], 16 * 7)
        nc.scalar.activation(gw_hi[:, :, :], gw[:, :, :], ACT.Copy).then_inc(S["gw_hi_ok"], 1)
        hi_w(S_KV, 8, 8)
        act.wait_ge(S["gate_mm"], 1)
        nc.scalar.activation(gsig[:, :, :], bank[3][:, 0:64].rearrange("p (t c) -> p t c", t=2)[:, :, 0:24],
                             ACT.Sigmoid).then_inc(S["gate_sig"], 1)
        for kv in range(2):
            act.wait_ge(S["hid_mm"], kv + 1)
            nc.scalar.activation(hid[0:30, kv, :], bank[(2, 4)[kv]][0:30, :], ACT.Gelu_apprx_tanh
                                 ).then_inc(S["hid_ready"], 1)
        hi_w(S_GRP, 0, 4)
        with act.Fori(0, NG) as g:
            s = S_GRP + GRP_SLOTS * g

            def expo(r):
                act.wait_ge(S["biased"], R * g + r + 1)
                for b in range(2):
                    nc.scalar.activation(sc1[:, b, :], sc1[:, b, :], ACT.Exp, bias=nmx[:, b:b + 1],
                                         accum_out=sums[:, b:b + 1])
                for b in range(2):
                    nc.scalar.activation(sc0[:, b, :], sc0[:, b, :], ACT.Exp, bias=nmx[:, 2 + b:3 + b],
                                         accum_out=sums[:, 2 + b:3 + b])
                for t in range(2):
                    ins = nc.scalar.activation(scc[:, t, 0:NCMP], scc[:, t, 0:NCMP], ACT.Exp,
                                               bias=nmx[:, 4 + t:5 + t], accum_out=sums[:, 4 + t:5 + t])
                ins.then_inc(S["exps"], 1)

            def probs_out(r):
                act.wait_ge(S["pt_done"], R * g + r + 1)
                nc.scalar.activation(pT1[:, :, :, :].rearrange("p b c t -> p (b c t)"), bank[4][:, :], ACT.Copy
                                     ).then_inc(S["pt_act"], 1)

            def att_out(r):
                act.wait_ge(S["o_done"], R * g + r + 1)
                nc.scalar.activation(y_sb[:, r, :], bank[6][:, 0:SEQ], ACT.Copy).then_inc(S["y_att"], 1)

            def tile_out(dst, src, end, scale=1.0):
                act.wait_ge(S["slot_used"], s + end)
                nc.scalar.activation(dst, src, ACT.Copy, scale=scale).then_inc(S["acc_act"], 1)

            hi_w(s, 4, 8)
            tile_out(kT[:, :, :], bview(0, 2, SEQ), 8)
            hi_w(s, 12, 8)
            tile_out(v_sb[:, :, :, :].rearrange("p t b c -> p (t b c)"), bank[1][:, :], 16)
            hi_w(s, 20, 8)
            tile_out(qT[:, 0:2, :], bview(0, 2, SEQ), 24, SCALE)
            hi_w(s, 28, 8)
            tile_out(qT[:, 2:4, :], bview(1, 2, SEQ), 32, SCALE)
            expo(0)
            hi_w(s, 36, 8)
            tile_out(c_sb[:, :, :], bview(0, 2, SEQ), 40)
            probs_out(0)
            expo(1)
            hi_w(s, 44, 8)
            att_out(0)
            probs_out(1)
            expo(2)
            hi_w(s, 52, 8)
            att_out(1)
            probs_out(2)
            expo(3)
            hi_w(s, 60, 8)
            tile_out(c_sb[:, :, :], bview(1, 2, SEQ), 64)
            att_out(2)
            probs_out(3)
            hi_w(s, 68, 8)
            att_out(3)
            act.drain()
            for n in range(2):
                nc.scalar.activation(sq[:, 2 * n:2 * n + 2, :], y_sb[:, 2 * n:2 * n + 2, :], ACT.Square
                                     ).then_inc(S["squared"], 1)
            hi_w(s, 76, 8)
            for n in range(2, 4):
                act.wait_ge(S["y_conv"], 2 * g + n - 1)
                nc.scalar.activation(sq[:, 2 * n:2 * n + 2, :], y_sb[:, 2 * n:2 * n + 2, :], ACT.Square
                                     ).then_inc(S["squared"], 1)
            for n in range(4):
                act.wait_ge(S["norm_mm"], 4 * g + n + 1)
                nc.scalar.activation(sq[:, 2 * n:2 * n + 2, :], bview(2 + n, 2, SEQ), ACT.Sqrt,
                                     bias=eps[:, 0:1]).then_inc(S["rms_ok"], 1)
            for n in range(2):
                act.wait_ge(S["mixf_ready"], 2 * g + n + 1)
                nc.scalar.activation(mix_hi[:, bass.ds(R * g + 8 * n, R), :], y_sb[:, 4 * n:4 * n + 4, :], ACT.Copy
                                     ).then_inc(S["mix_hi_ok"], 1)
        with act.Fori(0, 4) as j:
            hi_w(S_OUT + 16 * j, 4, 16)
        act.wait_ge(S["var_ok"], 1)
        nc.scalar.activation(lnrs[:, :], lnmv[:, :, 1], ACT.Sqrt, bias=eps[:, 1:2]).then_inc(S["std_ok"], 1)
        for n in range(4):
            act.wait_ge(S["sk_mm"], n + 1)
            nc.scalar.activation(skT[:, 4 * n:4 * n + 4, :].rearrange("p a n -> p (a n)"), bank[2 + n % 2][:, :],
                                 ACT.Copy).then_inc(S["sk_ok"], 1)
        transpose_hi(8)

        def head_out(h, b, slots):
            act.wait_ge(S["slot_used"], slots)
            nc.scalar.activation(qp[:, b, :, :], bview(b, 2, SEQ), ACT.Copy).then_inc(S["acc_act"], 1)

        def score_out(h, b):
            act.wait_ge(S["score_mm"], h + 1)
            nc.scalar.activation(scores[:, bass.ds(2 * h, 2), :, :], bview(2 + b, 2, 2, NKEY), ACT.Copy
                                 ).then_inc(S["score_ok"], 1)

        def q_body(j, last):
            s = S_Q + 16 * j
            hi_w(s, 4, 8)
            head_out(2 * j, 0, s + 8)
            hi_w(s, 12, 4)
            score_out(2 * j, 0)
            if not last:
                hi_w(s, 16, 4)
            head_out(2 * j + 1, 1, s + 16)
            score_out(2 * j + 1, 1)

        with act.Fori(0, 3) as j:
            q_body(j, False)
        q_body(3, True)

        def hi_u(i, c):
            act.wait_ge(S["u_tr"], 16 * i + c + 1)
            act.wait_ge(S["slot_used"], S_U + 16 * i + c - 3)
            nc.scalar.activation(w_hi[:, c % 4, :], bank[4 + c % 4][:, :], ACT.Copy).then_inc(S["hi_done"], 1)

        def u_body(i, last):
            for tt in range(4):
                for c in range(4 * tt + 3, 4 * tt + 7):
                    if not (last and c >= 16):
                        hi_u(i, c)
                act.wait_ge(S["slot_used"], S_U + 16 * i + 4 * tt + 4)
                nc.scalar.activation(coef[:, bass.ds(4 * i + tt, 1), :].rearrange("p a t -> p (a t)"),
                                     bank[tt % 2][:, 0:SEQ], ACT.Gelu_apprx_tanh).then_inc(S["gelu_done"], 1)

        act.wait_ge(S["s_hspill"], 16)
        for c in range(3):
            hi_u(0, c)
        with act.Fori(0, 16) as i:
            u_body(i, False)
        act.wait_ge(S["picks_raw"], 1)
        nc.scalar.activation(picks[:, 2, :, :], picks[:, 2, :, :], ACT.Exp).then_inc(S["picks_exp"], 1)
        with act.Fori(16, 31) as i:
            u_body(i, False)
        u_body(31, True)

        def v_body(cc, i, waits_gates):
            for tt in range(4):
                n = ET * cc + 4 * i + tt
                if not (isinstance(n, int) and n < 2):
                    act.wait_ge(S["slot_used"], S_V + 2 * n - 2)
                nc.scalar.activation(c_hi[:, tt % 2, :], coef[:, bass.ds(4 * i + tt, 1), :].rearrange("p a t -> p (a t)"),
                                     ACT.Copy).then_inc(S["c_hi_ok"], 1)
                for jc in range(2):
                    c = 2 * tt + jc
                    if tt % 2 == 0 and jc == 0:
                        act.wait_ge(s_v[tt // 2], 16 * (32 * cc + i + 1))
                    act.wait_ge(S["slot_used"], S_V + 2 * ET * cc + 8 * i + c - 3)
                    nc.scalar.activation(w_hi[:, c % 4, :], v_ring[:, tt // 2, tt % 2, 512 * jc:512 * jc + 512],
                                         ACT.Copy).then_inc(S["hi_done"], 1)

        act.wait_ge(S["g_mul"], 32)
        v_body(0, 0, False)
        with act.Fori(1, 16) as i:
            v_body(0, i, False)
        act.wait_ge(S["g_mul"], 64)
        with act.Fori(16, 32) as i:
            v_body(0, i, False)
        with act.Fori(0, 32) as i:
            v_body(1, i, False)
        act.wait_ge(S["var2_ok"], 1)
        nc.scalar.activation(l2rs[:, :], l2mv[:, :, 1], ACT.Sqrt, bias=eps2[:, 0:1]).then_inc(S["std2_ok"], 1)

    @block.vector
    def _(dve):
        V = nc.vector

        def lo_w(s, c, n):
            for q in range(c, c + n):
                dve.wait_ge(S["hi_done"], s + q + 1)
                src = w_ring[:, (q // 4) % 4, 2 * (q % 4):2 * (q % 4) + 2, :].rearrange("p k c -> p (k c)")
                V.tensor_tensor(w_lo[:, q % 4, :], src, w_hi[:, q % 4, :].bitcast(F32), ALU.subtract
                                ).then_inc(S["lo_done"], 1)

        def transpose_lo(n0):
            for u in range(8):
                dve.wait_ge(S["tr_hi"], n0 + u + 1)
                V.tensor_tensor(act_lo[:, 2 * u:2 * u + 2, :], bview(4 + u % 4, 2, SEQ),
                                act_hi[:, 2 * u:2 * u + 2, :].bitcast(F32), ALU.subtract).then_inc(S["tr_lo"], 1)

        transpose_lo(0)
        lo_w(S_KV, 0, 8)
        dve.wait_ge(S["params_T"], 1)
        V.tensor_copy(params[:, :], bank[2][:, 0:104]).then_inc(S["params_ok"], 1)
        dve.wait_ge(S["gw_hi_ok"], 1)
        V.tensor_tensor(gw_lo[:, :, :], gw[:, :, :], gw_hi[:, :, :].bitcast(F32), ALU.subtract
                        ).then_inc(S["gw_ready"], 1)
        dve.drain()

        def blocks(kv):
            dve.wait_ge(S["slot_used"], S_KV + 8 * (kv + 1))
            for g in range(NG):
                for hh in range(2):
                    src = bank[kv][:, 256 * g + 16 * hh:256 * g + 16 * hh + 240].rearrange("p (n s) -> p s n", s=16)
                    add = params[:, 40 + 32 * kv + 16 * hh:56 + 32 * kv + 16 * hh].unsqueeze(2).to_broadcast([P, 16, NCMP])
                    ins = V.tensor_tensor(blk[:, kv, 16 * hh:16 * hh + 16, 15 * g:15 * g + 15], src, add, ALU.add)
            dve.drain().then_inc(S["blk_ready"], 1)
            dve.drain().then_inc(S["acc_dve"], 1)

        lo_w(S_KV, 8, 4)
        blocks(0)
        lo_w(S_KV, 12, 4)
        blocks(1)
        dve.wait_ge(S["gate_sig"], 1)
        for n, (t, b) in enumerate(((1, 1), (1, 2), (0, 1), (0, 2), (0, 0), (1, 0))):
            V.tensor_copy(gates[:, :, n], gsig[:, t, :].rearrange("p (h b) -> p h b", b=3)[:, :, b])
        dve.wait_ge(S["hidT_mm"], 1)
        V.tensor_copy(hidT[:, :, :, 0:30], bank[5][:, 0:256].rearrange("p (a m n) -> p a m n", a=2, m=4)[:, :, :, 0:30]
                      ).then_inc(S["hidT_ok"], 1)
        dve.wait_ge(S["cmp_mm"], 1)
        V.tensor_copy(kc_all[:, :, 0:NCMP], bank[6][:, 0:30].rearrange("p (g n) -> p g n", g=2))
        V.tensor_copy(vc_all[0:NCMP, :, :], bank[7][0:NCMP, 0:256].rearrange("p (g n) -> p g n", g=2)
                      ).then_inc(S["cmp_ok"], 1)
        lo_w(S_GRP, 0, 4)
        dve.drain()
        with dve.Fori(0, NG) as g:
            s = S_GRP + GRP_SLOTS * g

            def squeeze1(ap):
                return ap.rearrange("p a b -> p (a b)")

            V.tensor_copy(nslope_g[:, :], nslope[:, bass.ds(R * g, R)])
            V.tensor_copy(gates_g[:, :, :], gates[:, bass.ds(R * g, R), :])
            V.tensor_copy(conv_g[:, :, :], params[:, 0:24].rearrange("p (j b) -> p j b", j=3)[:, :, bass.ds(R * g, R)])
            V.tensor_copy(norm_g[:, :, :], params[:, 24:40].rearrange("p (a b) -> p a b", a=2)[:, :, bass.ds(R * g, R)])
            V.tensor_copy(kc_g[:, :], squeeze1(kc_all[:, bass.ds(g, 1), :]))
            V.tensor_copy(vc_g[0:NCMP, :], squeeze1(vc_all[0:NCMP, bass.ds(g, 1), :])).then_inc(S["grp_ready"], 1)

            def bias(r):
                dve.wait_ge(S["qk_done"], R * g + r + 1)
                sl = nslope_g[:, r:r + 1]
                V.scalar_tensor_tensor(sc1[:, :, :], dist1[:, :].unsqueeze(1).to_broadcast([P, 2, 256]), sl,
                                       bview(2, 2, 256), ALU.mult, ALU.add)
                V.scalar_tensor_tensor(sc0[:, :, :], dist0[:, :].unsqueeze(1).to_broadcast([P, 2, 128]), sl,
                                       bview(3, 2, 128), ALU.mult, ALU.add)
                V.scalar_tensor_tensor(scc[:, :, 0:NCMP], distc[:, :, 0:NCMP], sl,
                                       bank[3][:, 256:288].rearrange("p (t n) -> p t n", t=2)[:, :, 0:NCMP],
                                       ALU.mult, ALU.add)
                dve.drain()
                V.tensor_reduce(mx[:, 0:2], sc1[:, :, :], AX.X, ALU.max)
                V.tensor_reduce(mx[:, 2:4], sc0[:, :, :], AX.X, ALU.max)
                V.tensor_reduce(mx[:, 4:6], scc[:, :, 0:NCMP], AX.X, ALU.max)
                dve.drain()
                V.tensor_scalar(nmx[:, :], mx[:, :], -1.0, None, ALU.mult).then_inc(S["biased"], 1)

            def scale(r):
                dve.wait_ge(S["exps"], R * g + r + 1)
                V.reciprocal(rg[:, :], sums[:, :])
                V.tensor_tensor(scc[:, :, 0:NCMP], scc[:, :, 0:NCMP], validc[:, :, 0:NCMP], ALU.mult)
                dve.drain()
                V.tensor_tensor(rg[:, :], rg[:, :], gates_g[:, r, :], ALU.mult)
                dve.drain()
                V.tensor_tensor(sc1[:, :, :], sc1[:, :, :], rg[:, 0:2].unsqueeze(2).to_broadcast([P, 2, 256]), ALU.mult)
                V.tensor_tensor(sc0[:, :, :], sc0[:, :, :], rg[:, 2:4].unsqueeze(2).to_broadcast([P, 2, 128]), ALU.mult)
                V.tensor_tensor(scc[:, :, 0:NCMP], scc[:, :, 0:NCMP],
                                rg[:, 4:6].unsqueeze(2).to_broadcast([P, 2, NCMP]), ALU.mult
                                ).then_inc(S["probs_ready"], 1)

            def probs_out(r):
                dve.wait_ge(S["pt_done"], R * g + r + 1)
                V.tensor_copy(pT0[:, :, :], bview(5, 2, 128))
                V.tensor_copy(pTc[0:16, :, :], bank[5][0:16, 256:512].rearrange("p (t n) -> p t n", t=2)
                              ).then_inc(S["pt_dve"], 1)

            def conv_in(b, end):
                dve.wait_ge(S["slot_used"], s + end)
                dve.wait_ge(S["acc_act"], 6 * g + 5 + (b == 0))
                V.tensor_tensor(cu[:, :, 2:SEQ + 2], bview(b, 2, SEQ), c_sb[:, :, :], ALU.mult
                                ).then_inc(S["acc_dve"], 1)
                dve.drain()

            def conv_tap(pair, tap):
                for b in range(2):
                    w = conv_g[:, tap, 2 * pair + b:2 * pair + b + 1]
                    if tap == 0:
                        V.tensor_scalar(cv[:, b, :], cu[:, b, 0:SEQ], w, None, ALU.mult)
                    else:
                        V.scalar_tensor_tensor(cv[:, b, :], cu[:, b, tap:tap + SEQ], w, cv[:, b, :], ALU.mult, ALU.add)
                dve.drain()

            def conv_out(pair, b, end):
                dve.wait_ge(S["slot_used"], s + end)
                V.tensor_tensor(y_sb[:, 4 + 2 * pair:6 + 2 * pair, :], bview(b, 2, SEQ), cv[:, :, :], ALU.mult)
                dve.drain().then_inc(S["acc_dve"], 1)
                dve.drain().then_inc(S["y_conv"], 1)

            lo_w(s, 4, 32)
            bias(0)
            lo_w(s, 36, 2)
            scale(0)
            lo_w(s, 38, 6)
            probs_out(0)
            bias(1)
            lo_w(s, 44, 2)
            scale(1)
            lo_w(s, 46, 6)
            probs_out(1)
            bias(2)
            lo_w(s, 52, 1)
            conv_in(1, 48)
            lo_w(s, 53, 1)
            scale(2)
            lo_w(s, 54, 2)
            conv_tap(0, 0)
            lo_w(s, 56, 4)
            probs_out(2)
            bias(3)
            lo_w(s, 60, 1)
            conv_tap(0, 1)
            lo_w(s, 61, 1)
            scale(3)
            lo_w(s, 62, 1)
            conv_tap(0, 2)
            lo_w(s, 63, 1)
            conv_out(0, 0, 56)
            lo_w(s, 64, 4)
            probs_out(3)
            lo_w(s, 68, 8)
            conv_in(0, 72)
            lo_w(s, 76, 2)
            conv_tap(1, 0)
            conv_tap(1, 1)
            lo_w(s, 78, 2)
            conv_tap(1, 2)
            lo_w(s, 80, 4)
            conv_out(1, 1, 80)
            for n in range(4):
                dve.wait_ge(S["rms_ok"], 4 * g + n + 1)
                V.reciprocal(sq[:, 2 * n:2 * n + 2, :], sq[:, 2 * n:2 * n + 2, :])
                dve.drain()
                for b in range(2 * n, 2 * n + 2):
                    V.scalar_tensor_tensor(y_sb[:, b, :], y_sb[:, b, :], norm_g[:, b // 4, b % 4:b % 4 + 1],
                                           sq[:, b, :], ALU.mult, ALU.mult)
                if n % 2:
                    dve.drain().then_inc(S["mixf_ready"], 1)
            for n in range(2):
                dve.wait_ge(S["mix_hi_ok"], 2 * g + n + 1)
                V.tensor_tensor(mix_lo[:, bass.ds(R * g + 8 * n, R), :], y_sb[:, 4 * n:4 * n + 4, :],
                                mix_hi[:, bass.ds(R * g + 8 * n, R), :].bitcast(F32), ALU.subtract)
            dve.drain().then_inc(S["mix_ready"], 1)

        with dve.Fori(0, 4) as j:
            s = S_OUT + 16 * j
            for t in range(2):
                lo_w(s, 8 * t + 4, 8)
                dve.wait_ge(S["slot_used"], s + 8 * t + 8)
                cols = xh[:, :, bass.ds(512 * j + 256 * t, 256)]
                V.scalar_tensor_tensor(cols, cols, ALPHA, bview(t, 2, 256), ALU.mult, ALU.add
                                       ).then_inc(S["acc_dve"], 1)

        def layer_norm(buf, st, mv, rs_, done_var, done_std, ready, g_row, b_row, row_sem, n_rows):
            dve.drain()
            for t in range(2):
                for q in range(4):
                    V.bn_stats(st[:, t, q, :], buf[:, t, 512 * q:512 * q + 512])
            dve.drain()
            for t in range(2):
                V.bn_aggr(mv[:, t, :], st[:, t, :, :])
            dve.drain().then_inc(done_var, 1)
            dve.wait_ge(done_std, 1)
            V.reciprocal(rs_[:, :], rs_[:, :])
            dve.wait_ge(row_sem, n_rows)
            dve.drain()
            for t in range(2):
                V.tensor_scalar(buf[:, t, :], buf[:, t, :], mv[:, t, 0:1], rs_[:, t:t + 1], ALU.subtract, ALU.mult)
            dve.drain()
            for t in range(2):
                V.tensor_tensor(buf[:, t, :], buf[:, t, :], g_row[:, :], ALU.mult)
            dve.drain()
            for t in range(2):
                V.tensor_tensor(buf[:, t, :], buf[:, t, :], b_row[:, :], ALU.add).then_inc(ready, 1)

        layer_norm(xh, lnst, lnmv, lnrs, S["var_ok"], S["std_ok"], S["ln1_done"], ln_g, ln_b, S["s_lnrow"], 32)
        transpose_lo(8)
        with dve.Fori(0, 3) as j:
            lo_w(S_Q + 16 * j, 4, 16)
        lo_w(S_Q + 48, 4, 12)

        def lo_u(i, c, n):
            for q in range(c, c + n):
                dve.wait_ge(S["hi_done"], S_U + 16 * i + q + 1)
                V.tensor_tensor(w_lo[:, q % 4, :], bank[4 + q % 4][:, :], w_hi[:, q % 4, :].bitcast(F32),
                                ALU.subtract).then_inc(S["lo_done"], 1)

        def top16(val, idx, src, other):
            V.max(val[:, 0:8], src)
            dve.drain()
            V.max_index(idx[:, 0:8], val[:, 0:8], src)
            V.match_replace(other, val[:, 0:8], src, -3.0e38)
            dve.drain()
            V.max(val[:, 8:16], other)
            dve.drain()
            V.max_index(idx[:, 8:16], val[:, 8:16], other)

        dve.wait_ge(S["score_ok"], 8)
        V.tensor_copy(iota16[:, :], iota[:, 0:16])
        with dve.Fori(0, 16) as i:
            lo_u(i, 0, 2)
            V.tensor_copy(rs[:, :, :], scores[:, bass.ds(i, 1), :, :].rearrange("p a c n -> p (a c) n"))
            dve.drain()
            lo_u(i, 2, 1)
            top16(t_val[:, 0, :], t_idx[:, 0, :], rs[:, 0, :], rs2[:, 0, :])
            lo_u(i, 3, 2)
            top16(t_val[:, 1, :], t_idx[:, 1, :], rs[:, 1, :], rs2[:, 1, :])
            lo_u(i, 5, 2)
            dve.drain()
            V.tensor_copy(t_idf[:, :, :], t_idx[:, :, :])
            V.tensor_tensor(cand[:, :, :], t_val[:, 0, :].unsqueeze(2).to_broadcast([P, 16, 16]),
                            t_val[:, 1, :].unsqueeze(1).to_broadcast([P, 16, 16]), ALU.add)
            dve.drain()
            lo_u(i, 7, 2)
            flat, flat2 = (a[:, :, :].rearrange("p a b -> p (a b)") for a in (cand, cand2))
            V.max(b_val[:, 0:8], flat)
            dve.drain()
            V.max_index(b_idx[:, 0:8], b_val[:, 0:8], flat)
            V.match_replace(flat2, b_val[:, 0:8], flat, -3.0e38)
            dve.drain()
            lo_u(i, 9, 2)
            V.max(b_val[:, 8:16], flat2)
            dve.drain()
            V.max_index(b_idx[:, 8:16], b_val[:, 8:16], flat2)
            dve.drain()
            V.tensor_single_scalar(b_ij[:, 0, :], b_idx[:, :], 4, ALU.logical_shift_right)
            V.tensor_single_scalar(b_ij[:, 1, :], b_idx[:, :], 15, ALU.bitwise_and)
            dve.drain()
            V.tensor_copy(b_ijf[:, :, :], b_ij[:, :, :])
            dve.drain()
            lo_u(i, 11, 2)
            for a in range(2):
                V.tensor_tensor(eq[:, a, :, :], b_ijf[:, a, :].unsqueeze(2).to_broadcast([P, TOPK, 16]),
                                iota16[:, :].unsqueeze(1).to_broadcast([P, TOPK, 16]), ALU.is_equal)
            dve.drain()
            lo_u(i, 13, 1)
            for a in range(2):
                V.tensor_tensor(eq[:, a, :, :], eq[:, a, :, :],
                                t_idf[:, a, :].unsqueeze(1).to_broadcast([P, TOPK, 16]), ALU.mult)
            dve.drain()
            lo_u(i, 14, 1)
            V.tensor_reduce(b_id[:, :, :], eq[:, :, :, :], AX.X, ALU.add)
            dve.drain()
            for a in range(2):
                V.tensor_copy(picks[:, a, bass.ds(i, 1), :].rearrange("p a k -> p (a k)"), b_id[:, a, :])
            V.tensor_copy(picks[:, 2, bass.ds(i, 1), :].rearrange("p a k -> p (a k)"), b_val[:, :])
            lo_u(i, 15, 1)
        dve.drain()
        lo_u(16, 0, 1)
        V.tensor_copy(psum_k[:, :], picks[:, 2, :, 0])
        dve.drain()
        V.tensor_tensor(picks[:, 2, :, :], picks[:, 2, :, :], psum_k[:, :].unsqueeze(2).to_broadcast([P, 16, TOPK]),
                        ALU.subtract).then_inc(S["picks_raw"], 1)
        dve.wait_ge(S["picks_exp"], 1)
        V.tensor_reduce(psum_k[:, :], picks[:, 2, :, :], AX.X, ALU.add)
        dve.drain()
        V.reciprocal(psum_k[:, :], psum_k[:, :])
        dve.drain()
        V.tensor_tensor(picks[:, 2, :, :], picks[:, 2, :, :], psum_k[:, :].unsqueeze(2).to_broadcast([P, 16, TOPK]),
                        ALU.mult)
        dve.drain()
        for a in range(3):
            V.tensor_copy(picks_t[:, a, :, :, :], picks[:, a, :, :].rearrange("p (h t) k -> p t h k", t=2))
        dve.drain().then_inc(S["picks_ok"], 1)
        dve.wait_ge(S["tok_mm"], 1)
        V.tensor_copy(tokT[:, 0:2, :], bview(2, 2, SEQ))
        V.tensor_copy(tokT[:, 2, :], bank[3][:, 0:SEQ]).then_inc(S["tok_ok"], 1)
        dve.drain()

        def hots(nb, c0, n, first_key):
            for c in range(c0, c0 + n):
                if c % 8 == 0:
                    V.tensor_copy(tok8[:, :, :], tokT[:, :, bass.ds(8 * nb + c, 8)])
                    dve.drain()
                if not (isinstance(nb, int) and nb == 0 and c < 4):
                    dve.wait_ge(S["hot_used"], 8 * nb_all(nb, first_key) + c - 3)
                q = c % 8
                V.tensor_scalar(oneB[:, c % 4, :], iota[:, :], tok8[:, 1, q:q + 1], None, ALU.is_equal)
                V.tensor_scalar(oneA[:, c % 4, :], iota[:, first_key:first_key + HALF], tok8[:, 0, q:q + 1],
                                tok8[:, 2, q:q + 1], ALU.is_equal, ALU.mult)
                dve.drain().then_inc(S["hot_ready"], 1)

        def nb_all(nb, first_key):
            return nb + (32 if first_key else 0)

        def gate_mul(nb, b, first_key):
            n = 8 * (nb_all(nb, first_key) + b)
            dve.wait_ge(S["hot_used"], n + 8)
            view = coef[:, first_key:first_key + HALF, bass.ds(8 * (nb + b), 8)].rearrange("p k t -> p t k")
            V.tensor_tensor(view, view, bview(2 + b, 8, HALF), ALU.mult).then_inc(S["g_mul"], 1)

        dve.wait_ge(S["gelu_done"], HALF)

        def u_gated(i, done):
            nb = 2 * i - 32
            for c in range(16):
                if c >= done:
                    lo_u(i, c, 1)
                hots(nb, c, 1, 0)
                if c in (11,):
                    gate_mul(nb, 0, 0)
            gate_mul(nb, 1, 0)

        u_gated(16, 1)
        with dve.Fori(17, 32) as i:
            u_gated(i, 0)

        def v_body(cc, i, gated):
            for tt in range(4):
                n = ET * cc + 4 * i + tt
                dve.wait_ge(S["c_hi_ok"], n + 1)
                V.tensor_tensor(c_lo[:, tt % 2, :], coef[:, bass.ds(4 * i + tt, 1), :].rearrange("p a t -> p (a t)"),
                                c_hi[:, tt % 2, :].bitcast(F32), ALU.subtract).then_inc(S["c_lo_ok"], 1)
                for jc in range(2):
                    c = 2 * tt + jc
                    dve.wait_ge(S["hi_done"], S_V + 2 * ET * cc + 8 * i + c + 1)
                    V.tensor_tensor(w_lo[:, c % 4, :], v_ring[:, tt // 2, tt % 2, 512 * jc:512 * jc + 512],
                                    w_hi[:, c % 4, :].bitcast(F32), ALU.subtract).then_inc(S["lo_done"], 1)
                    if gated:
                        hots(2 * i, 2 * c, 2, HALF)
                        if c == 5:
                            gate_mul(2 * i, 0, HALF)
            if gated:
                gate_mul(2 * i, 1, HALF)

        dve.drain()
        v_body(0, 0, True)
        with dve.Fori(1, 16) as i:
            v_body(0, i, True)
        with dve.Fori(16, 32) as i:
            v_body(0, i, False)

        def add_pass(cc):
            dve.wait_ge(S["slot_used"], S_V + 2 * ET * (cc + 1))
            for t in range(2):
                for jc in range(2):
                    cols = res[:, t, 1024 * cc + 512 * jc:1024 * cc + 512 * jc + 512]
                    V.scalar_tensor_tensor(cols, cols, ALPHA, bank[4 - 4 * cc + 2 * t + jc][:, :], ALU.mult, ALU.add)

        dve.wait_ge(S["s_res"], 16)
        v_body(1, 0, False)
        add_pass(0)
        with dve.Fori(1, 32) as i:
            v_body(1, i, False)
        V.memset(eps2[:, :], LN_EPS)
        add_pass(1)
        layer_norm(res, l2st, l2mv, l2rs, S["var2_ok"], S["std2_ok"], S["final_ok"], ln2g_sb, ln2b_sb,
                   S["s_ln2row"], 32)

    block_cm.__exit__(None, None, None)


_INS = ['x', 'w_in', 'cmp_k_pos', 'cmp_k_w1', 'cmp_k_b1', 'cmp_k_w2', 'cmp_v_pos', 'cmp_v_w1', 'cmp_v_b1',
        'cmp_v_w2', 'conv_w', 'head_norm_g', 'w_out', 'ln1_g', 'ln1_b', 'w_query', 'sub_keys', 'expert_u',
        'expert_v', 'ln2_g', 'ln2_b']


def kernel(**inputs):
    import numpy as _np
    import concourse.bacc as _bacc
    from concourse import mybir as _mybir
    from concourse.bass_utils import run_bass_kernel_spmd as _run

    nc = _bacc.Bacc("TRN2", target_bir_lowering=False, num_devices=1)
    arrays, args = {}, []
    for name in _INS:
        a = _np.ascontiguousarray(inputs[name])
        arrays[f"in_{name}_dram"] = a
        args.append(nc.dram_tensor(f"in_{name}_dram", a.shape, _mybir.dt.from_np(a.dtype), kind="ExternalInput").ap())
    out = nc.dram_tensor("out_0_dram", (1, SEQ, D), _mybir.dt.float32, kind="ExternalOutput").ap()
    build(nc, *args, out)
    r = _run(nc, [arrays], core_ids=[0])
    return r.results[0]["out_0_dram"]
```

```python
import concourse.bass as bass
from concourse import mybir

F32 = mybir.dt.float32
F32R = mybir.dt.float32r
U32 = mybir.dt.uint32
ALU = mybir.AluOpType
ACT = mybir.ActivationFunctionType
AX = mybir.AxisListType

P = 128
D = 2048
SEQ = 256
KC = D // P
HD = 128
NH, NG = 8, 2
R = NH // NG
ATT_W = NH * HD
CONV_W = 1024
KV0 = ATT_W
GATE0 = KV0 + 6 * 256
U0 = GATE0 + 3 * NH
B0 = U0 + CONV_W
C0 = B0 + CONV_W
NCMP = (SEQ - 32) // 16 + 1
CHID = 512
NKEY = 128
TOPK = 16
PH = 8
ET = 128
HALF = ET // 2
ALPHA = 2.0 ** 0.25
SCALE = HD ** -0.5
LN_EPS = 1e-5
RMS_EPS = 1e-6
MASKED = 1e30
SLOPES = [2.0 ** (-8.0 * (h + 1) / NH) for h in range(NH)]

S_KV = 0
S_GRP = S_KV + 16
GRP_SLOTS = 80
S_OUT = S_GRP + NG * GRP_SLOTS
S_Q = S_OUT + 64
S_U = S_Q + 64
S_V = S_U + 4 * ET


def build(nc, x, w_in, cmp_k_pos, cmp_k_w1, cmp_k_b1, cmp_k_w2, cmp_v_pos, cmp_v_w1, cmp_v_b1, cmp_v_w2,
          conv_w, head_norm_g, w_out, ln1_g, ln1_b, w_query, sub_keys, expert_u, expert_v, ln2_g, ln2_b, out):
    h_spill = nc.dram_tensor("h_spill", (SEQ, D), F32).ap()

    x_v = x[0].rearrange("(t p) d -> p t d", p=P)
    out_v = out[0].rearrange("(t p) d -> p t d", p=P)
    h_v = h_spill.rearrange("(t p) d -> p t d", p=P)
    win_v = w_in[0].rearrange("(k p) c -> p k c", p=P)
    kv_v = w_in[0][:, KV0 + 512:GATE0].rearrange("(k p) (b v g c) -> v g b p k c", p=P, b=2, v=2, g=NG)
    wout_v = w_out[0].rearrange("(k p) c -> p k c", p=P)
    wq_v = w_query[0].rearrange("(k p) c -> p k c", p=P)
    w1_v = [w[0].rearrange("(j p) c -> p j c", p=P) for w in (cmp_k_w1, cmp_v_w1)]
    eu_v = expert_u[0].rearrange("(t p) d -> t p d", p=P)
    ev_v = expert_v[0].rearrange("(q e p) (c d) -> q c p e d", e=2, p=P, c=2)

    base = (nc.sbuf_base + 63) // 64 * 64
    top = [base]

    def at(name, shape, dt, offset=None):
        n = 4
        for s in shape[1:]:
            n *= s
        if offset is None:
            offset, top[0] = top[0], top[0] + (n + 31) // 32 * 32
        assert offset + n <= nc.sbuf_usable_end, name
        return nc.alloc_sbuf_tensor_at(name, shape, dt, offset=offset)

    K = 1024
    o_act = top[0]
    act_hi = at("act_hi", [P, KC, SEQ], F32R)
    act_lo = at("act_lo", [P, KC, SEQ], F32R)
    w_hi = at("w_hi", [P, 4, 512], F32R)
    w_lo = at("w_lo", [P, 4, 512], F32R)
    o_ring = top[0]
    u_ring = at("u_ring", [P, 2, D], F32)
    v_ring = at("v_ring", [P, 2, 2, 1024], F32, o_ring)
    w_ring = at("w_ring", [P, 4, 8, 256], F32, o_ring)
    coef = at("coef", [P, ET, SEQ], F32)
    oc = o_ring + 16 * K
    end_coef = oc + 128 * K
    xh = at("xh", [P, 2, D], F32, oc + 16 * K)
    mix_hi = at("mix_hi", [P, KC, SEQ], F32R, oc + 32 * K)
    mix_lo = at("mix_lo", [P, KC, SEQ], F32R, oc + 48 * K)
    pos = [oc + 64 * K]

    def tmp(name, shape, dt=F32):
        n = 4
        for s in shape[1:]:
            n *= s
        t = at(name, shape, dt, pos[0])
        pos[0] += (n + 31) // 32 * 32
        assert pos[0] <= oc + 112 * K, name
        return t

    kT = tmp("kT", [P, 2, SEQ])
    v_sb = tmp("v_sb", [P, 2, 2, HD])
    qT = tmp("qT", [P, R, SEQ])
    sc1 = tmp("sc1", [P, 2, 256])
    sc0 = tmp("sc0", [P, 2, 128])
    scc = tmp("scc", [P, 2, 16])
    pT1 = tmp("pT1", [P, 2, 2, 128])
    pT0 = tmp("pT0", [P, 2, 128])
    pTc = tmp("pTc", [16, 2, 128])
    mx = tmp("mx", [P, 6])
    nmx = tmp("nmx", [P, 6])
    sums = tmp("sums", [P, 6])
    rg = tmp("rg", [P, 6])
    cu = tmp("cu", [P, 2, SEQ + 2])
    dist1 = tmp("dist1", [P, 256])
    dist0 = tmp("dist0", [P, 128])
    distc = tmp("distc", [P, 2, 16])
    validc = tmp("validc", [P, 2, 16])
    nslope = tmp("nslope", [P, NH])
    gates = tmp("gates", [P, NH, 6])
    params = tmp("params", [P, 104])
    prow = tmp("prow", [104, P])
    kc_all = tmp("kc_all", [P, 2, 16])
    vc_all = tmp("vc_all", [16, 2, HD])
    nslope_g = tmp("nslope_g", [P, R])
    gates_g = tmp("gates_g", [P, R, 6])
    conv_g = tmp("conv_g", [P, 3, 4])
    norm_g = tmp("norm_g", [P, 2, 4])
    kc_g = tmp("kc_g", [P, 16])
    vc_g = tmp("vc_g", [16, HD])
    ones = tmp("ones", [P, P])
    onerow = tmp("onerow", [1, 32])
    eps = tmp("eps", [P, 2])
    b1row = tmp("b1row", [1, 2, CHID])
    gsig = tmp("gsig", [P, 2, 3 * NH])
    lnst = tmp("lnst", [P, 2, 4, 6])
    lnmv = tmp("lnmv", [P, 2, 2])
    lnrs = tmp("lnrs", [P, 2])
    assert pos[0] <= oc + 96 * K, pos[0] - oc
    c_sb = tmp("c_sb", [P, 2, SEQ])
    cv = tmp("cv", [P, 2, SEQ])
    y_sb = tmp("y_sb", [P, 8, SEQ])
    sq = tmp("sq", [P, 8, SEQ])
    assert pos[0] <= oc + 116 * K
    w1_ring = at("w1_ring", [P, 4, 4, CHID], F32, oc + 96 * K)
    blk = at("blk", [P, 2, 32, 30], F32, oc + 32 * K)
    hid = at("hid", [32, 2, CHID], F32, oc + 40 * K)
    hidT = at("hidT", [P, 2, 4, 32], F32, oc + 44 * K)
    w2 = at("w2", [P, 2, 4, HD], F32, oc + 46 * K)
    gw = at("gw", [P, KC, 24], F32, oc + 52 * K)
    gw_hi = at("gw_hi", [P, KC, 24], F32R, oc + 54 * K)
    gw_lo = at("gw_lo", [P, KC, 24], F32R, oc + 56 * K)
    ln_g = at("ln_g", [P, D], F32, oc + 112 * K)
    ln_b = at("ln_b", [P, D], F32, oc + 120 * K)
    skeys = at("skeys", [P, 16, P], F32, oc + 32 * K)
    skT = at("skT", [P, 16, P], F32, oc + 40 * K)
    qp = at("qp", [P, 2, 2, SEQ], F32, oc + 48 * K)
    scores = at("scores", [P, 16, 2, NKEY], F32, oc + 112 * K)
    rpos = [oc + 104 * K]

    def rtmp(name, shape, dt=F32):
        n = 4
        for s in shape[1:]:
            n *= s
        t = at(name, shape, dt, rpos[0])
        rpos[0] += (n + 31) // 32 * 32
        assert rpos[0] <= oc + 112 * K, name
        return t

    rs = rtmp("rs", [P, 2, NKEY])
    rs2 = rtmp("rs2", [P, 2, NKEY])
    t_val = rtmp("t_val", [P, 2, TOPK])
    t_idx = rtmp("t_idx", [P, 2, TOPK], U32)
    t_idf = rtmp("t_idf", [P, 2, TOPK])
    cand = rtmp("cand", [P, 16, 16])
    cand2 = rtmp("cand2", [P, 16, 16])
    b_idx = rtmp("b_idx", [P, TOPK], U32)
    b_ij = rtmp("b_ij", [P, 2, TOPK], U32)
    b_ijf = rtmp("b_ijf", [P, 2, TOPK])
    b_val = rtmp("b_val", [P, TOPK])
    eq = rtmp("eq", [P, 2, TOPK, 16])
    b_id = rtmp("b_id", [P, 2, TOPK])
    iota16 = rtmp("iota16", [P, 16])
    picks = at("picks", [P, 3, 16, TOPK], F32, oc + 96 * K)
    picks_t = at("picks_t", [P, 3, 2, PH, TOPK], F32, oc + 99 * K)
    psum_k = at("psum_k", [P, 16], F32, oc + 102 * K)
    res = at("res", [P, 2, D], F32, o_act)
    c_hi = at("c_hi", [P, 2, SEQ], F32R, o_act + 16 * K)
    c_lo = at("c_lo", [P, 2, SEQ], F32R, o_act + 18 * K)
    l2st = at("l2st", [P, 2, 4, 6], F32, o_act + 20 * K)
    l2mv = at("l2mv", [P, 2, 2], F32, o_act + 21 * K)
    l2rs = at("l2rs", [P, 2], F32, o_act + 21 * K + 64)
    eps2 = at("eps2", [P, 1], F32, o_act + 21 * K + 128)
    ln2g_sb = at("ln2g_sb", [P, D], F32, oc)
    ln2b_sb = at("ln2b_sb", [P, D], F32, oc + 8 * K)
    ident = at("ident", [P, P], F32)
    iota = at("iota", [P, P], F32)
    tokT = at("tokT", [P, 3, SEQ], F32)
    oneB = at("oneB", [P, 2, 4, NKEY], F32)
    oneA = at("oneA", [P, 2, 4, HALF], F32)

    bank = [nc.alloc_psum_tensor(f"bank{i}", [P, 512], F32) for i in range(8)]

    names = """s_const s_x s_small s_cw2 s_skeys s_lnrow s_ln2row s_hspill s_res s_out
        tr_done tr_hi tr_lo params_T params_ok gw_hi_ok gw_ready gate_mm gate_sig gate_ok
        blk_ready w1_used hid_mm hid_ready hidT_mm hidT_ok cmp_mm cmp_ok
        hi_done lo_done slot_used acc_act acc_dve grp_ready
        qk_done biased exps probs_ready pt_done pt_act pt_dve o_done y_att
        squared y_conv norm_mm rms_ok mixf_ready mix_hi_ok mix_ready
        var_ok std_ok ln1_done sk_mm sk_ok score_mm score_ok
        u_tr gelu_done picks_raw picks_exp picks_ok tok_mm tok_ok
        equal_ready hot_ready hot_used g_mul c_hi_ok c_lo_ok pass_read var2_ok std2_ok final_ok""".split()
    S = {n: nc.alloc_semaphore(n) for n in names}
    s_w = [nc.alloc_semaphore(f"s_w{i}") for i in range(4)]
    s_w1 = [nc.alloc_semaphore(f"s_w1_{i}") for i in range(4)]
    s_u = [nc.alloc_semaphore(f"s_u{i}") for i in range(2)]
    s_v = [nc.alloc_semaphore(f"s_v{i}") for i in range(2)]

    def bview(i, *shape):
        n = 1
        for s in shape:
            n *= s
        names_ = "abc"[:len(shape)]
        if len(shape) == 1:
            return bank[i][:, 0:n]
        return bank[i][:, 0:n].rearrange("p (%s) -> p %s" % (" ".join(names_), " ".join(names_)),
                                         **dict(zip(names_, shape)))

    block_cm = nc.Block()
    block = block_cm.__enter__()

    @block.sync
    def _(sp):
        sp.dma_start(xh[:, :, :], x_v).then_inc(S["s_x"], 16)

        def load_w(c, src, after):
            if after is not None:
                sp.wait_ge(S["lo_done"], after)
            for n in range(2):
                sp.dma_start(w_ring[:, c % 4, 4 * n:4 * n + 4, :], src[:, 4 * n:4 * n + 4, :]
                             ).then_inc(s_w[c % 4], 16)

        for c in range(4):
            t, hh = divmod(c, 2)
            load_w(c, win_v[:, 8 * hh:8 * hh + 8, KV0 + 256 * t:KV0 + 256 * t + 256], None)
        with sp.Fori(0, NG) as g:
            for t in range(10):
                for hh in range(2):
                    c = 2 * t + hh
                    after = S_GRP + GRP_SLOTS * g + 4 * (c - 3)
                    if t < 2:
                        sp.wait_ge(S["lo_done"], after)
                        for b in range(2):
                            src = kv_v[t, bass.ds(g, 1), b].rearrange("g p k c -> p k (g c)")
                            sp.dma_start(w_ring[:, c % 4, :, 128 * b:128 * b + 128],
                                         src[:, 8 * hh:8 * hh + 8, :]).then_inc(s_w[c % 4], 16)
                        continue
                    col = (0, 256, C0, U0, B0, C0 + 256, U0 + 256, B0 + 256)[t - 2] + 512 * g
                    load_w(c, win_v[:, 8 * hh:8 * hh + 8, bass.ds(col, 256)], after)
        for s0, view in ((S_OUT, wout_v), (S_Q, wq_v)):
            with sp.Fori(0, 4) as j:
                for c in range(4):
                    t, hh = divmod(c, 2)
                    load_w(c, view[:, 8 * hh:8 * hh + 8, bass.ds(512 * j + 256 * t, 256)],
                           s0 + 16 * j + 4 * (c - 3))

        def load_u(t, r):
            sp.dma_start(u_ring[:, r, :], eu_v[bass.ds(t, 1)].rearrange("t p d -> p (t d)")).then_inc(s_u[r], 16)

        for r in range(2):
            sp.wait_ge(S["lo_done"], S_U - 8 + 4 * r)
            load_u(r, r)
        with sp.Fori(1, ET // 2) as j:
            for r in range(2):
                sp.wait_ge(S["u_tr"], 8 * j + 4 * r - 4)
                load_u(2 * j + r, r)
        sp.wait_ge(S["slot_used"], S_V)
        sp.dma_start(res[:, :, :], h_v).then_inc(S["s_res"], 16)
        def load_v(ps, i, r):
            sp.dma_start(v_ring[:, r, :, :],
                         ev_v[bass.ds(32 * (ps // 2) + 2 * i + r, 1), ps % 2].rearrange("q p e d -> p (q e) d")
                         ).then_inc(s_v[r], 16)

        for r in range(2):
            load_v(0, 0, r)
        for ps in range(4):
            if ps == 3:
                sp.wait_ge(S["slot_used"], S_V + 2 * 128)
                for row, src in ((ln2g_sb, ln2_g), (ln2b_sb, ln2_b)):
                    sp.dma_start(row[:, :], src.partition_broadcast(P).rearrange("p a d -> p (a d)")
                                 ).then_inc(S["s_ln2row"], 16)
            with sp.Fori(1 if ps == 0 else 0, 16) as i:
                for r in range(2):
                    sp.wait_ge(S["lo_done"], S_V + 128 * ps + 8 * i + 4 * r - 4)
                    load_v(ps, i, r)
        for t in range(2):
            sp.wait_ge(S["final_ok"], t + 1)
            sp.dma_start(out_v[:, t, :], res[:, t, :]).then_inc(S["s_out"], 16)
        sp.wait_ge(S["s_out"], 32)

    @block.gpsimd
    def _(pool):
        small = [
            (prow[0:24, :], conv_w[0].rearrange("j (b c) -> (j b) c", c=P)),
            (prow[24:40, :], head_norm_g[0].rearrange("(b c) -> b c", c=P)),
            (prow[40:72, :], cmp_k_pos[0]),
            (prow[72:104, :], cmp_v_pos[0]),
            (b1row[0:1, 0, :], cmp_k_b1),
            (b1row[0:1, 1, :], cmp_v_b1),
            (gw[:, :, :], win_v[:, :, GATE0:GATE0 + 24]),
        ]
        for dst, src in small:
            pool.dma_start(dst, src).then_inc(S["s_small"], 16)
        for kv in range(2):
            pool.dma_start(w2[:, kv, :, :], (cmp_k_w2, cmp_v_w2)[kv][0].rearrange("(m p) d -> p m d", p=P)
                           ).then_inc(S["s_cw2"], 16)
        for c in range(4):
            pool.dma_start(w1_ring[:, c, :, :], w1_v[0][:, 4 * c:4 * c + 4, :]).then_inc(s_w1[c], 16)
        nc.gpsimd.memset(ident[:, :], 0.0)
        nc.gpsimd.memset(ones[:, :], 1.0 / HD)
        nc.gpsimd.memset(onerow[:, :], 1.0)
        nc.gpsimd.memset(eps[:, 0:1], RMS_EPS)
        nc.gpsimd.memset(eps[:, 1:2], LN_EPS)
        nc.gpsimd.memset(cu[:, :, :], 0.0)
        nc.gpsimd.memset(scc[:, :, :], 0.0)
        nc.gpsimd.memset(validc[:, :, :], 1.0)
        nc.gpsimd.memset(kc_all[:, :, :], 0.0)
        for h in range(NH):
            nc.gpsimd.memset(nslope[:, h:h + 1], -SLOPES[h])
        kw = dict(allow_small_or_imprecise_dtypes=True)
        nc.gpsimd.iota(iota[:, :], [[1, P]], base=0, channel_multiplier=0, **kw)
        nc.gpsimd.iota(dist1[:, :], [[-1, 256]], base=128, channel_multiplier=1, **kw)
        nc.gpsimd.iota(dist0[:, :], [[-1, 128]], base=0, channel_multiplier=1, **kw)
        nc.gpsimd.iota(distc[:, :, :], [[128, 2], [-16, 16]], base=0, channel_multiplier=1, **kw)
        pool.drain()
        nc.gpsimd.tensor_scalar(distc[:, :, :], distc[:, :, :], -15.5, None, ALU.add)
        nc.gpsimd.affine_select(out=ident[:, :], in_=ident[:, :], compare_op=ALU.not_equal, fill=1.0,
                                base=0, pattern=[[-1, P]], channel_multiplier=1)
        nc.gpsimd.affine_select(out=dist1[:, :], in_=dist1[:, :], compare_op=ALU.is_ge, fill=MASKED,
                                base=128, pattern=[[-1, 256]], channel_multiplier=1)
        nc.gpsimd.affine_select(out=dist0[:, :], in_=dist0[:, :], compare_op=ALU.is_ge, fill=MASKED,
                                base=0, pattern=[[-1, 128]], channel_multiplier=1)
        pool.drain()
        nc.gpsimd.affine_select(out=distc[:, :, :], in_=distc[:, :, :], compare_op=ALU.is_ge, fill=MASKED,
                                base=-31, pattern=[[128, 2], [-16, 16]], channel_multiplier=1)
        nc.gpsimd.affine_select(out=validc[:, :, :], in_=validc[:, :, :], compare_op=ALU.is_ge, fill=0.0,
                                base=-31, pattern=[[128, 2], [-16, 16]], channel_multiplier=1)
        pool.drain()
        pool.nop().then_inc(S["s_const"], 1)
        for i in range(4, 16):
            pool.wait_ge(S["w1_used"], i - 3)
            pool.dma_start(w1_ring[:, i % 4, :, :], w1_v[i // 8][:, 4 * (i % 8):4 * (i % 8) + 4, :]
                           ).then_inc(s_w1[i % 4], 16)
        pool.wait_ge(S["w1_used"], 16)
        pool.dma_start(ln_g[:, :], ln1_g.partition_broadcast(P).rearrange("p a d -> p (a d)")).then_inc(S["s_lnrow"], 16)
        pool.dma_start(ln_b[:, :], ln1_b.partition_broadcast(P).rearrange("p a d -> p (a d)")).then_inc(S["s_lnrow"], 16)
        pool.wait_ge(S["slot_used"], S_Q)
        pool.dma_start(skeys[:, :, :], sub_keys[0].rearrange("h c n d -> n (h c) d")).then_inc(S["s_skeys"], 16)
        pool.wait_ge(S["ln1_done"], 2)
        pool.dma_start(h_v, xh[:, :, :]).then_inc(S["s_hspill"], 16)
        pool.wait_ge(S["s_hspill"], 16)

        def weigh(half, n, b):
            pool.wait_ge(S["equal_ready"], n + 1)
            gate = tokT[:, 2, bass.ds(4 * n - 256 * half, 4)].unsqueeze(2).to_broadcast([P, 4, HALF])
            nc.gpsimd.tensor_tensor(oneA[:, b, :, :], oneA[:, b, :, :], gate, ALU.mult).then_inc(S["hot_ready"], 1)

        for half in range(2):
            with pool.Fori(0, 32) as j:
                for b in range(2):
                    weigh(half, 64 * half + 2 * j + b, b)

    @block.tensor
    def _(pe):
        def tile(kind, acc, s, lo=0, hi=8):
            for c in range(lo, hi):
                pe.wait_ge(S["lo_done"], s + c + 1)
                r = c % 4
                for kk in range(2):
                    k = 2 * c + kk
                    for b in range(2):
                        o = bank[acc][:, 256 * b:256 * b + 256]
                        half = slice(128 * b, 128 * b + 128)
                        if kind == "T":
                            w = slice(256 * kk + 128 * b, 256 * kk + 128 * b + 128)
                            pairs = ((w_hi[:, r, w], act_hi[:, k, :]), (w_hi[:, r, w], act_lo[:, k, :]),
                                     (w_lo[:, r, w], act_hi[:, k, :]))
                        else:
                            a_hi, a_lo = (act_hi, act_lo) if kind == "V" else (mix_hi, mix_lo)
                            w = slice(256 * kk, 256 * kk + 256)
                            pairs = ((a_hi[:, k, half], w_hi[:, r, w]), (a_hi[:, k, half], w_lo[:, r, w]),
                                     (a_lo[:, k, half], w_hi[:, r, w]))
                        for n, (st, mv) in enumerate(pairs):
                            ins = nc.tensor.matmul(o, st, mv, start=(k == 0 and b == 0 and n == 0),
                                                   stop=(k == KC - 1 and n == 2), skip_group_check=True)
                ins.then_inc(S["slot_used"], 1)

        def transpose_act(n0):
            for u in range(8):
                n = n0 + u
                if n >= 4:
                    pe.wait_ge(S["tr_lo"], n - 3)
                for kk in range(2):
                    for t in range(2):
                        col = 128 * (2 * u + kk)
                        ins = nc.tensor.transpose(bank[4 + u % 4][:, 256 * kk + 128 * t:256 * kk + 128 * t + 128],
                                                  xh[:, t, col:col + 128], ident[:, :])
                ins.then_inc(S["tr_done"], 1)

        pe.wait_ge(S["s_const"], 1)
        pe.wait_ge(S["s_x"], 16)
        transpose_act(0)
        pe.wait_ge(S["s_small"], 16 * 7)
        nc.tensor.transpose(bank[2][:, 0:104], prow[0:104, :], ident[0:104, 0:104]).then_inc(S["params_T"], 1)
        pe.wait_ge(S["tr_lo"], 8)
        for t in range(2):
            tile("T", t, S_KV + 8 * t)
        pe.wait_ge(S["gw_ready"], 1)
        for t in range(2):
            tk = slice(128 * t, 128 * t + 128)
            for k in range(KC):
                o = bank[3][:, 32 * t:32 * t + 24]
                nc.tensor.matmul(o, act_hi[:, k, tk], gw_hi[:, k, :], start=(k == 0), stop=False)
                nc.tensor.matmul(o, act_hi[:, k, tk], gw_lo[:, k, :], start=False, stop=False)
                ins = nc.tensor.matmul(o, act_lo[:, k, tk], gw_hi[:, k, :], start=False, stop=(k == KC - 1))
        ins.then_inc(S["gate_mm"], 1)
        pe.wait_ge(S["params_ok"], 1)
        for kv in range(2):
            pe.wait_ge(S["blk_ready"], kv + 1)
            for c in range(8):
                i = 8 * kv + c
                pe.wait_ge(s_w1[i % 4], 16 * (i // 4 + 1))
                for jj in range(4):
                    ins = nc.tensor.matmul(bank[(2, 4)[kv]][0:30, :], blk[:, kv, 4 * c + jj, :],
                                           w1_ring[:, i % 4, jj, :], start=(c == 0 and jj == 0), stop=False)
                ins.then_inc(S["w1_used"], 1)
            nc.tensor.matmul(bank[(2, 4)[kv]][0:30, :], onerow[0:1, 0:30], b1row[0:1, kv, :],
                             start=False, stop=True).then_inc(S["hid_mm"], 1)
        pe.wait_ge(S["hid_ready"], 2)
        for kv in range(2):
            for m in range(4):
                o = bank[5][:, 128 * kv + 32 * m:128 * kv + 32 * m + 30]
                ins = nc.tensor.transpose(o, hid[0:30, kv, 128 * m:128 * m + 128], ident[0:30, 0:30])
        ins.then_inc(S["hidT_mm"], 1)
        pe.wait_ge(S["hidT_ok"], 1)
        pe.wait_ge(S["s_cw2"], 32)
        for m in range(4):
            nc.tensor.matmul(bank[6][:, 0:30], w2[:, 0, m, :], hidT[:, 0, m, 0:30], start=(m == 0), stop=(m == 3))
        for g in range(NG):
            for m in range(4):
                ins = nc.tensor.matmul(bank[7][0:NCMP, 128 * g:128 * g + 128], hidT[:, 1, m, 15 * g:15 * g + 15],
                                       w2[:, 1, m, :], start=(m == 0), stop=(m == 3))
        ins.then_inc(S["cmp_mm"], 1)
        pe.wait_ge(S["cmp_ok"], 1)
        pe.wait_ge(S["gate_sig"], 1)

        with pe.Fori(0, NG) as g:
            s = S_GRP + GRP_SLOTS * g

            def score(r):
                for b in range(2):
                    nc.tensor.matmul(bank[2][:, 256 * b:256 * b + 256], qT[:, r, 128:256], kT[:, b, :],
                                     start=True, stop=True)
                for b in range(2):
                    nc.tensor.matmul(bank[3][:, 128 * b:128 * b + 128], qT[:, r, 0:128], kT[:, b, 0:128],
                                     start=True, stop=True)
                for t in range(2):
                    ins = nc.tensor.matmul(bank[3][:, 256 + 16 * t:272 + 16 * t], qT[:, r, 128 * t:128 * t + 128],
                                           kc_g[:, :], start=True, stop=True)
                ins.then_inc(S["qk_done"], 1)

            def transpose_probs(r):
                pe.wait_ge(S["probs_ready"], R * g + r + 1)
                for b in range(2):
                    for c in range(2):
                        nc.tensor.transpose(bank[4][:, 256 * b + 128 * c:256 * b + 128 * c + 128],
                                            sc1[:, b, 128 * c:128 * c + 128], ident[:, :])
                for b in range(2):
                    nc.tensor.transpose(bank[5][:, 128 * b:128 * b + 128], sc0[:, b, :], ident[:, :])
                for t in range(2):
                    ins = nc.tensor.transpose(bank[5][0:16, 256 + 128 * t:384 + 128 * t], scc[:, t, :], ident[:, :])
                ins.then_inc(S["pt_done"], 1)

            def attend(r):
                pe.wait_ge(S["pt_act"], R * g + r + 1)
                pe.wait_ge(S["pt_dve"], R * g + r + 1)
                if r:
                    pe.wait_ge(S["y_att"], R * g + r)
                parts0 = [(v_sb[:, 0, b, :], pT0[:, b, :]) for b in range(2)]
                parts0.append((vc_g[0:NCMP, :], pTc[0:NCMP, 0, :]))
                parts1 = [(v_sb[:, c, b, :], pT1[:, b, c, :]) for b in range(2) for c in range(2)]
                parts1.append((vc_g[0:NCMP, :], pTc[0:NCMP, 1, :]))
                for t, parts in ((0, parts0), (1, parts1)):
                    for n, (vv, pp) in enumerate(parts):
                        ins = nc.tensor.matmul(bank[6][:, 128 * t:128 * t + 128], vv, pp,
                                               start=(n == 0), stop=(n == len(parts) - 1))
                ins.then_inc(S["o_done"], 1)

            pe.wait_ge(S["acc_dve"], 4 * g + 1)
            tile("T", 0, s)
            pe.wait_ge(S["acc_dve"], 4 * g + 2)
            tile("V", 1, s + 8)
            pe.wait_ge(S["acc_act"], 6 * g + 1)
            tile("T", 0, s + 16)
            pe.wait_ge(S["acc_act"], 6 * g + 2)
            tile("T", 1, s + 24)
            pe.wait_ge(S["acc_act"], 6 * g + 3)
            pe.wait_ge(S["grp_ready"], g + 1)
            score(0)
            tile("T", 0, s + 32)
            transpose_probs(0)
            score(1)
            pe.wait_ge(S["acc_act"], 6 * g + 4)
            tile("T", 1, s + 40)
            attend(0)
            transpose_probs(1)
            score(2)
            pe.wait_ge(S["acc_act"], 6 * g + 5)
            tile("T", 0, s + 48)
            attend(1)
            transpose_probs(2)
            score(3)
            pe.wait_ge(S["acc_dve"], 4 * g + 3)
            tile("T", 1, s + 56)
            attend(2)
            transpose_probs(3)
            pe.wait_ge(S["acc_dve"], 4 * g + 4)
            tile("T", 0, s + 64)
            attend(3)
            pe.wait_ge(S["acc_act"], 6 * g + 6)
            tile("T", 1, s + 72)
            for n in range(4):
                pe.wait_ge(S["squared"], 4 * g + n + 1)
                nc.tensor.matmul(bank[2 + n][:, :], ones[:, :],
                                 sq[:, 2 * n:2 * n + 2, :].rearrange("p a t -> p (a t)"),
                                 start=True, stop=True).then_inc(S["norm_mm"], 1)

        pe.wait_ge(S["mix_ready"], NG)
        with pe.Fori(0, 4) as j:
            for t in range(2):
                pe.wait_ge(S["acc_dve"], 1 + 4 * NG + 2 * j + t)
                tile("M", t, S_OUT + 16 * j + 8 * t)

        pe.wait_ge(S["s_skeys"], 16)
        for n in range(4):
            if n >= 2:
                pe.wait_ge(S["sk_ok"], n - 1)
            for i in range(4):
                ins = nc.tensor.transpose(bank[2 + n % 2][:, 128 * i:128 * i + 128], skeys[:, 4 * n + i, :], ident[:, :])
            ins.then_inc(S["sk_mm"], 1)
        pe.wait_ge(S["ln1_done"], 2)
        transpose_act(8)
        pe.wait_ge(S["tr_lo"], 16)
        pe.wait_ge(S["sk_ok"], 4)
        pe.wait_ge(S["acc_dve"], 2 + 4 * NG + 8)

        def scores_of(h, b):
            pe.wait_ge(S["acc_act"], 6 * NG + h + 1)
            for t in range(2):
                for c in range(2):
                    ins = nc.tensor.matmul(bank[2 + b][:, 256 * t + 128 * c:256 * t + 128 * c + 128],
                                           qp[:, b, c, 128 * t:128 * t + 128],
                                           skT[:, bass.ds(2 * h + c, 1), :].rearrange("p a n -> p (a n)"),
                                           start=True, stop=True)
            ins.then_inc(S["score_mm"], 1)

        with pe.Fori(0, 4) as j:
            s = S_Q + 16 * j
            pe.wait_ge(S["acc_act"], 6 * NG + 2 * j)
            tile("T", 0, s)
            tile("T", 1, s + 8, 0, 4)
            scores_of(2 * j, 0)
            tile("T", 1, s + 8, 4, 8)
            scores_of(2 * j + 1, 1)
        pe.wait_ge(S["score_ok"], 8)

        def transpose_u(count, k, slot):
            if k == 0:
                pe.wait_ge(s_u[slot], count)
            for i in range(4):
                col = 512 * k + 128 * i
                ins = nc.tensor.transpose(bank[4 + k][:, 128 * i:128 * i + 128],
                                          u_ring[:, slot, col:col + 128], ident[:, :])
            ins.then_inc(S["u_tr"], 1)

        def gate_tokens(n, b, q0, q1):
            if q0 == 0:
                if not (isinstance(n, int) and n < 2):
                    pe.wait_ge(S["g_mul"], n - 1)
                pe.wait_ge(S["hot_ready"], n + 1)
            for q in range(q0, q1):
                ins = nc.tensor.matmul(bank[2 + b][:, HALF * q:HALF * q + HALF], oneB[:, b, q, :], oneA[:, b, q, :],
                                       start=True, stop=True)
            if q1 == 4:
                ins.then_inc(S["hot_used"], 1)

        def u_body(i, gated, last):
            for c in range(16):
                tt, k = divmod(c, 4)
                if not (last and c >= 13):
                    at_, ak = divmod(c + 3, 4)
                    transpose_u(16 * (2 * i + at_ // 2 + 1), ak, at_ % 2)
                pe.wait_ge(S["lo_done"], S_U + 16 * i + c + 1)
                if k == 0 and not (isinstance(i, int) and 4 * i + tt < 2):
                    pe.wait_ge(S["gelu_done"], 4 * i + tt - 1)
                for n in range(4):
                    dk = 4 * k + n
                    o = bank[tt % 2][:, 0:SEQ]
                    wh, wl = w_hi[:, k, 128 * n:128 * n + 128], w_lo[:, k, 128 * n:128 * n + 128]
                    nc.tensor.matmul(o, wh, act_hi[:, dk, :], start=(dk == 0), stop=False)
                    nc.tensor.matmul(o, wh, act_lo[:, dk, :], start=False, stop=False)
                    ins = nc.tensor.matmul(o, wl, act_hi[:, dk, :], start=False, stop=(dk == KC - 1))
                ins.then_inc(S["slot_used"], 1)
                if gated and c % 4 < 2:
                    gate_tokens(4 * i - 64 + c // 4, (c // 4) % 2, 2 * (c % 4), 2 * (c % 4) + 2)

        for k in range(3):
            transpose_u(16, k, 0)
        u_body(0, False, False)
        with pe.Fori(1, 16) as i:
            u_body(i, False, False)
        pe.wait_ge(S["picks_ok"], 1)
        for n in range(6):
            a, t = divmod(n, 2)
            ins = nc.tensor.transpose(bank[2 + n // 4][:, 128 * (n % 4):128 * (n % 4) + 128],
                                      picks_t[:, a, t, :, :].rearrange("p h k -> p (h k)"), ident[:, :])
        ins.then_inc(S["tok_mm"], 1)
        pe.wait_ge(S["tok_ok"], 1)
        u_body(16, True, False)
        with pe.Fori(17, 31) as i:
            u_body(i, True, False)
        u_body(31, True, True)

        def v_body(ps, i, first, last):
            b0 = (4, 4, 0, 4)[ps]
            for c in range(8):
                tt, jc = divmod(c, 2)
                r = c % 4
                pe.wait_ge(S["lo_done"], S_V + 128 * ps + 8 * i + c + 1)
                if jc == 0:
                    pe.wait_ge(S["c_lo_ok"], 64 * ps + 4 * i + tt + 1)
                for t in range(2):
                    o = bank[b0 + 2 * t + jc][:, :]
                    tk = slice(128 * t, 128 * t + 128)
                    nc.tensor.matmul(o, c_hi[:, tt % 2, tk], w_hi[:, r, :], start=first and tt == 0, stop=False)
                    nc.tensor.matmul(o, c_hi[:, tt % 2, tk], w_lo[:, r, :], start=False, stop=False)
                    ins = nc.tensor.matmul(o, c_lo[:, tt % 2, tk], w_hi[:, r, :], start=False,
                                           stop=last and tt == 3)
                ins.then_inc(S["slot_used"], 1)
                if ps < 2 and c in (0, 1, 3, 4):
                    b = c // 3
                    q0 = 2 * (c % 3)
                    gate_tokens(64 + 32 * ps + 2 * i + b, b, q0, q0 + 2)

        for ps in range(4):
            if ps in (1, 3):
                pe.wait_ge(S["pass_read"], (ps + 1) // 2)
            if ps == 2:
                pe.wait_ge(S["g_mul"], 128)
            v_body(ps, 0, True, False)
            with pe.Fori(1, 15) as i:
                v_body(ps, i, False, False)
            v_body(ps, 15, False, True)

    @block.scalar
    def _(act):
        def hi_w(s, c, n):
            for q in range(c, c + n):
                if q % 4 == 0:
                    act.wait_ge(s_w[(q // 4) % 4], s_count(s, q))
                if not (isinstance(s, int) and s + q < 4):
                    act.wait_ge(S["slot_used"], s + q - 3)
                src = w_ring[:, (q // 4) % 4, 2 * (q % 4):2 * (q % 4) + 2, :].rearrange("p k c -> p (k c)")
                nc.scalar.activation(w_hi[:, q % 4, :], src, ACT.Copy).then_inc(S["hi_done"], 1)

        def s_count(s, q):
            return 2 * s + (q // 16 + 1) * 32

        def transpose_hi(n0):
            for u in range(8):
                act.wait_ge(S["tr_done"], n0 + u + 1)
                nc.scalar.activation(act_hi[:, 2 * u:2 * u + 2, :], bview(4 + u % 4, 2, SEQ), ACT.Copy
                                     ).then_inc(S["tr_hi"], 1)

        transpose_hi(0)
        hi_w(S_KV, 0, 8)
        act.wait_ge(S["s_small"], 16 * 7)
        nc.scalar.activation(gw_hi[:, :, :], gw[:, :, :], ACT.Copy).then_inc(S["gw_hi_ok"], 1)
        hi_w(S_KV, 8, 8)
        act.wait_ge(S["gate_mm"], 1)
        nc.scalar.activation(gsig[:, :, :], bank[3][:, 0:64].rearrange("p (t c) -> p t c", t=2)[:, :, 0:24],
                             ACT.Sigmoid).then_inc(S["gate_sig"], 1)
        for kv in range(2):
            act.wait_ge(S["hid_mm"], kv + 1)
            nc.scalar.activation(hid[0:30, kv, :], bank[(2, 4)[kv]][0:30, :], ACT.Gelu_apprx_tanh
                                 ).then_inc(S["hid_ready"], 1)
        hi_w(S_GRP, 0, 4)
        with act.Fori(0, NG) as g:
            s = S_GRP + GRP_SLOTS * g

            def expo(r, c):
                act.wait_ge(S["biased"], R * g + r + 1)
                for b in range(2):
                    nc.scalar.activation(sc1[:, b, :], sc1[:, b, :], ACT.Exp, bias=nmx[:, b:b + 1],
                                         accum_out=sums[:, b:b + 1])
                hi_w(s, c, 1)
                for b in range(2):
                    nc.scalar.activation(sc0[:, b, :], sc0[:, b, :], ACT.Exp, bias=nmx[:, 2 + b:3 + b],
                                         accum_out=sums[:, 2 + b:3 + b])
                hi_w(s, c + 1, 1)
                for t in range(2):
                    ins = nc.scalar.activation(scc[:, t, 0:NCMP], scc[:, t, 0:NCMP], ACT.Exp,
                                               bias=nmx[:, 4 + t:5 + t], accum_out=sums[:, 4 + t:5 + t])
                ins.then_inc(S["exps"], 1)
                hi_w(s, c + 2, 1)

            def probs_out(r):
                act.wait_ge(S["pt_done"], R * g + r + 1)
                nc.scalar.activation(pT1[:, :, :, :].rearrange("p b c t -> p (b c t)"), bank[4][:, :], ACT.Copy
                                     ).then_inc(S["pt_act"], 1)

            def att_out(r):
                act.wait_ge(S["o_done"], R * g + r + 1)
                nc.scalar.activation(y_sb[:, r, :], bank[6][:, 0:SEQ], ACT.Copy).then_inc(S["y_att"], 1)

            def tile_out(dst, src, end, scale=1.0):
                act.wait_ge(S["slot_used"], s + end)
                nc.scalar.activation(dst, src, ACT.Copy, scale=scale).then_inc(S["acc_act"], 1)

            hi_w(s, 4, 8)
            tile_out(kT[:, :, :], bview(0, 2, SEQ), 8)
            hi_w(s, 12, 8)
            tile_out(v_sb[:, :, :, :].rearrange("p t b c -> p (t b c)"), bank[1][:, :], 16)
            hi_w(s, 20, 8)
            tile_out(qT[:, 0:2, :], bview(0, 2, SEQ), 24, SCALE)
            hi_w(s, 28, 8)
            tile_out(qT[:, 2:4, :], bview(1, 2, SEQ), 32, SCALE)
            expo(0, 36)
            hi_w(s, 39, 5)
            tile_out(c_sb[:, :, :], bview(0, 2, SEQ), 40)
            probs_out(0)
            expo(1, 44)
            hi_w(s, 47, 5)
            att_out(0)
            probs_out(1)
            expo(2, 52)
            hi_w(s, 55, 5)
            att_out(1)
            probs_out(2)
            expo(3, 60)
            hi_w(s, 63, 5)
            tile_out(c_sb[:, :, :], bview(1, 2, SEQ), 64)
            att_out(2)
            probs_out(3)
            hi_w(s, 68, 8)
            att_out(3)
            act.drain()
            for n in range(2):
                nc.scalar.activation(sq[:, 2 * n:2 * n + 2, :], y_sb[:, 2 * n:2 * n + 2, :], ACT.Square
                                     ).then_inc(S["squared"], 1)
            hi_w(s, 76, 8)
            for n in range(2, 4):
                act.wait_ge(S["y_conv"], 2 * g + n - 1)
                nc.scalar.activation(sq[:, 2 * n:2 * n + 2, :], y_sb[:, 2 * n:2 * n + 2, :], ACT.Square
                                     ).then_inc(S["squared"], 1)
            for n in range(4):
                act.wait_ge(S["norm_mm"], 4 * g + n + 1)
                nc.scalar.activation(sq[:, 2 * n:2 * n + 2, :], bview(2 + n, 2, SEQ), ACT.Ln, bias=eps[:, 0:1])
            act.drain()
            for n in range(4):
                nc.scalar.activation(sq[:, 2 * n:2 * n + 2, :], sq[:, 2 * n:2 * n + 2, :], ACT.Exp, scale=-0.5
                                     ).then_inc(S["rms_ok"], 1)
            for n in range(2):
                act.wait_ge(S["mixf_ready"], 2 * g + n + 1)
                nc.scalar.activation(mix_hi[:, bass.ds(R * g + 8 * n, R), :], y_sb[:, 4 * n:4 * n + 4, :], ACT.Copy
                                     ).then_inc(S["mix_hi_ok"], 1)
        with act.Fori(0, 4) as j:
            hi_w(S_OUT + 16 * j, 4, 16)
        act.wait_ge(S["var_ok"], 1)
        nc.scalar.activation(lnrs[:, :], lnmv[:, :, 1], ACT.Sqrt, bias=eps[:, 1:2]).then_inc(S["std_ok"], 1)
        for n in range(4):
            act.wait_ge(S["sk_mm"], n + 1)
            nc.scalar.activation(skT[:, 4 * n:4 * n + 4, :].rearrange("p a n -> p (a n)"), bank[2 + n % 2][:, :],
                                 ACT.Copy).then_inc(S["sk_ok"], 1)
        transpose_hi(8)

        def head_out(h, b, slots):
            act.wait_ge(S["slot_used"], slots)
            nc.scalar.activation(qp[:, b, :, :], bview(b, 2, SEQ), ACT.Copy).then_inc(S["acc_act"], 1)

        def score_out(h, b):
            act.wait_ge(S["score_mm"], h + 1)
            nc.scalar.activation(scores[:, bass.ds(2 * h, 2), :, :], bview(2 + b, 2, 2, NKEY), ACT.Copy
                                 ).then_inc(S["score_ok"], 1)

        def q_body(j, last):
            s = S_Q + 16 * j
            hi_w(s, 4, 8)
            head_out(2 * j, 0, s + 8)
            hi_w(s, 12, 4)
            score_out(2 * j, 0)
            if not last:
                hi_w(s, 16, 4)
            head_out(2 * j + 1, 1, s + 16)
            score_out(2 * j + 1, 1)

        with act.Fori(0, 3) as j:
            q_body(j, False)
        q_body(3, True)

        def hi_u(i, c):
            act.wait_ge(S["u_tr"], 16 * i + c + 1)
            act.wait_ge(S["slot_used"], S_U + 16 * i + c - 3)
            nc.scalar.activation(w_hi[:, c % 4, :], bank[4 + c % 4][:, :], ACT.Copy).then_inc(S["hi_done"], 1)

        def u_body(i, last):
            for tt in range(4):
                for c in range(4 * tt + 3, 4 * tt + 7):
                    if not (last and c >= 16):
                        hi_u(i, c)
                act.wait_ge(S["slot_used"], S_U + 16 * i + 4 * tt + 4)
                nc.scalar.activation(coef[:, bass.ds(4 * i + tt, 1), :].rearrange("p a t -> p (a t)"),
                                     bank[tt % 2][:, 0:SEQ], ACT.Gelu_apprx_tanh).then_inc(S["gelu_done"], 1)

        act.wait_ge(S["s_hspill"], 16)
        for c in range(3):
            hi_u(0, c)
        with act.Fori(0, 16) as i:
            u_body(i, False)
        act.wait_ge(S["picks_raw"], 1)
        nc.scalar.activation(picks[:, 2, :, :], picks[:, 2, :, :], ACT.Exp).then_inc(S["picks_exp"], 1)
        with act.Fori(16, 31) as i:
            u_body(i, False)
        u_body(31, True)

        def hi_v(ps, i, c):
            if c % 4 == 0:
                act.wait_ge(s_v[c // 4], 16 * (16 * ps + i + 1))
            act.wait_ge(S["slot_used"], S_V + 128 * ps + 8 * i + c - 3)
            tt, jc = divmod(c, 2)
            nc.scalar.activation(w_hi[:, c % 4, :], v_ring[:, tt // 2, tt % 2, 512 * jc:512 * jc + 512],
                                 ACT.Copy).then_inc(S["hi_done"], 1)

        def hi_c(ps, i, tt):
            m = 64 * ps + 4 * i + tt
            if not (isinstance(m, int) and m < 2):
                act.wait_ge(S["slot_used"], S_V + 2 * m - 2)
            nc.scalar.activation(c_hi[:, tt % 2, :],
                                 coef[:, bass.ds(64 * (ps // 2) + 4 * i + tt, 1), :].rearrange("p a t -> p (a t)"),
                                 ACT.Copy).then_inc(S["c_hi_ok"], 1)

        def v_body(ps, i):
            for tt in range(4):
                for jc in range(2):
                    hi_v(ps, i, 2 * tt + jc)
                if tt == 0 and isinstance(i, int):
                    act.wait_ge(S["g_mul"], 64 * (ps // 2 + 1))
                hi_c(ps, i, tt)

        for ps in range(4):
            v_body(ps, 0)
            with act.Fori(1, 16) as i:
                v_body(ps, i)
        act.wait_ge(S["var2_ok"], 1)
        nc.scalar.activation(l2rs[:, :], l2mv[:, :, 1], ACT.Sqrt, bias=eps2[:, 0:1]).then_inc(S["std2_ok"], 1)

    @block.vector
    def _(dve):
        V = nc.vector

        def lo_w(s, c, n):
            for q in range(c, c + n):
                dve.wait_ge(S["hi_done"], s + q + 1)
                src = w_ring[:, (q // 4) % 4, 2 * (q % 4):2 * (q % 4) + 2, :].rearrange("p k c -> p (k c)")
                V.tensor_tensor(w_lo[:, q % 4, :], src, w_hi[:, q % 4, :].bitcast(F32), ALU.subtract
                                ).then_inc(S["lo_done"], 1)

        def transpose_lo(n0):
            for u in range(8):
                dve.wait_ge(S["tr_hi"], n0 + u + 1)
                V.tensor_tensor(act_lo[:, 2 * u:2 * u + 2, :], bview(4 + u % 4, 2, SEQ),
                                act_hi[:, 2 * u:2 * u + 2, :].bitcast(F32), ALU.subtract).then_inc(S["tr_lo"], 1)

        transpose_lo(0)
        lo_w(S_KV, 0, 8)
        dve.wait_ge(S["params_T"], 1)
        V.tensor_copy(params[:, :], bank[2][:, 0:104]).then_inc(S["params_ok"], 1)
        dve.wait_ge(S["gw_hi_ok"], 1)
        V.tensor_tensor(gw_lo[:, :, :], gw[:, :, :], gw_hi[:, :, :].bitcast(F32), ALU.subtract
                        ).then_inc(S["gw_ready"], 1)
        dve.drain()

        def blocks(kv):
            dve.wait_ge(S["slot_used"], S_KV + 8 * (kv + 1))
            for g in range(NG):
                for hh in range(2):
                    src = bank[kv][:, 256 * g + 16 * hh:256 * g + 16 * hh + 240].rearrange("p (n s) -> p s n", s=16)
                    add = params[:, 40 + 32 * kv + 16 * hh:56 + 32 * kv + 16 * hh].unsqueeze(2).to_broadcast([P, 16, NCMP])
                    ins = V.tensor_tensor(blk[:, kv, 16 * hh:16 * hh + 16, 15 * g:15 * g + 15], src, add, ALU.add)
            dve.drain().then_inc(S["blk_ready"], 1)
            dve.drain().then_inc(S["acc_dve"], 1)

        lo_w(S_KV, 8, 4)
        blocks(0)
        lo_w(S_KV, 12, 4)
        blocks(1)
        dve.wait_ge(S["gate_sig"], 1)
        for n, (t, b) in enumerate(((1, 1), (1, 2), (0, 1), (0, 2), (0, 0), (1, 0))):
            V.tensor_copy(gates[:, :, n], gsig[:, t, :].rearrange("p (h b) -> p h b", b=3)[:, :, b])
        dve.wait_ge(S["hidT_mm"], 1)
        V.tensor_copy(hidT[:, :, :, 0:30], bank[5][:, 0:256].rearrange("p (a m n) -> p a m n", a=2, m=4)[:, :, :, 0:30]
                      ).then_inc(S["hidT_ok"], 1)
        dve.wait_ge(S["cmp_mm"], 1)
        V.tensor_copy(kc_all[:, :, 0:NCMP], bank[6][:, 0:30].rearrange("p (g n) -> p g n", g=2))
        V.tensor_copy(vc_all[0:NCMP, :, :], bank[7][0:NCMP, 0:256].rearrange("p (g n) -> p g n", g=2)
                      ).then_inc(S["cmp_ok"], 1)
        lo_w(S_GRP, 0, 4)
        dve.drain()
        with dve.Fori(0, NG) as g:
            s = S_GRP + GRP_SLOTS * g

            def squeeze1(ap):
                return ap.rearrange("p a b -> p (a b)")

            V.tensor_copy(nslope_g[:, :], nslope[:, bass.ds(R * g, R)])
            V.tensor_copy(gates_g[:, :, :], gates[:, bass.ds(R * g, R), :])
            V.tensor_copy(conv_g[:, :, :], params[:, 0:24].rearrange("p (j b) -> p j b", j=3)[:, :, bass.ds(R * g, R)])
            V.tensor_copy(norm_g[:, :, :], params[:, 24:40].rearrange("p (a b) -> p a b", a=2)[:, :, bass.ds(R * g, R)])
            V.tensor_copy(kc_g[:, :], squeeze1(kc_all[:, bass.ds(g, 1), :]))
            V.tensor_copy(vc_g[0:NCMP, :], squeeze1(vc_all[0:NCMP, bass.ds(g, 1), :])).then_inc(S["grp_ready"], 1)

            def bias(r):
                dve.wait_ge(S["qk_done"], R * g + r + 1)
                sl = nslope_g[:, r:r + 1]
                V.scalar_tensor_tensor(sc1[:, :, :], dist1[:, :].unsqueeze(1).to_broadcast([P, 2, 256]), sl,
                                       bview(2, 2, 256), ALU.mult, ALU.add)
                V.scalar_tensor_tensor(sc0[:, :, :], dist0[:, :].unsqueeze(1).to_broadcast([P, 2, 128]), sl,
                                       bview(3, 2, 128), ALU.mult, ALU.add)
                V.scalar_tensor_tensor(scc[:, :, 0:NCMP], distc[:, :, 0:NCMP], sl,
                                       bank[3][:, 256:288].rearrange("p (t n) -> p t n", t=2)[:, :, 0:NCMP],
                                       ALU.mult, ALU.add)
                dve.drain()
                V.tensor_reduce(mx[:, 0:2], sc1[:, :, :], AX.X, ALU.max)
                V.tensor_reduce(mx[:, 2:4], sc0[:, :, :], AX.X, ALU.max)
                V.tensor_reduce(mx[:, 4:6], scc[:, :, 0:NCMP], AX.X, ALU.max)
                dve.drain()
                V.tensor_scalar(nmx[:, :], mx[:, :], -1.0, None, ALU.mult).then_inc(S["biased"], 1)

            def scale(r):
                dve.wait_ge(S["exps"], R * g + r + 1)
                V.reciprocal(rg[:, :], sums[:, :])
                V.tensor_tensor(scc[:, :, 0:NCMP], scc[:, :, 0:NCMP], validc[:, :, 0:NCMP], ALU.mult)
                dve.drain()
                V.tensor_tensor(rg[:, :], rg[:, :], gates_g[:, r, :], ALU.mult)
                dve.drain()
                V.tensor_tensor(sc1[:, :, :], sc1[:, :, :], rg[:, 0:2].unsqueeze(2).to_broadcast([P, 2, 256]), ALU.mult)
                V.tensor_tensor(sc0[:, :, :], sc0[:, :, :], rg[:, 2:4].unsqueeze(2).to_broadcast([P, 2, 128]), ALU.mult)
                V.tensor_tensor(scc[:, :, 0:NCMP], scc[:, :, 0:NCMP],
                                rg[:, 4:6].unsqueeze(2).to_broadcast([P, 2, NCMP]), ALU.mult
                                ).then_inc(S["probs_ready"], 1)

            def probs_out(r):
                dve.wait_ge(S["pt_done"], R * g + r + 1)
                V.tensor_copy(pT0[:, :, :], bview(5, 2, 128))
                V.tensor_copy(pTc[0:16, :, :], bank[5][0:16, 256:512].rearrange("p (t n) -> p t n", t=2)
                              ).then_inc(S["pt_dve"], 1)

            def conv_in(b, end):
                dve.wait_ge(S["slot_used"], s + end)
                dve.wait_ge(S["acc_act"], 6 * g + 5 + (b == 0))
                V.tensor_tensor(cu[:, :, 2:SEQ + 2], bview(b, 2, SEQ), c_sb[:, :, :], ALU.mult
                                ).then_inc(S["acc_dve"], 1)
                dve.drain()

            def conv_tap(pair, tap):
                for b in range(2):
                    w = conv_g[:, tap, 2 * pair + b:2 * pair + b + 1]
                    if tap == 0:
                        V.tensor_scalar(cv[:, b, :], cu[:, b, 0:SEQ], w, None, ALU.mult)
                    else:
                        V.scalar_tensor_tensor(cv[:, b, :], cu[:, b, tap:tap + SEQ], w, cv[:, b, :], ALU.mult, ALU.add)
                dve.drain()

            def conv_out(pair, b, end):
                dve.wait_ge(S["slot_used"], s + end)
                V.tensor_tensor(y_sb[:, 4 + 2 * pair:6 + 2 * pair, :], bview(b, 2, SEQ), cv[:, :, :], ALU.mult)
                dve.drain().then_inc(S["acc_dve"], 1)
                dve.drain().then_inc(S["y_conv"], 1)

            lo_w(s, 4, 32)
            bias(0)
            lo_w(s, 36, 3)
            scale(0)
            lo_w(s, 39, 5)
            probs_out(0)
            bias(1)
            lo_w(s, 44, 3)
            scale(1)
            lo_w(s, 47, 5)
            probs_out(1)
            bias(2)
            lo_w(s, 52, 2)
            conv_in(1, 48)
            lo_w(s, 54, 1)
            scale(2)
            lo_w(s, 55, 5)
            probs_out(2)
            bias(3)
            lo_w(s, 60, 1)
            conv_tap(0, 0)
            lo_w(s, 61, 1)
            conv_tap(0, 1)
            lo_w(s, 62, 1)
            scale(3)
            lo_w(s, 63, 1)
            conv_tap(0, 2)
            conv_out(0, 0, 56)
            lo_w(s, 64, 4)
            probs_out(3)
            lo_w(s, 68, 8)
            conv_in(0, 72)
            lo_w(s, 76, 1)
            conv_tap(1, 0)
            lo_w(s, 77, 1)
            conv_tap(1, 1)
            lo_w(s, 78, 1)
            conv_tap(1, 2)
            lo_w(s, 79, 5)
            conv_out(1, 1, 80)
            for n in range(4):
                dve.wait_ge(S["rms_ok"], 4 * g + n + 1)
                for b in range(2 * n, 2 * n + 2):
                    V.scalar_tensor_tensor(y_sb[:, b, :], y_sb[:, b, :], norm_g[:, b // 4, b % 4:b % 4 + 1],
                                           sq[:, b, :], ALU.mult, ALU.mult)
                if n % 2:
                    dve.drain().then_inc(S["mixf_ready"], 1)
            for n in range(2):
                dve.wait_ge(S["mix_hi_ok"], 2 * g + n + 1)
                V.tensor_tensor(mix_lo[:, bass.ds(R * g + 8 * n, R), :], y_sb[:, 4 * n:4 * n + 4, :],
                                mix_hi[:, bass.ds(R * g + 8 * n, R), :].bitcast(F32), ALU.subtract)
            dve.drain().then_inc(S["mix_ready"], 1)

        with dve.Fori(0, 4) as j:
            s = S_OUT + 16 * j
            for t in range(2):
                lo_w(s, 8 * t + 4, 8)
                dve.wait_ge(S["slot_used"], s + 8 * t + 8)
                cols = xh[:, :, bass.ds(512 * j + 256 * t, 256)]
                V.scalar_tensor_tensor(cols, cols, ALPHA, bview(t, 2, 256), ALU.mult, ALU.add
                                       ).then_inc(S["acc_dve"], 1)

        def layer_norm(buf, st, mv, rs_, done_var, done_std, ready, g_row, b_row, row_sem, n_rows):
            dve.drain()
            for t in range(2):
                for q in range(4):
                    V.bn_stats(st[:, t, q, :], buf[:, t, 512 * q:512 * q + 512])
            dve.drain()
            for t in range(2):
                V.bn_aggr(mv[:, t, :], st[:, t, :, :])
            dve.drain().then_inc(done_var, 1)
            dve.wait_ge(done_std, 1)
            V.reciprocal(rs_[:, :], rs_[:, :])
            dve.wait_ge(row_sem, n_rows)
            dve.drain()
            for t in range(2):
                V.tensor_scalar(buf[:, t, :], buf[:, t, :], mv[:, t, 0:1], rs_[:, t:t + 1], ALU.subtract, ALU.mult)
            dve.drain()
            for t in range(2):
                V.tensor_tensor(buf[:, t, :], buf[:, t, :], g_row[:, :], ALU.mult)
            dve.drain()
            for t in range(2):
                V.tensor_tensor(buf[:, t, :], buf[:, t, :], b_row[:, :], ALU.add).then_inc(ready, 1)

        layer_norm(xh, lnst, lnmv, lnrs, S["var_ok"], S["std_ok"], S["ln1_done"], ln_g, ln_b, S["s_lnrow"], 32)
        transpose_lo(8)
        with dve.Fori(0, 3) as j:
            lo_w(S_Q + 16 * j, 4, 16)
        lo_w(S_Q + 48, 4, 12)

        def lo_u(i, c, n):
            for q in range(c, c + n):
                dve.wait_ge(S["hi_done"], S_U + 16 * i + q + 1)
                V.tensor_tensor(w_lo[:, q % 4, :], bank[4 + q % 4][:, :], w_hi[:, q % 4, :].bitcast(F32),
                                ALU.subtract).then_inc(S["lo_done"], 1)

        def top16(val, idx, src, other):
            V.max(val[:, 0:8], src)
            dve.drain()
            V.max_index(idx[:, 0:8], val[:, 0:8], src)
            V.match_replace(other, val[:, 0:8], src, -3.0e38)
            dve.drain()
            V.max(val[:, 8:16], other)
            dve.drain()
            V.max_index(idx[:, 8:16], val[:, 8:16], other)

        dve.wait_ge(S["score_ok"], 8)
        V.tensor_copy(iota16[:, :], iota[:, 0:16])
        with dve.Fori(0, 16) as i:
            lo_u(i, 0, 2)
            V.tensor_copy(rs[:, :, :], scores[:, bass.ds(i, 1), :, :].rearrange("p a c n -> p (a c) n"))
            dve.drain()
            lo_u(i, 2, 1)
            top16(t_val[:, 0, :], t_idx[:, 0, :], rs[:, 0, :], rs2[:, 0, :])
            lo_u(i, 3, 2)
            top16(t_val[:, 1, :], t_idx[:, 1, :], rs[:, 1, :], rs2[:, 1, :])
            lo_u(i, 5, 2)
            dve.drain()
            V.tensor_copy(t_idf[:, :, :], t_idx[:, :, :])
            V.tensor_tensor(cand[:, :, :], t_val[:, 0, :].unsqueeze(2).to_broadcast([P, 16, 16]),
                            t_val[:, 1, :].unsqueeze(1).to_broadcast([P, 16, 16]), ALU.add)
            dve.drain()
            lo_u(i, 7, 2)
            flat, flat2 = (a[:, :, :].rearrange("p a b -> p (a b)") for a in (cand, cand2))
            V.max(b_val[:, 0:8], flat)
            dve.drain()
            V.max_index(b_idx[:, 0:8], b_val[:, 0:8], flat)
            V.match_replace(flat2, b_val[:, 0:8], flat, -3.0e38)
            dve.drain()
            lo_u(i, 9, 2)
            V.max(b_val[:, 8:16], flat2)
            dve.drain()
            V.max_index(b_idx[:, 8:16], b_val[:, 8:16], flat2)
            dve.drain()
            V.tensor_single_scalar(b_ij[:, 0, :], b_idx[:, :], 4, ALU.logical_shift_right)
            V.tensor_single_scalar(b_ij[:, 1, :], b_idx[:, :], 15, ALU.bitwise_and)
            dve.drain()
            V.tensor_copy(b_ijf[:, :, :], b_ij[:, :, :])
            dve.drain()
            lo_u(i, 11, 2)
            for a in range(2):
                V.tensor_tensor(eq[:, a, :, :], b_ijf[:, a, :].unsqueeze(2).to_broadcast([P, TOPK, 16]),
                                iota16[:, :].unsqueeze(1).to_broadcast([P, TOPK, 16]), ALU.is_equal)
            dve.drain()
            lo_u(i, 13, 1)
            for a in range(2):
                V.tensor_tensor(eq[:, a, :, :], eq[:, a, :, :],
                                t_idf[:, a, :].unsqueeze(1).to_broadcast([P, TOPK, 16]), ALU.mult)
            dve.drain()
            lo_u(i, 14, 1)
            V.tensor_reduce(b_id[:, :, :], eq[:, :, :, :], AX.X, ALU.add)
            dve.drain()
            for a in range(2):
                V.tensor_copy(picks[:, a, bass.ds(i, 1), :].rearrange("p a k -> p (a k)"), b_id[:, a, :])
            V.tensor_copy(picks[:, 2, bass.ds(i, 1), :].rearrange("p a k -> p (a k)"), b_val[:, :])
            lo_u(i, 15, 1)
        dve.drain()
        lo_u(16, 0, 1)
        V.tensor_copy(psum_k[:, :], picks[:, 2, :, 0])
        dve.drain()
        V.tensor_tensor(picks[:, 2, :, :], picks[:, 2, :, :], psum_k[:, :].unsqueeze(2).to_broadcast([P, 16, TOPK]),
                        ALU.subtract).then_inc(S["picks_raw"], 1)
        dve.wait_ge(S["picks_exp"], 1)
        V.tensor_reduce(psum_k[:, :], picks[:, 2, :, :], AX.X, ALU.add)
        dve.drain()
        V.reciprocal(psum_k[:, :], psum_k[:, :])
        dve.drain()
        V.tensor_tensor(picks[:, 2, :, :], picks[:, 2, :, :], psum_k[:, :].unsqueeze(2).to_broadcast([P, 16, TOPK]),
                        ALU.mult)
        dve.drain()
        for a in range(3):
            V.tensor_copy(picks_t[:, a, :, :, :], picks[:, a, :, :].rearrange("p (h t) k -> p t h k", t=2))
        dve.drain().then_inc(S["picks_ok"], 1)
        dve.wait_ge(S["tok_mm"], 1)
        V.tensor_copy(tokT[:, 0:2, :], bview(2, 2, SEQ))
        V.tensor_copy(tokT[:, 2, :], bank[3][:, 0:SEQ]).then_inc(S["tok_ok"], 1)
        dve.drain()

        def equal(n, b, half):
            if not (isinstance(n, int) and n < 2):
                dve.wait_ge(S["hot_used"], n - 1)
            tok = bass.ds(4 * n - 256 * half, 4)
            V.tensor_tensor(oneB[:, b, :, :], iota[:, :].unsqueeze(1).to_broadcast([P, 4, NKEY]),
                            tokT[:, 1, tok].unsqueeze(2).to_broadcast([P, 4, NKEY]), ALU.is_equal)
            V.tensor_tensor(oneA[:, b, :, :],
                            iota[:, HALF * half:HALF * half + HALF].unsqueeze(1).to_broadcast([P, 4, HALF]),
                            tokT[:, 0, tok].unsqueeze(2).to_broadcast([P, 4, HALF]), ALU.is_equal
                            ).then_inc(S["equal_ready"], 1)

        def gate_mul(n, b, half):
            dve.wait_ge(S["hot_used"], n + 1)
            view = coef[:, HALF * half:HALF * half + HALF, bass.ds(4 * n - 256 * half, 4)].rearrange("p k t -> p t k")
            V.tensor_tensor(view, view, bview(2 + b, 4, HALF), ALU.mult).then_inc(S["g_mul"], 1)

        dve.wait_ge(S["gelu_done"], HALF)

        def u_gated(i, done, last):
            n = 4 * i - 64
            for c in range(16):
                if c >= done:
                    lo_u(i, c, 1)
                if c % 4 == 2 and not (last and c == 14):
                    equal(n + c // 4 + 1, (c // 4 + 1) % 2, 0)
                if c in (5, 9, 13):
                    gate_mul(n + c // 4 - 1, (c // 4 - 1) % 2, 0)
            gate_mul(n + 3, 1, 0)

        equal(0, 0, 0)
        u_gated(16, 1, False)
        with dve.Fori(17, 31) as i:
            u_gated(i, 0, False)
        u_gated(31, 0, True)

        def v_body(ps, i):
            n = 64 + 32 * ps + 2 * i
            for c in range(8):
                tt, jc = divmod(c, 2)
                dve.wait_ge(S["hi_done"], S_V + 128 * ps + 8 * i + c + 1)
                V.tensor_tensor(w_lo[:, c % 4, :], v_ring[:, tt // 2, tt % 2, 512 * jc:512 * jc + 512],
                                w_hi[:, c % 4, :].bitcast(F32), ALU.subtract).then_inc(S["lo_done"], 1)
                if jc == 1:
                    dve.wait_ge(S["c_hi_ok"], 64 * ps + 4 * i + tt + 1)
                    tile_c = coef[:, bass.ds(64 * (ps // 2) + 4 * i + tt, 1), :].rearrange("p a t -> p (a t)")
                    V.tensor_tensor(c_lo[:, tt % 2, :], tile_c, c_hi[:, tt % 2, :].bitcast(F32), ALU.subtract
                                    ).then_inc(S["c_lo_ok"], 1)
                if ps < 2 and c in (1, 5) and not (ps == 1 and isinstance(i, int) and i == 15 and c == 5):
                    equal(n + c // 4 + 1, (c // 4 + 1) % 2, 1)
                if ps < 2 and c in (4, 7):
                    gate_mul(n + c // 7, c // 7, 1)

        def add_pass(ps):
            dve.wait_ge(S["slot_used"], S_V + 128 * (ps + 1))
            for t in range(2):
                for jc in range(2):
                    col = 1024 * (ps % 2) + 512 * jc
                    cols = res[:, t, col:col + 512]
                    acc = bank[(4, 4, 0, 4)[ps] + 2 * t + jc][:, :]
                    if ps < 2:
                        ins = V.scalar_tensor_tensor(cols, cols, ALPHA, acc, ALU.mult, ALU.add)
                    else:
                        ins = V.tensor_tensor(cols, cols, acc, ALU.add)
            ins.then_inc(S["pass_read"], 1)

        dve.drain()
        dve.wait_ge(S["s_res"], 16)
        equal(64, 0, 1)
        with dve.Fori(0, 16) as i:
            v_body(0, i)
        add_pass(0)
        for ps in range(1, 4):
            if ps > 1:
                v_body(ps, 0)
                add_pass(ps - 1)
                with dve.Fori(1, 16) as i:
                    v_body(ps, i)
            else:
                with dve.Fori(0, 15) as i:
                    v_body(ps, i)
                v_body(ps, 15)
        V.memset(eps2[:, :], LN_EPS)
        add_pass(3)
        layer_norm(res, l2st, l2mv, l2rs, S["var2_ok"], S["std2_ok"], S["final_ok"], ln2g_sb, ln2b_sb,
                   S["s_ln2row"], 32)

    block_cm.__exit__(None, None, None)


_INS = ['x', 'w_in', 'cmp_k_pos', 'cmp_k_w1', 'cmp_k_b1', 'cmp_k_w2', 'cmp_v_pos', 'cmp_v_w1', 'cmp_v_b1',
        'cmp_v_w2', 'conv_w', 'head_norm_g', 'w_out', 'ln1_g', 'ln1_b', 'w_query', 'sub_keys', 'expert_u',
        'expert_v', 'ln2_g', 'ln2_b']


def kernel(**inputs):
    import numpy as _np
    import concourse.bacc as _bacc
    from concourse import mybir as _mybir
    from concourse.bass_utils import run_bass_kernel_spmd as _run

    nc = _bacc.Bacc("TRN2", target_bir_lowering=False, num_devices=1)
    arrays, args = {}, []
    for name in _INS:
        a = _np.ascontiguousarray(inputs[name])
        arrays[f"in_{name}_dram"] = a
        args.append(nc.dram_tensor(f"in_{name}_dram", a.shape, _mybir.dt.from_np(a.dtype), kind="ExternalInput").ap())
    out = nc.dram_tensor("out_0_dram", (1, SEQ, D), _mybir.dt.float32, kind="ExternalOutput").ap()
    build(nc, *args, out)
    r = _run(nc, [arrays], core_ids=[0])
    return r.results[0]["out_0_dram"]
```

```python
import concourse.bass as bass
from concourse import mybir

F32 = mybir.dt.float32
F32R = mybir.dt.float32r
BF16 = mybir.dt.bfloat16
U32 = mybir.dt.uint32
ALU = mybir.AluOpType
ACT = mybir.ActivationFunctionType
AX = mybir.AxisListType

P = 128
D = 2048
SEQ = 256
KC = D // P
HD = 128
NH, NG = 8, 2
R = NH // NG
ATT_W = NH * HD
CONV_W = 1024
KV0 = ATT_W
GATE0 = KV0 + 6 * 256
U0 = GATE0 + 3 * NH
B0 = U0 + CONV_W
C0 = B0 + CONV_W
NCMP = (SEQ - 32) // 16 + 1
CHID = 512
NKEY = 128
TOPK = 16
PH = 8
ET = 128
HALF = ET // 2
ALPHA = 2.0 ** 0.25
SCALE = HD ** -0.5
LN_EPS = 1e-5
RMS_EPS = 1e-6
MASKED = 1e30
SLOPES = [2.0 ** (-8.0 * (h + 1) / NH) for h in range(NH)]

S_KV = 0
S_CMP = S_KV + 16
S_GRP = S_CMP + 64
GRP_SLOTS = 80
S_OUT = S_GRP + NG * GRP_SLOTS
S_Q = S_OUT + 64
S_U = S_Q + 64
S_V = S_U + 4 * ET


def build(nc, x, w_in, cmp_k_pos, cmp_k_w1, cmp_k_b1, cmp_k_w2, cmp_v_pos, cmp_v_w1, cmp_v_b1, cmp_v_w2,
          conv_w, head_norm_g, w_out, ln1_g, ln1_b, w_query, sub_keys, expert_u, expert_v, ln2_g, ln2_b, out):
    h_spill = nc.dram_tensor("h_spill", (SEQ, D), F32).ap()

    x_v = x[0].rearrange("(t p) d -> p t d", p=P)
    out_v = out[0].rearrange("(t p) d -> p t d", p=P)
    h_v = h_spill.rearrange("(t p) d -> p t d", p=P)
    win_v = w_in[0].rearrange("(k p) c -> p k c", p=P)
    kv_v = w_in[0][:, KV0 + 512:GATE0].rearrange("(k p) (b v g c) -> v g b p k c", p=P, b=2, v=2, g=NG)
    wout_v = w_out[0].rearrange("(k p) c -> p k c", p=P)
    wq_v = w_query[0].rearrange("(k p) c -> p k c", p=P)
    w1_v = [w[0].rearrange("(j p) c -> p j c", p=P) for w in (cmp_k_w1, cmp_v_w1)]
    eu_v = expert_u[0].rearrange("(t p) d -> t p d", p=P)
    ev_v = expert_v[0].rearrange("(q e p) (c d) -> q c p e d", e=2, p=P, c=2)

    base = (nc.sbuf_base + 63) // 64 * 64
    top = [base]

    def at(name, shape, dt, offset=None):
        n = 2 if dt is BF16 else 4
        for s in shape[1:]:
            n *= s
        if offset is None:
            offset, top[0] = top[0], top[0] + (n + 31) // 32 * 32
        assert offset + n <= nc.sbuf_usable_end, name
        return nc.alloc_sbuf_tensor_at(name, shape, dt, offset=offset)

    K = 1024
    o_act = top[0]
    act_hi = at("act_hi", [P, KC, SEQ], F32R)
    act_lo = at("act_lo", [P, KC, SEQ], F32R)
    w_hi = at("w_hi", [P, 4, 512], F32R)
    w_lo = at("w_lo", [P, 4, 512], F32R)
    o_ring = top[0]
    u_ring = at("u_ring", [P, 2, D], F32)
    v_ring = at("v_ring", [P, 2, 2, 1024], F32, o_ring)
    w_ring = at("w_ring", [P, 4, 8, 256], F32, o_ring)
    coef = at("coef", [P, ET, SEQ], F32)
    oc = o_ring + 16 * K
    end_coef = oc + 128 * K
    xh = at("xh", [P, 2, D], F32, oc + 16 * K)
    mix_hi = at("mix_hi", [P, KC, SEQ], F32R, oc + 32 * K)
    mix_lo = at("mix_lo", [P, KC, SEQ], F32R, oc + 48 * K)
    pos = [oc + 64 * K]

    def tmp(name, shape, dt=F32):
        n = 4
        for s in shape[1:]:
            n *= s
        t = at(name, shape, dt, pos[0])
        pos[0] += (n + 31) // 32 * 32
        assert pos[0] <= oc + 112 * K, name
        return t

    kT = tmp("kT", [P, 2, SEQ])
    v_sb = tmp("v_sb", [P, 2, 2, HD])
    o_qT = pos[0]
    qT = tmp("qT", [P, R, SEQ])
    sc1 = tmp("sc1", [P, 2, 256])
    sc0 = tmp("sc0", [P, 2, 128])
    scc = tmp("scc", [P, 2, 16])
    pT1 = tmp("pT1", [P, 2, 2, 128])
    pT0 = tmp("pT0", [P, 2, 128])
    pTc = tmp("pTc", [16, 2, 128])
    mx = tmp("mx", [P, 6])
    nmx = tmp("nmx", [P, 6])
    sums = tmp("sums", [P, 6])
    rg = tmp("rg", [P, 6])
    cu = tmp("cu", [P, 2, SEQ + 2])
    dist1 = tmp("dist1", [P, 256])
    dist0 = tmp("dist0", [P, 128])
    distc = tmp("distc", [P, 2, 16])
    validc = tmp("validc", [P, 2, 16])
    nslope = tmp("nslope", [P, NH])
    gates = tmp("gates", [P, NH, 6])
    params = tmp("params", [P, 104])
    prow = tmp("prow", [104, P])
    kc_all = tmp("kc_all", [P, 2, 16])
    vc_all = tmp("vc_all", [16, 2, HD])
    nslope_g = tmp("nslope_g", [P, R])
    gates_g = tmp("gates_g", [P, R, 6])
    conv_g = tmp("conv_g", [P, 3, 4])
    norm_g = tmp("norm_g", [P, 2, 4])
    kc_g = tmp("kc_g", [P, 16])
    vc_g = tmp("vc_g", [16, HD])
    ones = tmp("ones", [P, P])
    onerow = tmp("onerow", [1, 32])
    eps = tmp("eps", [P, 2])
    b1row = tmp("b1row", [1, 2, CHID])
    gsig = tmp("gsig", [P, 2, 3 * NH])
    lnst = tmp("lnst", [P, 2, 8, 6])
    lnmv = tmp("lnmv", [P, 2, 2])
    lnrs = tmp("lnrs", [P, 2])
    assert pos[0] <= oc + 96 * K, pos[0] - oc
    c_sb = tmp("c_sb", [P, 2, SEQ])
    cv = tmp("cv", [P, 2, SEQ])
    y_sb = tmp("y_sb", [P, 8, SEQ])
    sq = tmp("sq", [P, 8, SEQ])
    assert pos[0] <= oc + 116 * K
    w1_ring = at("w1_ring", [P, 4, 4, CHID], F32, oc + 96 * K)
    blk_hi = at("blk_hi", [P, 2, 32, 30], F32R, oc + 32 * K)
    blk_lo = at("blk_lo", [P, 2, 32, 30], F32R, oc + 56 * K)
    blk = at("blk", [P, 32, 30], F32, o_qT)
    hid = at("hid", [32, 2, CHID], F32, oc + 40 * K)
    hidT = at("hidT", [P, 2, 4, 32], F32, oc + 44 * K)
    w2 = at("w2", [P, 2, 4, HD], F32, oc + 46 * K)
    gw = at("gw", [P, KC, 24], F32, oc + 50 * K)
    gw_hi = at("gw_hi", [P, KC, 24], F32R, oc + 52 * K)
    gw_lo = at("gw_lo", [P, KC, 24], F32R, oc + 54 * K)
    ln_g = at("ln_g", [P, D], F32, oc + 112 * K)
    ln_b = at("ln_b", [P, D], F32, oc + 120 * K)
    skeys = at("skeys", [P, 16, P], F32, oc + 32 * K)
    skT = at("skT", [P, 16, P], F32, oc + 40 * K)
    qp = at("qp", [P, 2, 2, SEQ], F32, oc + 48 * K)
    scores = at("scores", [P, 16, 2, NKEY], F32, oc + 112 * K)
    rpos = [oc + 104 * K]

    def rtmp(name, shape, dt=F32):
        n = 4
        for s in shape[1:]:
            n *= s
        t = at(name, shape, dt, rpos[0])
        rpos[0] += (n + 31) // 32 * 32
        assert rpos[0] <= oc + 112 * K, name
        return t

    rs = rtmp("rs", [P, 2, NKEY])
    rs2 = rtmp("rs2", [P, 2, NKEY])
    t_val = rtmp("t_val", [P, 2, TOPK])
    t_idx = rtmp("t_idx", [P, 2, TOPK], U32)
    t_idf = rtmp("t_idf", [P, 2, TOPK])
    cand = rtmp("cand", [P, 16, 16])
    cand2 = rtmp("cand2", [P, 16, 16])
    b_idx = rtmp("b_idx", [P, TOPK], U32)
    b_ij = rtmp("b_ij", [P, 2, TOPK], U32)
    b_ijf = rtmp("b_ijf", [P, 2, TOPK])
    b_val = rtmp("b_val", [P, TOPK])
    eq = rtmp("eq", [P, 2, TOPK, 16])
    b_id = rtmp("b_id", [P, 2, TOPK])
    iota16 = rtmp("iota16", [P, 16])
    g_rest = rtmp("g_rest", [P, SEQ])
    picks = at("picks", [P, 3, 16, TOPK], F32, oc + 96 * K)
    picks_t = at("picks_t", [P, 3, 2, PH, TOPK], F32, oc + 99 * K)
    pick_ref = at("pick_ref", [P, 16], F32, oc + 102 * K)
    res = at("res", [P, 2, D], F32, o_act)
    c_hi = at("c_hi", [P, 4, SEQ], F32R, o_act + 16 * K)
    c_lo = at("c_lo", [P, 4, SEQ], F32R, o_act + 20 * K)
    l2st = at("l2st", [P, 2, 4, 6], F32, o_act + 24 * K)
    l2mv = at("l2mv", [P, 2, 2], F32, o_act + 25 * K)
    l2rs = at("l2rs", [P, 2], F32, o_act + 25 * K + 64)
    l2shift = at("l2shift", [P, 1], F32, o_act + 25 * K + 96)
    eps2 = at("eps2", [P, 2], F32, o_act + 25 * K + 128)
    ln2g_sb = at("ln2g_sb", [P, D], F32, oc)
    ln2b_sb = at("ln2b_sb", [P, D], F32, oc + 8 * K)
    ident = at("ident", [P, P], F32)
    iota = at("iota", [P, P], F32)
    iota_h = at("iota_h", [P, P], BF16)
    tok_id = at("tok_id", [P, 2, SEQ], BF16)
    tok_g = at("tok_g", [P, 3, SEQ], BF16)
    oneB = at("oneB", [P, 2, 4, NKEY], BF16)
    oneA = at("oneA", [P, 2, 4, HALF], BF16)
    hotA = at("hotA", [P, 2, 3, 4, HALF], BF16)

    bank = [nc.alloc_psum_tensor(f"bank{i}", [P, 512], F32) for i in range(8)]

    names = """s_ident s_const s_small s_cw2 s_skeys s_lnrow s_ln2row s_hspill s_res s_out
        tr_done tr_hi tr_lo params_T params_ok gw_hi_ok gw_ready gate_mm gate_sig
        blk_raw blk_hi_ok blk_ready hid_mm hid_ready hidT_mm hidT_ok cmp_mm cmp_ok
        hi_done lo_done slot_used acc_act acc_dve grp_ready
        qk_done biased exps probs_ready pt_done pt_act pt_dve o_done y_att
        squared y_conv norm_mm rms_ok mixf_ready mix_hi_ok mix_ready
        var_ok std_ok ln1_done sk_mm sk_ok score_mm score_ok
        u_tr gelu_done picks_raw picks_exp picks_ok tok_mm tok_ok
        equal_ready hot_ready hot_used g_mul c_hi_ok c_lo_ok pass_read eps2_ok var2_ok std2_ok shift2_ok scaled2
        final_ok final_pool""".split()
    S = {n: nc.alloc_semaphore(n) for n in names}
    s_w = [nc.alloc_semaphore(f"s_w{i}") for i in range(4)]
    s_x = [nc.alloc_semaphore(f"s_x{i}") for i in range(4)]
    s_w1 = [nc.alloc_semaphore(f"s_w1_{i}") for i in range(4)]
    s_u = [nc.alloc_semaphore(f"s_u{i}") for i in range(2)]
    s_v = [nc.alloc_semaphore(f"s_v{i}") for i in range(2)]

    def bview(i, *shape):
        n = 1
        for s in shape:
            n *= s
        names_ = "abc"[:len(shape)]
        if len(shape) == 1:
            return bank[i][:, 0:n]
        return bank[i][:, 0:n].rearrange("p (%s) -> p %s" % (" ".join(names_), " ".join(names_)),
                                         **dict(zip(names_, shape)))

    block_cm = nc.Block()
    block = block_cm.__enter__()

    @block.sync
    def _(sp):
        def load_w(c, src, after):
            if after is not None:
                sp.wait_ge(S["lo_done"], after)
            for n in range(2):
                sp.dma_start(w_ring[:, c % 4, 4 * n:4 * n + 4, :], src[:, 4 * n:4 * n + 4, :]
                             ).then_inc(s_w[c % 4], 16)

        def load_x(q):
            sp.dma_start(xh[:, :, 512 * q:512 * q + 512], x_v[:, :, 512 * q:512 * q + 512]).then_inc(s_x[q], 16)

        for c in range(4):
            if c < 2:
                load_x(2 * c)
                load_x(2 * c + 1)
            t, hh = divmod(c, 2)
            load_w(c, win_v[:, 8 * hh:8 * hh + 8, KV0 + 256 * t:KV0 + 256 * t + 256], None)
        with sp.Fori(0, NG) as g:
            for t in range(10):
                for hh in range(2):
                    c = 2 * t + hh
                    after = S_GRP + GRP_SLOTS * g + 4 * (c - 3) if c >= 4 else 4 + 4 * c + (S_GRP + GRP_SLOTS - 16) * g
                    if t < 2:
                        sp.wait_ge(S["lo_done"], after)
                        for b in range(2):
                            src = kv_v[t, bass.ds(g, 1), b].rearrange("g p k c -> p k (g c)")
                            sp.dma_start(w_ring[:, c % 4, :, 128 * b:128 * b + 128],
                                         src[:, 8 * hh:8 * hh + 8, :]).then_inc(s_w[c % 4], 16)
                        continue
                    col = (0, 256, C0, U0, B0, C0 + 256, U0 + 256, B0 + 256)[t - 2] + 512 * g
                    load_w(c, win_v[:, 8 * hh:8 * hh + 8, bass.ds(col, 256)], after)
        for s0, view in ((S_OUT, wout_v), (S_Q, wq_v)):
            with sp.Fori(0, 4) as j:
                for c in range(4):
                    t, hh = divmod(c, 2)
                    load_w(c, view[:, 8 * hh:8 * hh + 8, bass.ds(512 * j + 256 * t, 256)],
                           s0 + 16 * j + 4 * (c - 3))

        def load_u(t, r):
            sp.dma_start(u_ring[:, r, :], eu_v[bass.ds(t, 1)].rearrange("t p d -> p (t d)")).then_inc(s_u[r], 16)

        for r in range(2):
            sp.wait_ge(S["lo_done"], S_U - 8 + 4 * r)
            load_u(r, r)
        with sp.Fori(1, ET // 2) as j:
            for r in range(2):
                sp.wait_ge(S["u_tr"], 8 * j + 4 * r - 4)
                load_u(2 * j + r, r)
        def load_v(ps, i, r):
            sp.dma_start(v_ring[:, r, :, :],
                         ev_v[bass.ds(32 * (ps // 2) + 2 * i + r, 1), ps % 2].rearrange("q p e d -> p (q e) d")
                         ).then_inc(s_v[r], 16)

        for r in range(2):
            sp.wait_ge(S["u_tr"], 4 * ET - 4 + 4 * r)
            load_v(0, 0, r)
        sp.wait_ge(S["slot_used"], S_V)
        sp.dma_start(res[:, :, :], h_v).then_inc(S["s_res"], 16)
        for ps in range(4):
            with sp.Fori(1 if ps == 0 else 0, 16) as i:
                for r in range(2):
                    sp.wait_ge(S["lo_done"], S_V + 128 * ps + 8 * i + 4 * r - 4)
                    load_v(ps, i, r)
        def store(t, q, sem, count):
            sp.wait_ge(sem, count)
            sp.dma_start(out_v[:, t, 512 * q:512 * q + 512], res[:, t, 512 * q:512 * q + 512]).then_inc(S["s_out"], 16)

        for q in range(3):
            store(0, q, S["final_ok"], q + 1)
            store(1, q, S["final_pool"], q + 1)
        store(0, 3, S["final_ok"], 4)
        store(1, 3, S["final_ok"], 5)
        sp.wait_ge(S["s_out"], 16 * 8)

    @block.gpsimd
    def _(pool):
        nc.gpsimd.memset(ident[:, :], 0.0)
        pool.drain()
        nc.gpsimd.affine_select(out=ident[:, :], in_=ident[:, :], compare_op=ALU.not_equal, fill=1.0,
                                base=0, pattern=[[-1, P]], channel_multiplier=1).then_inc(S["s_ident"], 1)
        nc.gpsimd.memset(ones[:, :], 1.0 / HD)
        nc.gpsimd.memset(onerow[:, :], 1.0)
        nc.gpsimd.memset(eps[:, 0:1], RMS_EPS)
        nc.gpsimd.memset(eps[:, 1:2], LN_EPS)
        nc.gpsimd.memset(cu[:, :, :], 0.0)
        nc.gpsimd.memset(scc[:, :, :], 0.0)
        nc.gpsimd.memset(validc[:, :, :], 1.0)
        nc.gpsimd.memset(kc_all[:, :, :], 0.0)
        for h in range(NH):
            nc.gpsimd.memset(nslope[:, h:h + 1], -SLOPES[h])
        kw = dict(allow_small_or_imprecise_dtypes=True)
        nc.gpsimd.iota(iota[:, :], [[1, P]], base=0, channel_multiplier=0, **kw)
        nc.gpsimd.iota(dist1[:, :], [[-1, 256]], base=128, channel_multiplier=1, **kw)
        nc.gpsimd.iota(dist0[:, :], [[-1, 128]], base=0, channel_multiplier=1, **kw)
        nc.gpsimd.iota(distc[:, :, :], [[128, 2], [-16, 16]], base=0, channel_multiplier=1, **kw)
        pool.drain()
        nc.gpsimd.tensor_scalar(distc[:, :, :], distc[:, :, :], -15.5, None, ALU.add)
        nc.gpsimd.affine_select(out=dist1[:, :], in_=dist1[:, :], compare_op=ALU.is_ge, fill=MASKED,
                                base=128, pattern=[[-1, 256]], channel_multiplier=1)
        nc.gpsimd.affine_select(out=dist0[:, :], in_=dist0[:, :], compare_op=ALU.is_ge, fill=MASKED,
                                base=0, pattern=[[-1, 128]], channel_multiplier=1)
        pool.drain()
        nc.gpsimd.affine_select(out=distc[:, :, :], in_=distc[:, :, :], compare_op=ALU.is_ge, fill=MASKED,
                                base=-31, pattern=[[128, 2], [-16, 16]], channel_multiplier=1)
        nc.gpsimd.affine_select(out=validc[:, :, :], in_=validc[:, :, :], compare_op=ALU.is_ge, fill=0.0,
                                base=-31, pattern=[[128, 2], [-16, 16]], channel_multiplier=1)
        pool.drain()
        pool.nop().then_inc(S["s_const"], 1)
        for i in range(16):
            if i < 4:
                pool.wait_ge(s_w[i], 32)
            else:
                pool.wait_ge(S["lo_done"], S_CMP + 4 * (i - 3))
            pool.dma_start(w1_ring[:, i % 4, :, :], w1_v[i // 8][:, 4 * (i % 8):4 * (i % 8) + 4, :]
                           ).then_inc(s_w1[i % 4], 16)
        pool.wait_ge(S["lo_done"], S_CMP + 64)
        pool.dma_start(ln_g[:, :], ln1_g.partition_broadcast(P).rearrange("p a d -> p (a d)")).then_inc(S["s_lnrow"], 16)
        pool.dma_start(ln_b[:, :], ln1_b.partition_broadcast(P).rearrange("p a d -> p (a d)")).then_inc(S["s_lnrow"], 16)
        pool.wait_ge(S["slot_used"], S_Q)
        pool.dma_start(skeys[:, :, :], sub_keys[0].rearrange("h c n d -> n (h c) d")).then_inc(S["s_skeys"], 16)
        pool.wait_ge(S["ln1_done"], 4)
        pool.dma_start(h_v, xh[:, :, :]).then_inc(S["s_hspill"], 16)
        pool.wait_ge(S["s_hspill"], 16)

        def weigh(half, n, b):
            pool.wait_ge(S["equal_ready"], n + 1)
            gate = tok_g[:, :, bass.ds(4 * n - 256 * half, 4)].unsqueeze(3).to_broadcast([P, 3, 4, HALF])
            nc.gpsimd.tensor_tensor(hotA[:, b, :, :, :], oneA[:, b, :, :].unsqueeze(1).to_broadcast([P, 3, 4, HALF]),
                                    gate, ALU.mult).then_inc(S["hot_ready"], 1)

        for half in range(2):
            with pool.Fori(0, 32) as j:
                for b in range(2):
                    weigh(half, 64 * half + 2 * j + b, b)

        pool.wait_ge(S["slot_used"], S_V + 2 * 128)
        for row, src in ((ln2g_sb, ln2_g), (ln2b_sb, ln2_b)):
            pool.dma_start(row[:, :], src.partition_broadcast(P).rearrange("p a d -> p (a d)")
                           ).then_inc(S["s_ln2row"], 16)
        pool.wait_ge(S["s_ln2row"], 32)
        for q in range(3):
            cols = slice(512 * q, 512 * q + 512)
            pool.wait_ge(S["scaled2"], q + 1)
            nc.gpsimd.tensor_tensor(res[:, 1, cols], res[:, 1, cols], ln2g_sb[:, cols], ALU.mult)
            pool.drain()
            nc.gpsimd.tensor_tensor(res[:, 1, cols], res[:, 1, cols], ln2b_sb[:, cols], ALU.add
                                    ).then_inc(S["final_pool"], 1)

    @block.tensor
    def _(pe):
        def tile(kind, acc, s, lo=0, hi=8):
            for c in range(lo, hi):
                pe.wait_ge(S["lo_done"], s + c + 1)
                r = c % 4
                for kk in range(2):
                    k = 2 * c + kk
                    for b in range(2):
                        o = bank[acc][:, 256 * b:256 * b + 256]
                        half = slice(128 * b, 128 * b + 128)
                        if kind == "T":
                            w = slice(256 * kk + 128 * b, 256 * kk + 128 * b + 128)
                            pairs = ((w_hi[:, r, w], act_hi[:, k, :]), (w_hi[:, r, w], act_lo[:, k, :]),
                                     (w_lo[:, r, w], act_hi[:, k, :]))
                        else:
                            a_hi, a_lo = (act_hi, act_lo) if kind == "V" else (mix_hi, mix_lo)
                            w = slice(256 * kk, 256 * kk + 256)
                            pairs = ((a_hi[:, k, half], w_hi[:, r, w]), (a_hi[:, k, half], w_lo[:, r, w]),
                                     (a_lo[:, k, half], w_hi[:, r, w]))
                        for n, (st, mv) in enumerate(pairs):
                            ins = nc.tensor.matmul(o, st, mv, start=(k == 0 and b == 0 and n == 0),
                                                   stop=(k == KC - 1 and n == 2), skip_group_check=True)
                ins.then_inc(S["slot_used"], 1)

        def transpose_unit(n0, u):
            if u % 2 == 0 and n0 == 0:
                pe.wait_ge(s_x[u // 2], 16)
            if u % 2 == 0 and n0:
                pe.wait_ge(S["ln1_done"], u // 2 + 1)
            if n0 + u >= 4:
                pe.wait_ge(S["tr_lo"], n0 + u - 3)
            for kk in range(2):
                for t in range(2):
                    col = 128 * (2 * u + kk)
                    ins = nc.tensor.transpose(bank[4 + u % 4][:, 256 * kk + 128 * t:256 * kk + 128 * t + 128],
                                              xh[:, t, col:col + 128], ident[:, :])
            ins.then_inc(S["tr_done"], 1)

        def first_tile(n0, s, units):
            for c in range(8):
                for u in range(units[c - 1] if c else 0, units[c]):
                    transpose_unit(n0, u)
                pe.wait_ge(S["tr_lo"], n0 + c + 1)
                tile("T", 0, s, c, c + 1)

        pe.wait_ge(S["s_ident"], 1)
        first_tile(0, S_KV, (4, 4, 6, 6, 8, 8, 8, 8))
        pe.wait_ge(S["s_small"], 16 * 7)
        nc.tensor.transpose(bank[2][:, 0:104], prow[0:104, :], ident[0:104, 0:104]).then_inc(S["params_T"], 1)
        tile("T", 1, S_KV + 8)
        pe.wait_ge(S["gw_ready"], 1)
        for t in range(2):
            tk = slice(128 * t, 128 * t + 128)
            for k in range(KC):
                o = bank[3][:, 32 * t:32 * t + 24]
                nc.tensor.matmul(o, act_hi[:, k, tk], gw_hi[:, k, :], start=(k == 0), stop=False)
                nc.tensor.matmul(o, act_hi[:, k, tk], gw_lo[:, k, :], start=False, stop=False)
                ins = nc.tensor.matmul(o, act_lo[:, k, tk], gw_hi[:, k, :], start=False, stop=(k == KC - 1))
        ins.then_inc(S["gate_mm"], 1)
        pe.wait_ge(S["s_const"], 1)
        pe.wait_ge(S["params_ok"], 1)
        for kv in range(2):
            pe.wait_ge(S["blk_ready"], kv + 1)
            o = bank[(2, 4)[kv]][0:30, :]
            for j in range(32):
                q = 32 * kv + j
                pe.wait_ge(S["lo_done"], S_CMP + q + 1)
                nc.tensor.matmul(o, blk_hi[:, kv, j, :], w_hi[:, q % 4, :], start=(j == 0), stop=False)
                nc.tensor.matmul(o, blk_hi[:, kv, j, :], w_lo[:, q % 4, :], start=False, stop=False)
                nc.tensor.matmul(o, blk_lo[:, kv, j, :], w_hi[:, q % 4, :], start=False, stop=False
                                 ).then_inc(S["slot_used"], 1)
            nc.tensor.matmul(bank[(2, 4)[kv]][0:30, :], onerow[0:1, 0:30], b1row[0:1, kv, :],
                             start=False, stop=True).then_inc(S["hid_mm"], 1)
        pe.wait_ge(S["hid_ready"], 2)
        for kv in range(2):
            for m in range(4):
                o = bank[5][:, 128 * kv + 32 * m:128 * kv + 32 * m + 30]
                ins = nc.tensor.transpose(o, hid[0:30, kv, 128 * m:128 * m + 128], ident[0:30, 0:30])
        ins.then_inc(S["hidT_mm"], 1)
        pe.wait_ge(S["hidT_ok"], 1)
        pe.wait_ge(S["s_cw2"], 32)
        for m in range(4):
            nc.tensor.matmul(bank[6][:, 0:30], w2[:, 0, m, :], hidT[:, 0, m, 0:30], start=(m == 0), stop=(m == 3))
        for g in range(NG):
            for m in range(4):
                ins = nc.tensor.matmul(bank[7][0:NCMP, 128 * g:128 * g + 128], hidT[:, 1, m, 15 * g:15 * g + 15],
                                       w2[:, 1, m, :], start=(m == 0), stop=(m == 3))
        ins.then_inc(S["cmp_mm"], 1)
        pe.wait_ge(S["cmp_ok"], 1)
        pe.wait_ge(S["gate_sig"], 1)

        with pe.Fori(0, NG) as g:
            s = S_GRP + GRP_SLOTS * g

            def score(r):
                for b in range(2):
                    nc.tensor.matmul(bank[2][:, 256 * b:256 * b + 256], qT[:, r, 128:256], kT[:, b, :],
                                     start=True, stop=True)
                for b in range(2):
                    nc.tensor.matmul(bank[3][:, 128 * b:128 * b + 128], qT[:, r, 0:128], kT[:, b, 0:128],
                                     start=True, stop=True)
                for t in range(2):
                    ins = nc.tensor.matmul(bank[3][:, 256 + 16 * t:272 + 16 * t], qT[:, r, 128 * t:128 * t + 128],
                                           kc_g[:, :], start=True, stop=True)
                ins.then_inc(S["qk_done"], 1)

            def transpose_probs(r):
                pe.wait_ge(S["probs_ready"], R * g + r + 1)
                for b in range(2):
                    for c in range(2):
                        nc.tensor.transpose(bank[4][:, 256 * b + 128 * c:256 * b + 128 * c + 128],
                                            sc1[:, b, 128 * c:128 * c + 128], ident[:, :])
                for b in range(2):
                    nc.tensor.transpose(bank[5][:, 128 * b:128 * b + 128], sc0[:, b, :], ident[:, :])
                for t in range(2):
                    ins = nc.tensor.transpose(bank[5][0:16, 256 + 128 * t:384 + 128 * t], scc[:, t, :], ident[:, :])
                ins.then_inc(S["pt_done"], 1)

            def attend(r):
                pe.wait_ge(S["pt_act"], R * g + r + 1)
                pe.wait_ge(S["pt_dve"], R * g + r + 1)
                if r:
                    pe.wait_ge(S["y_att"], R * g + r)
                parts0 = [(v_sb[:, 0, b, :], pT0[:, b, :]) for b in range(2)]
                parts0.append((vc_g[0:NCMP, :], pTc[0:NCMP, 0, :]))
                parts1 = [(v_sb[:, c, b, :], pT1[:, b, c, :]) for b in range(2) for c in range(2)]
                parts1.append((vc_g[0:NCMP, :], pTc[0:NCMP, 1, :]))
                for t, parts in ((0, parts0), (1, parts1)):
                    for n, (vv, pp) in enumerate(parts):
                        ins = nc.tensor.matmul(bank[6][:, 128 * t:128 * t + 128], vv, pp,
                                               start=(n == 0), stop=(n == len(parts) - 1))
                ins.then_inc(S["o_done"], 1)

            pe.wait_ge(S["acc_dve"], 4 * g + 1)
            tile("T", 0, s)
            pe.wait_ge(S["acc_dve"], 4 * g + 2)
            tile("V", 1, s + 8)
            pe.wait_ge(S["acc_act"], 6 * g + 1)
            tile("T", 0, s + 16)
            pe.wait_ge(S["acc_act"], 6 * g + 2)
            tile("T", 1, s + 24)
            pe.wait_ge(S["acc_act"], 6 * g + 3)
            pe.wait_ge(S["grp_ready"], g + 1)
            score(0)
            tile("T", 0, s + 32)
            transpose_probs(0)
            score(1)
            pe.wait_ge(S["acc_act"], 6 * g + 4)
            tile("T", 1, s + 40)
            attend(0)
            transpose_probs(1)
            score(2)
            pe.wait_ge(S["acc_act"], 6 * g + 5)
            tile("T", 0, s + 48)
            attend(1)
            transpose_probs(2)
            score(3)
            pe.wait_ge(S["acc_dve"], 4 * g + 3)
            tile("T", 1, s + 56)
            attend(2)
            transpose_probs(3)
            pe.wait_ge(S["acc_dve"], 4 * g + 4)
            tile("T", 0, s + 64)
            attend(3)
            pe.wait_ge(S["acc_act"], 6 * g + 6)
            tile("T", 1, s + 72, 0, 4)

            def mean_square(n):
                pe.wait_ge(S["squared"], 4 * g + n + 1)
                nc.tensor.matmul(bank[2 + n][:, :], ones[:, :],
                                 sq[:, 2 * n:2 * n + 2, :].rearrange("p a t -> p (a t)"),
                                 start=True, stop=True).then_inc(S["norm_mm"], 1)

            for n in range(3):
                mean_square(n)
            tile("T", 1, s + 72, 4, 8)
            mean_square(3)

        pe.wait_ge(S["mix_ready"], 2 * NG - 1)
        with pe.Fori(0, 4) as j:
            for t in range(2):
                pe.wait_ge(S["acc_dve"], 1 + 4 * NG + 2 * j + t)
                tile("M", t, S_OUT + 16 * j + 8 * t, 0, 7)
                pe.wait_ge(S["mix_ready"], 2 * NG)
                tile("M", t, S_OUT + 16 * j + 8 * t, 7, 8)

        pe.wait_ge(S["acc_dve"], 2 + 4 * NG + 8)
        first_tile(8, S_Q, (3, 4, 5, 6, 7, 8, 8, 8))
        pe.wait_ge(S["s_skeys"], 16)
        pe.wait_ge(S["tr_lo"], 16)
        for n in range(4):
            for i in range(4):
                ins = nc.tensor.transpose(bank[4 + n][:, 128 * i:128 * i + 128], skeys[:, 4 * n + i, :], ident[:, :])
            ins.then_inc(S["sk_mm"], 1)

        def scores_of(h, b):
            pe.wait_ge(S["acc_act"], 6 * NG + h + 1)
            for t in range(2):
                for c in range(2):
                    ins = nc.tensor.matmul(bank[2 + b][:, 256 * t + 128 * c:256 * t + 128 * c + 128],
                                           qp[:, b, c, 128 * t:128 * t + 128],
                                           skT[:, bass.ds(2 * h + c, 1), :].rearrange("p a n -> p (a n)"),
                                           start=True, stop=True)
            ins.then_inc(S["score_mm"], 1)

        def odd_tile(j):
            tile("T", 1, S_Q + 16 * j + 8, 0, 4)
            pe.wait_ge(S["sk_ok"], 4)
            scores_of(2 * j, 0)
            tile("T", 1, S_Q + 16 * j + 8, 4, 8)

        odd_tile(0)
        with pe.Fori(1, 4) as j:
            pe.wait_ge(S["acc_act"], 6 * NG + 2 * j - 1)
            tile("T", 0, S_Q + 16 * j, 0, 2)
            scores_of(2 * j - 1, 1)
            tile("T", 0, S_Q + 16 * j, 2, 8)
            odd_tile(j)

        def transpose_u(count, k, slot):
            if k == 0:
                pe.wait_ge(s_u[slot], count)
            for i in range(4):
                col = 512 * k + 128 * i
                ins = nc.tensor.transpose(bank[4 + k][:, 128 * i:128 * i + 128],
                                          u_ring[:, slot, col:col + 128], ident[:, :])
            ins.then_inc(S["u_tr"], 1)

        def gate_tokens(n, b, q0, q1):
            if q0 == 0:
                if not (isinstance(n, int) and n < 2):
                    pe.wait_ge(S["g_mul"], n - 1)
                pe.wait_ge(S["hot_ready"], n + 1)
            for q in range(q0, q1):
                for part in range(3):
                    ins = nc.tensor.matmul(bank[2 + b][:, HALF * q:HALF * q + HALF], oneB[:, b, q, :],
                                           hotA[:, b, part, q, :], start=(part == 0), stop=(part == 2))
            if q1 == 4:
                ins.then_inc(S["hot_used"], 1)

        def transpose_picks():
            pe.wait_ge(S["picks_ok"], 1)
            for n in range(6):
                a, t = divmod(n, 2)
                ins = nc.tensor.transpose(bank[2 + n // 4][:, 128 * (n % 4):128 * (n % 4) + 128],
                                          picks_t[:, a, t, :, :].rearrange("p h k -> p (h k)"), ident[:, :])
            ins.then_inc(S["tok_mm"], 1)

        def u_body(i, gated, last):
            for c in range(16):
                tt, k = divmod(c, 4)
                if not (last and c >= 13):
                    at_, ak = divmod(c + 3, 4)
                    transpose_u(16 * (2 * i + at_ // 2 + 1), ak, at_ % 2)
                pe.wait_ge(S["lo_done"], S_U + 16 * i + c + 1)
                if k == 0 and not (isinstance(i, int) and 4 * i + tt < 2):
                    pe.wait_ge(S["gelu_done"], 4 * i + tt - 1)
                for n in range(4):
                    dk = 4 * k + n
                    o = bank[tt % 2][:, 0:SEQ]
                    wh, wl = w_hi[:, k, 128 * n:128 * n + 128], w_lo[:, k, 128 * n:128 * n + 128]
                    nc.tensor.matmul(o, wh, act_hi[:, dk, :], start=(dk == 0), stop=False)
                    nc.tensor.matmul(o, wh, act_lo[:, dk, :], start=False, stop=False)
                    ins = nc.tensor.matmul(o, wl, act_hi[:, dk, :], start=False, stop=(dk == KC - 1))
                ins.then_inc(S["slot_used"], 1)
                if isinstance(i, int) and i == 16 and c < 5:
                    if c == 1:
                        transpose_picks()
                    if c == 4:
                        pe.wait_ge(S["tok_ok"], 1)
                        gate_tokens(0, 0, 0, 4)
                if gated and c % 4 < 2 and not (isinstance(i, int) and i == 16 and c < 4):
                    gate_tokens(4 * i - 64 + c // 4, (c // 4) % 2, 2 * (c % 4), 2 * (c % 4) + 2)

        for k in range(3):
            transpose_u(16, k, 0)
        scores_of(7, 1)
        pe.wait_ge(S["score_ok"], 8)
        u_body(0, False, False)
        with pe.Fori(1, 16) as i:
            u_body(i, False, False)
        u_body(16, True, False)
        with pe.Fori(17, 31) as i:
            u_body(i, True, False)
        u_body(31, True, True)

        def v_body(ps, i, first, last):
            b0 = (4, 4, 0, 4)[ps]
            for c in range(8):
                tt, jc = divmod(c, 2)
                r = c % 4
                pe.wait_ge(S["lo_done"], S_V + 128 * ps + 8 * i + c + 1)
                if jc == 0:
                    pe.wait_ge(S["c_lo_ok"], 64 * ps + 4 * i + tt + 1)
                if first and ps in (1, 3) and tt == 0:
                    pe.wait_ge(S["pass_read"], ps + jc)
                for t in range(2):
                    o = bank[b0 + 2 * t + jc][:, :]
                    tk = slice(128 * t, 128 * t + 128)
                    nc.tensor.matmul(o, c_hi[:, tt, tk], w_hi[:, r, :], start=first and tt == 0, stop=False)
                    nc.tensor.matmul(o, c_hi[:, tt, tk], w_lo[:, r, :], start=False, stop=False)
                    ins = nc.tensor.matmul(o, c_lo[:, tt, tk], w_hi[:, r, :], start=False,
                                           stop=last and tt == 3)
                ins.then_inc(S["slot_used"], 1)
                if ps < 2 and c in (0, 1, 3, 4):
                    b = c // 3
                    q0 = 2 * (c % 3)
                    gate_tokens(64 + 32 * ps + 2 * i + b, b, q0, q0 + 2)

        for ps in range(4):
            if ps == 2:
                pe.wait_ge(S["g_mul"], 128)
            v_body(ps, 0, True, False)
            with pe.Fori(1, 15) as i:
                v_body(ps, i, False, False)
            v_body(ps, 15, False, True)

    @block.scalar
    def _(act):
        small = [
            (prow[0:24, :], conv_w[0].rearrange("j (b c) -> (j b) c", c=P)),
            (prow[24:40, :], head_norm_g[0].rearrange("(b c) -> b c", c=P)),
            (prow[40:72, :], cmp_k_pos[0]),
            (prow[72:104, :], cmp_v_pos[0]),
            (b1row[0:1, 0, :], cmp_k_b1),
            (b1row[0:1, 1, :], cmp_v_b1),
            (gw[:, :, :], win_v[:, :, GATE0:GATE0 + 24]),
        ]
        for dst, src in small:
            act.dma_start(dst, src).then_inc(S["s_small"], 16)
        for kv in range(2):
            act.dma_start(w2[:, kv, :, :], (cmp_k_w2, cmp_v_w2)[kv][0].rearrange("(m p) d -> p m d", p=P)
                           ).then_inc(S["s_cw2"], 16)

        def hi_w(s, c, n):
            for q in range(c, c + n):
                if q % 4 == 0:
                    act.wait_ge(s_w[(q // 4) % 4], s_count(s, q))
                if not (isinstance(s, int) and s + q < 4):
                    act.wait_ge(S["slot_used"], s + q - 3)
                src = w_ring[:, (q // 4) % 4, 2 * (q % 4):2 * (q % 4) + 2, :].rearrange("p k c -> p (k c)")
                nc.scalar.activation(w_hi[:, q % 4, :], src, ACT.Copy).then_inc(S["hi_done"], 1)

        def s_count(s, q):
            if s is S_KV:
                return 32
            return 2 * (s - 64) + (q // 16 + 1) * 32

        def transpose_hi(n0, u):
            act.wait_ge(S["tr_done"], n0 + u + 1)
            nc.scalar.activation(act_hi[:, 2 * u:2 * u + 2, :], bview(4 + u % 4, 2, SEQ), ACT.Copy
                                 ).then_inc(S["tr_hi"], 1)

        for u in range(8):
            transpose_hi(0, u)
            if u == 3:
                hi_w(S_KV, 0, 4)
        hi_w(S_KV, 4, 4)
        act.wait_ge(S["s_small"], 16 * 7)
        nc.scalar.activation(gw_hi[:, :, :], gw[:, :, :], ACT.Copy).then_inc(S["gw_hi_ok"], 1)
        hi_w(S_KV, 8, 8)
        for kv in range(2):
            act.wait_ge(S["blk_raw"], kv + 1)
            nc.scalar.activation(blk_hi[:, kv, :, :], blk[:, :, :], ACT.Copy).then_inc(S["blk_hi_ok"], 1)

        def hi_cmp(q0, q1):
            for q in range(q0, q1):
                if q % 4 == 0:
                    act.wait_ge(s_w1[(q // 4) % 4], 16 * (q // 16 + 1))
                act.wait_ge(S["slot_used"], S_CMP + q - 3)
                nc.scalar.activation(w_hi[:, q % 4, :], w1_ring[:, (q // 4) % 4, q % 4, :], ACT.Copy
                                     ).then_inc(S["hi_done"], 1)

        def hidden(kv):
            act.wait_ge(S["hid_mm"], kv + 1)
            nc.scalar.activation(hid[0:30, kv, :], bank[(2, 4)[kv]][0:30, :], ACT.Gelu_apprx_tanh
                                 ).then_inc(S["hid_ready"], 1)

        hi_cmp(0, 4)
        act.wait_ge(S["gate_mm"], 1)
        nc.scalar.activation(gsig[:, :, :], bank[3][:, 0:64].rearrange("p (t c) -> p t c", t=2)[:, :, 0:24],
                             ACT.Sigmoid).then_inc(S["gate_sig"], 1)
        hi_cmp(4, 36)
        hidden(0)
        hi_cmp(36, 64)
        hi_w(S_GRP, 0, 4)
        hidden(1)
        with act.Fori(0, NG) as g:
            s = S_GRP + GRP_SLOTS * g

            def expo(r, c):
                act.wait_ge(S["biased"], R * g + r + 1)
                for b in range(2):
                    nc.scalar.activation(sc1[:, b, :], sc1[:, b, :], ACT.Exp, bias=nmx[:, b:b + 1],
                                         accum_out=sums[:, b:b + 1])
                hi_w(s, c, 1)
                for b in range(2):
                    nc.scalar.activation(sc0[:, b, :], sc0[:, b, :], ACT.Exp, bias=nmx[:, 2 + b:3 + b],
                                         accum_out=sums[:, 2 + b:3 + b])
                hi_w(s, c + 1, 1)
                for t in range(2):
                    ins = nc.scalar.activation(scc[:, t, 0:NCMP], scc[:, t, 0:NCMP], ACT.Exp,
                                               bias=nmx[:, 4 + t:5 + t], accum_out=sums[:, 4 + t:5 + t])
                ins.then_inc(S["exps"], 1)
                hi_w(s, c + 2, 1)

            def probs_out(r):
                act.wait_ge(S["pt_done"], R * g + r + 1)
                nc.scalar.activation(pT1[:, :, :, :].rearrange("p b c t -> p (b c t)"), bank[4][:, :], ACT.Copy
                                     ).then_inc(S["pt_act"], 1)

            def att_out(r):
                act.wait_ge(S["o_done"], R * g + r + 1)
                nc.scalar.activation(y_sb[:, r, :], bank[6][:, 0:SEQ], ACT.Copy).then_inc(S["y_att"], 1)

            def tile_out(dst, src, end, scale=1.0):
                act.wait_ge(S["slot_used"], s + end)
                nc.scalar.activation(dst, src, ACT.Copy, scale=scale).then_inc(S["acc_act"], 1)

            hi_w(s, 4, 8)
            tile_out(kT[:, :, :], bview(0, 2, SEQ), 8)
            hi_w(s, 12, 8)
            tile_out(v_sb[:, :, :, :].rearrange("p t b c -> p (t b c)"), bank[1][:, :], 16)
            hi_w(s, 20, 8)
            tile_out(qT[:, 0:2, :], bview(0, 2, SEQ), 24, SCALE)
            hi_w(s, 28, 8)
            tile_out(qT[:, 2:4, :], bview(1, 2, SEQ), 32, SCALE)
            expo(0, 36)
            hi_w(s, 39, 5)
            tile_out(c_sb[:, :, :], bview(0, 2, SEQ), 40)
            probs_out(0)
            expo(1, 44)
            hi_w(s, 47, 5)
            att_out(0)
            probs_out(1)
            expo(2, 52)
            hi_w(s, 55, 5)
            att_out(1)
            probs_out(2)
            expo(3, 60)
            hi_w(s, 63, 5)
            tile_out(c_sb[:, :, :], bview(1, 2, SEQ), 64)
            att_out(2)
            probs_out(3)
            hi_w(s, 68, 8)
            att_out(3)
            act.drain()
            def square(n):
                nc.scalar.activation(sq[:, 2 * n:2 * n + 2, :], y_sb[:, 2 * n:2 * n + 2, :], ACT.Square
                                     ).then_inc(S["squared"], 1)

            def inverse_rms(n0, n1):
                for n in range(n0, n1):
                    act.wait_ge(S["norm_mm"], 4 * g + n + 1)
                    nc.scalar.activation(sq[:, 2 * n:2 * n + 2, :], bview(2 + n, 2, SEQ), ACT.Ln, bias=eps[:, 0:1])
                act.drain()
                for n in range(n0, n1):
                    nc.scalar.activation(sq[:, 2 * n:2 * n + 2, :], sq[:, 2 * n:2 * n + 2, :], ACT.Exp, scale=-0.5
                                         ).then_inc(S["rms_ok"], 1)
                    if n == 0:
                        hi_w(s, 79, 1)

            def mix_part(k, n0, n1):
                act.wait_ge(S["mixf_ready"], 2 * g + k + 1)
                if n0 == 0:
                    nc.scalar.activation(mix_hi[:, bass.ds(R * g, R), :], y_sb[:, 0:4, :], ACT.Copy)
                    n0 = 2
                w = 2 * (n1 - n0)
                nc.scalar.activation(mix_hi[:, bass.ds(R * g + NH + 2 * n0 - 4, w), :],
                                     y_sb[:, 2 * n0:2 * n1, :], ACT.Copy).then_inc(S["mix_hi_ok"], 1)

            for n in range(2):
                square(n)
            act.wait_ge(S["y_conv"], 2 * g + 1)
            square(2)
            hi_w(s, 76, 3)
            inverse_rms(0, 3)
            hi_w(s, 80, 1)
            mix_part(0, 0, 3)
            hi_w(s, 81, 1)
            act.wait_ge(S["y_conv"], 2 * g + 2)
            square(3)
            hi_w(s, 82, 2)
            inverse_rms(3, 4)
            mix_part(1, 3, 4)
        with act.Fori(0, 4) as j:
            hi_w(S_OUT + 16 * j, 4, 16)
        nc.scalar.activation(lnrs[:, :], eps[:, :], ACT.Sqrt)
        act.drain()
        act.wait_ge(S["var_ok"], 1)
        nc.scalar.activation(lnrs[:, :], lnmv[:, :, 1], ACT.Sqrt, bias=eps[:, 1:2]).then_inc(S["std_ok"], 1)
        for u in range(8):
            transpose_hi(8, u)
            if u >= 4:
                hi_w(S_Q, u, 1)

        def head_out(h, b, slots):
            act.wait_ge(S["slot_used"], slots)
            nc.scalar.activation(qp[:, b, :, :], bview(b, 2, SEQ), ACT.Copy).then_inc(S["acc_act"], 1)

        def score_out(h, b):
            act.wait_ge(S["score_mm"], h + 1)
            nc.scalar.activation(scores[:, bass.ds(2 * h, 2), :, :], bview(2 + b, 2, 2, NKEY), ACT.Copy
                                 ).then_inc(S["score_ok"], 1)

        def sub_keys_out():
            for n in range(4):
                act.wait_ge(S["sk_mm"], n + 1)
                nc.scalar.activation(skT[:, 4 * n:4 * n + 4, :].rearrange("p a n -> p (a n)"), bank[4 + n][:, :],
                                     ACT.Copy).then_inc(S["sk_ok"], 1)

        def q_rest(j, last):
            s = S_Q + 16 * j
            hi_w(s, 8, 4)
            head_out(2 * j, 0, s + 8)
            if isinstance(j, int) and j == 0:
                sub_keys_out()
            hi_w(s, 12, 3)
            score_out(2 * j, 0)
            hi_w(s, 15, 1 if last else 5)
            head_out(2 * j + 1, 1, s + 16)

        q_rest(0, False)
        def q_body(j, last):
            hi_w(S_Q + 16 * j, 4, 2)
            score_out(2 * j - 1, 1)
            hi_w(S_Q + 16 * j, 6, 2)
            q_rest(j, last)

        with act.Fori(1, 3) as j:
            q_body(j, False)
        q_body(3, True)

        def hi_u(i, c):
            act.wait_ge(S["u_tr"], 16 * i + c + 1)
            act.wait_ge(S["slot_used"], S_U + 16 * i + c - 3)
            nc.scalar.activation(w_hi[:, c % 4, :], bank[4 + c % 4][:, :], ACT.Copy).then_inc(S["hi_done"], 1)

        def gelu(i, tt):
            act.wait_ge(S["slot_used"], S_U + 16 * i + 4 * tt + 4)
            nc.scalar.activation(coef[:, bass.ds(4 * i + tt, 1), :].rearrange("p a t -> p (a t)"),
                                 bank[tt % 2][:, 0:SEQ], ACT.Gelu_apprx_tanh).then_inc(S["gelu_done"], 1)

        def u_body(i, last):
            for tt in range(4):
                for c in range(4 * tt + 3, 4 * tt + 7):
                    if not (last and c >= 16):
                        hi_u(i, c)
                if not (last and tt == 3):
                    gelu(i, tt)

        act.wait_ge(S["s_hspill"], 16)
        for c in range(3):
            hi_u(0, c)
        score_out(7, 1)
        with act.Fori(0, 16) as i:
            u_body(i, False)
        act.wait_ge(S["picks_raw"], 1)
        nc.scalar.activation(picks[:, 2, :, :], picks[:, 2, :, :], ACT.Exp).then_inc(S["picks_exp"], 1)
        with act.Fori(16, 31) as i:
            u_body(i, False)
        u_body(31, True)

        def hi_v(ps, i, c):
            if c % 4 == 0:
                act.wait_ge(s_v[c // 4], 16 * (16 * ps + i + 1))
            act.wait_ge(S["slot_used"], S_V + 128 * ps + 8 * i + c - 3)
            tt, jc = divmod(c, 2)
            nc.scalar.activation(w_hi[:, c % 4, :], v_ring[:, tt // 2, tt % 2, 512 * jc:512 * jc + 512],
                                 ACT.Copy).then_inc(S["hi_done"], 1)

        def hi_c(ps, i, tt):
            m = 64 * ps + 4 * i + tt
            if not (isinstance(m, int) and m < 4):
                act.wait_ge(S["slot_used"], S_V + 2 * m - 6)
            nc.scalar.activation(c_hi[:, tt, :],
                                 coef[:, bass.ds(64 * (ps // 2) + 4 * i + tt, 1), :].rearrange("p a t -> p (a t)"),
                                 ACT.Copy).then_inc(S["c_hi_ok"], 1)

        def v_body(ps, i):
            for tt in range(4):
                first = tt == 0 and isinstance(i, int)
                if not first:
                    hi_c(ps, i, tt)
                for jc in range(2):
                    hi_v(ps, i, 2 * tt + jc)
                if first:
                    act.wait_ge(S["g_mul"], 64 * (ps // 2 + 1))
                    hi_c(ps, i, tt)
                if first and ps == 0:
                    gelu(31, 3)

        for ps in range(4):
            v_body(ps, 0)
            with act.Fori(1, 16) as i:
                v_body(ps, i)
        act.wait_ge(S["eps2_ok"], 1)
        nc.scalar.activation(l2rs[:, :], eps2[:, :], ACT.Sqrt)
        act.drain()
        act.wait_ge(S["var2_ok"], 1)
        nc.scalar.activation(l2rs[:, :], l2mv[:, :, 1], ACT.Sqrt, bias=eps2[:, 0:1]).then_inc(S["std2_ok"], 1)
        act.wait_ge(S["shift2_ok"], 1)
        for q in range(3):
            cols = slice(512 * q, 512 * q + 512)
            nc.scalar.activation(res[:, 1, cols], res[:, 1, cols], ACT.Identity, scale=l2rs[:, 1:2],
                                 bias=l2shift[:, 0:1]).then_inc(S["scaled2"], 1)

    @block.vector
    def _(dve):
        V = nc.vector

        def lo_w(s, c, n):
            for q in range(c, c + n):
                dve.wait_ge(S["hi_done"], s + q + 1)
                src = w_ring[:, (q // 4) % 4, 2 * (q % 4):2 * (q % 4) + 2, :].rearrange("p k c -> p (k c)")
                V.tensor_tensor(w_lo[:, q % 4, :], src, w_hi[:, q % 4, :].bitcast(F32), ALU.subtract
                                ).then_inc(S["lo_done"], 1)

        def transpose_lo(n0, u):
            dve.wait_ge(S["tr_hi"], n0 + u + 1)
            V.tensor_tensor(act_lo[:, 2 * u:2 * u + 2, :], bview(4 + u % 4, 2, SEQ),
                            act_hi[:, 2 * u:2 * u + 2, :].bitcast(F32), ALU.subtract).then_inc(S["tr_lo"], 1)

        for u in range(8):
            transpose_lo(0, u)
            if u == 3:
                lo_w(S_KV, 0, 4)
        lo_w(S_KV, 4, 4)
        dve.wait_ge(S["params_T"], 1)
        V.tensor_copy(params[:, :], bank[2][:, 0:104]).then_inc(S["params_ok"], 1)
        dve.wait_ge(S["gw_hi_ok"], 1)
        V.tensor_tensor(gw_lo[:, :, :], gw[:, :, :], gw_hi[:, :, :].bitcast(F32), ALU.subtract
                        ).then_inc(S["gw_ready"], 1)
        dve.drain()

        def blocks(kv):
            dve.wait_ge(S["slot_used"], S_KV + 8 * (kv + 1))
            for g in range(NG):
                for hh in range(2):
                    src = bank[kv][:, 256 * g + 16 * hh:256 * g + 16 * hh + 240].rearrange("p (n s) -> p s n", s=16)
                    add = params[:, 40 + 32 * kv + 16 * hh:56 + 32 * kv + 16 * hh].unsqueeze(2).to_broadcast([P, 16, NCMP])
                    V.tensor_tensor(blk[:, 16 * hh:16 * hh + 16, 15 * g:15 * g + 15], src, add, ALU.add)
            dve.drain().then_inc(S["blk_raw"], 1)
            dve.drain().then_inc(S["acc_dve"], 1)

        def blocks_lo(kv):
            dve.wait_ge(S["blk_hi_ok"], kv + 1)
            V.tensor_tensor(blk_lo[:, kv, :, :], blk[:, :, :], blk_hi[:, kv, :, :].bitcast(F32), ALU.subtract
                            ).then_inc(S["blk_ready"], 1)
            dve.drain()

        def lo_cmp(q0, q1):
            for q in range(q0, q1):
                dve.wait_ge(S["hi_done"], S_CMP + q + 1)
                V.tensor_tensor(w_lo[:, q % 4, :], w1_ring[:, (q // 4) % 4, q % 4, :],
                                w_hi[:, q % 4, :].bitcast(F32), ALU.subtract).then_inc(S["lo_done"], 1)

        lo_w(S_KV, 8, 4)
        blocks(0)
        lo_w(S_KV, 12, 4)
        blocks_lo(0)
        blocks(1)
        blocks_lo(1)
        lo_cmp(0, 4)
        dve.wait_ge(S["gate_sig"], 1)
        for n, (t, b) in enumerate(((1, 1), (1, 2), (0, 1), (0, 2), (0, 0), (1, 0))):
            V.tensor_copy(gates[:, :, n], gsig[:, t, :].rearrange("p (h b) -> p h b", b=3)[:, :, b])
        lo_cmp(4, 64)
        lo_w(S_GRP, 0, 4)
        dve.wait_ge(S["hidT_mm"], 1)
        V.tensor_copy(hidT[:, :, :, 0:30], bank[5][:, 0:256].rearrange("p (a m n) -> p a m n", a=2, m=4)[:, :, :, 0:30]
                      ).then_inc(S["hidT_ok"], 1)
        dve.wait_ge(S["cmp_mm"], 1)
        V.tensor_copy(kc_all[:, :, 0:NCMP], bank[6][:, 0:30].rearrange("p (g n) -> p g n", g=2))
        V.tensor_copy(vc_all[0:NCMP, :, :], bank[7][0:NCMP, 0:256].rearrange("p (g n) -> p g n", g=2)
                      ).then_inc(S["cmp_ok"], 1)
        dve.drain()
        with dve.Fori(0, NG) as g:
            s = S_GRP + GRP_SLOTS * g

            def squeeze1(ap):
                return ap.rearrange("p a b -> p (a b)")

            def bias(r):
                dve.wait_ge(S["qk_done"], R * g + r + 1)
                sl = nslope_g[:, r:r + 1]
                V.scalar_tensor_tensor(sc1[:, :, :], dist1[:, :].unsqueeze(1).to_broadcast([P, 2, 256]), sl,
                                       bview(2, 2, 256), ALU.mult, ALU.add)
                V.scalar_tensor_tensor(sc0[:, :, :], dist0[:, :].unsqueeze(1).to_broadcast([P, 2, 128]), sl,
                                       bview(3, 2, 128), ALU.mult, ALU.add)
                V.scalar_tensor_tensor(scc[:, :, 0:NCMP], distc[:, :, 0:NCMP], sl,
                                       bank[3][:, 256:288].rearrange("p (t n) -> p t n", t=2)[:, :, 0:NCMP],
                                       ALU.mult, ALU.add)
                dve.drain()
                V.tensor_reduce(mx[:, 0:2], sc1[:, :, :], AX.X, ALU.max)
                V.tensor_reduce(mx[:, 2:4], sc0[:, :, :], AX.X, ALU.max)
                V.tensor_reduce(mx[:, 4:6], scc[:, :, 0:NCMP], AX.X, ALU.max)
                dve.drain()
                V.tensor_scalar(nmx[:, :], mx[:, :], -1.0, None, ALU.mult).then_inc(S["biased"], 1)

            def scale(r):
                dve.wait_ge(S["exps"], R * g + r + 1)
                V.reciprocal(rg[:, :], sums[:, :])
                V.tensor_tensor(scc[:, :, 0:NCMP], scc[:, :, 0:NCMP], validc[:, :, 0:NCMP], ALU.mult)
                dve.drain()
                V.tensor_tensor(rg[:, :], rg[:, :], gates_g[:, r, :], ALU.mult)
                dve.drain()
                V.tensor_tensor(sc1[:, :, :], sc1[:, :, :], rg[:, 0:2].unsqueeze(2).to_broadcast([P, 2, 256]), ALU.mult)
                V.tensor_tensor(sc0[:, :, :], sc0[:, :, :], rg[:, 2:4].unsqueeze(2).to_broadcast([P, 2, 128]), ALU.mult)
                V.tensor_tensor(scc[:, :, 0:NCMP], scc[:, :, 0:NCMP],
                                rg[:, 4:6].unsqueeze(2).to_broadcast([P, 2, NCMP]), ALU.mult
                                ).then_inc(S["probs_ready"], 1)

            def probs_out(r):
                dve.wait_ge(S["pt_done"], R * g + r + 1)
                V.tensor_copy(pT0[:, :, :], bview(5, 2, 128))
                V.tensor_copy(pTc[0:16, :, :], bank[5][0:16, 256:512].rearrange("p (t n) -> p t n", t=2)
                              ).then_inc(S["pt_dve"], 1)

            def conv_in(b, end):
                dve.wait_ge(S["slot_used"], s + end)
                dve.wait_ge(S["acc_act"], 6 * g + 5 + (b == 0))
                V.tensor_tensor(cu[:, :, 2:SEQ + 2], bview(b, 2, SEQ), c_sb[:, :, :], ALU.mult
                                ).then_inc(S["acc_dve"], 1)
                dve.drain()

            def conv_tap(pair, tap):
                for b in range(2):
                    w = conv_g[:, tap, 2 * pair + b:2 * pair + b + 1]
                    if tap == 0:
                        V.tensor_scalar(cv[:, b, :], cu[:, b, 0:SEQ], w, None, ALU.mult)
                    else:
                        V.scalar_tensor_tensor(cv[:, b, :], cu[:, b, tap:tap + SEQ], w, cv[:, b, :], ALU.mult, ALU.add)
                dve.drain()

            def conv_out(pair, b, end):
                dve.wait_ge(S["slot_used"], s + end)
                V.tensor_tensor(y_sb[:, 4 + 2 * pair:6 + 2 * pair, :], bview(b, 2, SEQ), cv[:, :, :], ALU.mult)
                dve.drain().then_inc(S["acc_dve"], 1)
                dve.drain().then_inc(S["y_conv"], 1)

            lo_w(s, 4, 4)
            V.tensor_copy(nslope_g[:, :], nslope[:, bass.ds(R * g, R)])
            V.tensor_copy(gates_g[:, :, :], gates[:, bass.ds(R * g, R), :])
            V.tensor_copy(conv_g[:, :, :], params[:, 0:24].rearrange("p (j b) -> p j b", j=3)[:, :, bass.ds(R * g, R)])
            V.tensor_copy(norm_g[:, :, :], params[:, 24:40].rearrange("p (a b) -> p a b", a=2)[:, :, bass.ds(R * g, R)])
            V.tensor_copy(kc_g[:, :], squeeze1(kc_all[:, bass.ds(g, 1), :]))
            V.tensor_copy(vc_g[0:NCMP, :], squeeze1(vc_all[0:NCMP, bass.ds(g, 1), :])).then_inc(S["grp_ready"], 1)
            lo_w(s, 8, 28)
            bias(0)
            lo_w(s, 36, 3)
            scale(0)
            lo_w(s, 39, 5)
            probs_out(0)
            bias(1)
            lo_w(s, 44, 3)
            scale(1)
            lo_w(s, 47, 5)
            probs_out(1)
            bias(2)
            lo_w(s, 52, 2)
            conv_in(1, 48)
            lo_w(s, 54, 1)
            scale(2)
            lo_w(s, 55, 5)
            probs_out(2)
            bias(3)
            lo_w(s, 60, 1)
            conv_tap(0, 0)
            lo_w(s, 61, 1)
            conv_tap(0, 1)
            lo_w(s, 62, 1)
            scale(3)
            lo_w(s, 63, 1)
            conv_tap(0, 2)
            conv_out(0, 0, 56)
            lo_w(s, 64, 4)
            probs_out(3)
            lo_w(s, 68, 8)
            conv_in(0, 72)
            lo_w(s, 76, 1)
            conv_tap(1, 0)
            lo_w(s, 77, 1)
            conv_tap(1, 1)
            conv_tap(1, 2)
            lo_w(s, 78, 1)

            def normed(k, n0, n1):
                for n in range(n0, n1):
                    dve.wait_ge(S["rms_ok"], 4 * g + n + 1)
                    for b in range(2 * n, 2 * n + 2):
                        ins = V.scalar_tensor_tensor(y_sb[:, b, :], y_sb[:, b, :], norm_g[:, b // 4, b % 4:b % 4 + 1],
                                                     sq[:, b, :], ALU.mult, ALU.mult)
                    if n == 0:
                        lo_w(s, 79, 1)
                ins.then_inc(S["mixf_ready"], 1)

            def mix_part(k, n0, n1):
                dve.wait_ge(S["mix_hi_ok"], 2 * g + k + 1)
                if n0 == 0:
                    V.tensor_tensor(mix_lo[:, bass.ds(R * g, R), :], y_sb[:, 0:4, :],
                                    mix_hi[:, bass.ds(R * g, R), :].bitcast(F32), ALU.subtract)
                    n0 = 2
                w = 2 * (n1 - n0)
                blocks_ = bass.ds(R * g + NH + 2 * n0 - 4, w)
                V.tensor_tensor(mix_lo[:, blocks_, :], y_sb[:, 2 * n0:2 * n1, :],
                                mix_hi[:, blocks_, :].bitcast(F32), ALU.subtract).then_inc(S["mix_ready"], 1)

            normed(0, 0, 3)
            lo_w(s, 80, 1)
            conv_out(1, 1, 80)
            mix_part(0, 0, 3)
            lo_w(s, 81, 3)
            normed(1, 3, 4)
            mix_part(1, 3, 4)

        with dve.Fori(0, 4) as j:
            s = S_OUT + 16 * j
            for t in range(2):
                lo_w(s, 8 * t + 4, 7)
                dve.wait_ge(S["slot_used"], s + 8 * t + 8)
                cols = xh[:, :, bass.ds(512 * j + 256 * t, 256)]
                V.scalar_tensor_tensor(cols, cols, ALPHA, bview(t, 2, 256), ALU.mult, ALU.add
                                       ).then_inc(S["acc_dve"], 1)
                dve.drain()
                for tt in range(2):
                    V.bn_stats(lnst[:, tt, bass.ds(2 * j + t, 1), :].rearrange("p a s -> p (a s)"),
                               xh[:, tt, bass.ds(512 * j + 256 * t, 256)])
                lo_w(s, 8 * t + 11, 1)

        def mean_rstd(st, mv, rs_, done_var, done_std):
            dve.drain()
            for t in range(2):
                V.bn_aggr(mv[:, t, :], st[:, t, :, :])
            dve.drain().then_inc(done_var, 1)
            dve.wait_ge(done_std, 1)
            V.reciprocal(rs_[:, :], rs_[:, :])
            dve.drain()

        def norm_cols(buf, mv, rs_, g_row, b_row, q, ready, tiles=(0, 1)):
            cols = slice(512 * q, 512 * q + 512)
            for t in tiles:
                V.scalar_tensor_tensor(buf[:, t, cols], buf[:, t, cols], mv[:, t, 0:1], g_row[:, cols],
                                       ALU.subtract, ALU.mult)
            dve.drain()
            for t in tiles:
                ins = V.scalar_tensor_tensor(buf[:, t, cols], buf[:, t, cols], rs_[:, t:t + 1], b_row[:, cols],
                                             ALU.mult, ALU.add)
            ins.then_inc(ready, 1)

        mean_rstd(lnst, lnmv, lnrs, S["var_ok"], S["std_ok"])
        dve.wait_ge(S["s_lnrow"], 32)
        norm_cols(xh, lnmv, lnrs, ln_g, ln_b, 0, S["ln1_done"])
        norm_cols(xh, lnmv, lnrs, ln_g, ln_b, 1, S["ln1_done"])
        for u in range(8):
            transpose_lo(8, u)
            if u >= 4:
                lo_w(S_Q, u, 1)
            if u in (1, 3):
                norm_cols(xh, lnmv, lnrs, ln_g, ln_b, 2 + u // 2, S["ln1_done"])
        lo_w(S_Q, 8, 12)
        with dve.Fori(1, 3) as j:
            lo_w(S_Q + 16 * j, 4, 16)
        lo_w(S_Q + 48, 4, 12)

        def lo_u(i, c, n):
            for q in range(c, c + n):
                dve.wait_ge(S["hi_done"], S_U + 16 * i + q + 1)
                V.tensor_tensor(w_lo[:, q % 4, :], bank[4 + q % 4][:, :], w_hi[:, q % 4, :].bitcast(F32),
                                ALU.subtract).then_inc(S["lo_done"], 1)

        def top16(val, idx, src, other):
            V.max(val[:, 0:8], src)
            dve.drain()
            V.max_index(idx[:, 0:8], val[:, 0:8], src)
            V.match_replace(other, val[:, 0:8], src, -3.0e38)
            dve.drain()
            V.max(val[:, 8:16], other)
            dve.drain()
            V.max_index(idx[:, 8:16], val[:, 8:16], other)

        dve.wait_ge(S["score_ok"], 8)
        V.tensor_copy(iota16[:, :], iota[:, 0:16])
        with dve.Fori(0, 16) as i:
            lo_u(i, 0, 2)
            V.tensor_copy(rs[:, :, :], scores[:, bass.ds(i, 1), :, :].rearrange("p a c n -> p (a c) n"))
            dve.drain()
            lo_u(i, 2, 1)
            top16(t_val[:, 0, :], t_idx[:, 0, :], rs[:, 0, :], rs2[:, 0, :])
            lo_u(i, 3, 2)
            top16(t_val[:, 1, :], t_idx[:, 1, :], rs[:, 1, :], rs2[:, 1, :])
            lo_u(i, 5, 2)
            dve.drain()
            V.tensor_copy(t_idf[:, :, :], t_idx[:, :, :])
            V.tensor_tensor(cand[:, :, :], t_val[:, 0, :].unsqueeze(2).to_broadcast([P, 16, 16]),
                            t_val[:, 1, :].unsqueeze(1).to_broadcast([P, 16, 16]), ALU.add)
            dve.drain()
            lo_u(i, 7, 2)
            flat, flat2 = (a[:, :, :].rearrange("p a b -> p (a b)") for a in (cand, cand2))
            V.max(b_val[:, 0:8], flat)
            dve.drain()
            V.max_index(b_idx[:, 0:8], b_val[:, 0:8], flat)
            V.match_replace(flat2, b_val[:, 0:8], flat, -3.0e38)
            dve.drain()
            lo_u(i, 9, 2)
            V.max(b_val[:, 8:16], flat2)
            dve.drain()
            V.max_index(b_idx[:, 8:16], b_val[:, 8:16], flat2)
            dve.drain()
            V.tensor_single_scalar(b_ij[:, 0, :], b_idx[:, :], 4, ALU.logical_shift_right)
            V.tensor_single_scalar(b_ij[:, 1, :], b_idx[:, :], 15, ALU.bitwise_and)
            dve.drain()
            V.tensor_copy(b_ijf[:, :, :], b_ij[:, :, :])
            dve.drain()
            lo_u(i, 11, 2)
            for a in range(2):
                V.tensor_tensor(eq[:, a, :, :], b_ijf[:, a, :].unsqueeze(2).to_broadcast([P, TOPK, 16]),
                                iota16[:, :].unsqueeze(1).to_broadcast([P, TOPK, 16]), ALU.is_equal)
            dve.drain()
            lo_u(i, 13, 1)
            for a in range(2):
                V.tensor_tensor(eq[:, a, :, :], eq[:, a, :, :],
                                t_idf[:, a, :].unsqueeze(1).to_broadcast([P, TOPK, 16]), ALU.mult)
            dve.drain()
            lo_u(i, 14, 1)
            V.tensor_reduce(b_id[:, :, :], eq[:, :, :, :], AX.X, ALU.add)
            dve.drain()
            for a in range(2):
                V.tensor_copy(picks[:, a, bass.ds(i, 1), :].rearrange("p a k -> p (a k)"), b_id[:, a, :])
            V.tensor_copy(picks[:, 2, bass.ds(i, 1), :].rearrange("p a k -> p (a k)"), b_val[:, :])
            lo_u(i, 15, 1)
        dve.drain()
        lo_u(16, 0, 1)
        V.tensor_copy(pick_ref[:, :], picks[:, 2, :, 0])
        dve.drain()
        V.tensor_tensor(picks[:, 2, :, :], picks[:, 2, :, :], pick_ref[:, :].unsqueeze(2).to_broadcast([P, 16, TOPK]),
                        ALU.subtract).then_inc(S["picks_raw"], 1)
        lo_u(16, 1, 1)
        dve.wait_ge(S["picks_exp"], 1)
        V.tensor_reduce(pick_ref[:, :], picks[:, 2, :, :], AX.X, ALU.add)
        dve.drain()
        V.reciprocal(pick_ref[:, :], pick_ref[:, :])
        dve.drain()
        V.tensor_tensor(picks[:, 2, :, :], picks[:, 2, :, :], pick_ref[:, :].unsqueeze(2).to_broadcast([P, 16, TOPK]),
                        ALU.mult)
        dve.drain()
        for a in range(3):
            V.tensor_copy(picks_t[:, a, :, :, :], picks[:, a, :, :].rearrange("p (h t) k -> p t h k", t=2))
        dve.drain().then_inc(S["picks_ok"], 1)
        lo_u(16, 2, 1)
        dve.wait_ge(S["tok_mm"], 1)
        V.tensor_copy(tok_id[:, :, :], bview(2, 2, SEQ))
        V.tensor_copy(g_rest[:, :], bank[3][:, 0:SEQ]).then_inc(S["tok_ok"], 1)
        V.tensor_copy(iota_h[:, :], iota[:, :])
        lo_u(16, 3, 1)
        for part in range(3):
            dve.drain()
            V.tensor_copy(tok_g[:, part, :], g_rest[:, :])
            dve.drain()
            if part < 2:
                V.tensor_tensor(g_rest[:, :], g_rest[:, :], tok_g[:, part, :], ALU.subtract)

        def equal(n, b, half):
            if not (isinstance(n, int) and n < 2):
                dve.wait_ge(S["hot_used"], n - 1)
            tok = bass.ds(4 * n - 256 * half, 4)
            V.tensor_tensor(oneB[:, b, :, :], iota_h[:, :].unsqueeze(1).to_broadcast([P, 4, NKEY]),
                            tok_id[:, 1, tok].unsqueeze(2).to_broadcast([P, 4, NKEY]), ALU.is_equal)
            V.tensor_tensor(oneA[:, b, :, :],
                            iota_h[:, HALF * half:HALF * half + HALF].unsqueeze(1).to_broadcast([P, 4, HALF]),
                            tok_id[:, 0, tok].unsqueeze(2).to_broadcast([P, 4, HALF]), ALU.is_equal
                            ).then_inc(S["equal_ready"], 1)

        def gate_mul(n, b, half):
            dve.wait_ge(S["hot_used"], n + 1)
            view = coef[:, HALF * half:HALF * half + HALF, bass.ds(4 * n - 256 * half, 4)].rearrange("p k t -> p t k")
            V.tensor_tensor(view, view, bview(2 + b, 4, HALF), ALU.mult).then_inc(S["g_mul"], 1)

        dve.wait_ge(S["gelu_done"], HALF)

        def u_gated(i, done, last):
            n = 4 * i - 64
            for c in range(16):
                if c >= done:
                    lo_u(i, c, 1)
                if c % 4 == 2 and not (last and c == 14):
                    equal(n + c // 4 + 1, (c // 4 + 1) % 2, 0)
                if c in (5, 9, 13):
                    gate_mul(n + c // 4 - 1, (c // 4 - 1) % 2, 0)
            gate_mul(n + 3, 1, 0)

        equal(0, 0, 0)
        u_gated(16, 4, False)
        with dve.Fori(17, 31) as i:
            u_gated(i, 0, False)
        u_gated(31, 0, True)

        def lo_c(ps, i, tt):
            dve.wait_ge(S["c_hi_ok"], 64 * ps + 4 * i + tt + 1)
            tile_c = coef[:, bass.ds(64 * (ps // 2) + 4 * i + tt, 1), :].rearrange("p a t -> p (a t)")
            V.tensor_tensor(c_lo[:, tt, :], tile_c, c_hi[:, tt, :].bitcast(F32), ALU.subtract
                            ).then_inc(S["c_lo_ok"], 1)

        def add_pass(ps, jc):
            dve.wait_ge(S["slot_used"], S_V + 128 * (ps + 1) - 1 + jc)
            col = 1024 * (ps % 2) + 512 * jc
            for t in range(2):
                cols = res[:, t, col:col + 512]
                acc = bank[(4, 4, 0, 4)[ps] + 2 * t + jc][:, :]
                if ps < 2:
                    ins = V.scalar_tensor_tensor(cols, cols, ALPHA, acc, ALU.mult, ALU.add)
                else:
                    ins = V.tensor_tensor(cols, cols, acc, ALU.add)
            if ps < 3:
                ins.then_inc(S["pass_read"], 1)

        def stats(q):
            for t in range(2):
                V.bn_stats(l2st[:, t, q, :], res[:, t, 512 * q:512 * q + 512])

        def v_body(ps, i):
            n = 64 + 32 * ps + 2 * i
            for c in range(8):
                tt, jc = divmod(c, 2)
                if jc == 0 and not (c == 0 and isinstance(i, int)):
                    lo_c(ps, i, tt)
                dve.wait_ge(S["hi_done"], S_V + 128 * ps + 8 * i + c + 1)
                V.tensor_tensor(w_lo[:, c % 4, :], v_ring[:, tt // 2, tt % 2, 512 * jc:512 * jc + 512],
                                w_hi[:, c % 4, :].bitcast(F32), ALU.subtract).then_inc(S["lo_done"], 1)
                if c == 1 and isinstance(i, int):
                    lo_c(ps, i, 0)
                if isinstance(i, int) and i == 0 and ps == 1 and c == 1:
                    dve.wait_ge(S["s_res"], 16)
                    add_pass(0, 0)
                    add_pass(0, 1)
                if isinstance(i, int) and i == 0 and ps > 1 and c in (4, 6):
                    add_pass(ps - 1, c // 2 - 2)
                if isinstance(i, int) and i == 15 and ps == 3 and c in (1, 4):
                    stats(c // 3)
                if ps < 2 and c in (1, 5) and not (ps == 1 and isinstance(i, int) and i == 15 and c == 5):
                    equal(n + c // 4 + 1, (c // 4 + 1) % 2, 1)
                if ps == 0 and c == 4 and isinstance(i, int):
                    dve.wait_ge(S["gelu_done"], ET)
                if ps < 2 and c in (4, 7):
                    gate_mul(n + c // 7, c // 7, 1)

        equal(64, 0, 1)
        v_body(0, 0)
        with dve.Fori(1, 16) as i:
            v_body(0, i)
        for ps in range(1, 4):
            v_body(ps, 0)
            with dve.Fori(1, 15) as i:
                v_body(ps, i)
            v_body(ps, 15)
        V.memset(eps2[:, :], LN_EPS).then_inc(S["eps2_ok"], 1)
        for jc in range(2):
            add_pass(3, jc)
            dve.drain()
            stats(2 + jc)
        mean_rstd(l2st, l2mv, l2rs, S["var2_ok"], S["std2_ok"])
        V.scalar_tensor_tensor(l2shift[:, :], l2mv[:, 1, 0:1], -1.0, l2rs[:, 1:2], ALU.mult, ALU.mult
                               ).then_inc(S["shift2_ok"], 1)
        dve.wait_ge(S["s_ln2row"], 32)
        for q in range(4):
            norm_cols(res, l2mv, l2rs, ln2g_sb, ln2b_sb, q, S["final_ok"], (0,))
        norm_cols(res, l2mv, l2rs, ln2g_sb, ln2b_sb, 3, S["final_ok"], (1,))

    block_cm.__exit__(None, None, None)


_INS = ['x', 'w_in', 'cmp_k_pos', 'cmp_k_w1', 'cmp_k_b1', 'cmp_k_w2', 'cmp_v_pos', 'cmp_v_w1', 'cmp_v_b1',
        'cmp_v_w2', 'conv_w', 'head_norm_g', 'w_out', 'ln1_g', 'ln1_b', 'w_query', 'sub_keys', 'expert_u',
        'expert_v', 'ln2_g', 'ln2_b']


def kernel(**inputs):
    import numpy as _np
    import concourse.bacc as _bacc
    from concourse import mybir as _mybir
    from concourse.bass_utils import run_bass_kernel_spmd as _run

    nc = _bacc.Bacc("TRN2", target_bir_lowering=False, num_devices=1)
    arrays, args = {}, []
    for name in _INS:
        a = _np.ascontiguousarray(inputs[name])
        arrays[f"in_{name}_dram"] = a
        args.append(nc.dram_tensor(f"in_{name}_dram", a.shape, _mybir.dt.from_np(a.dtype), kind="ExternalInput").ap())
    out = nc.dram_tensor("out_0_dram", (1, SEQ, D), _mybir.dt.float32, kind="ExternalOutput").ap()
    build(nc, *args, out)
    r = _run(nc, [arrays], core_ids=[0])
    return r.results[0]["out_0_dram"]
```
